# Optimizing a Trainium2 kernel written in Bass

```python
import math
import jax, jax.numpy as jnp
from jax import lax
import numpy as np

D_MODEL = 1024
BATCH = 1
SEQ = 512
DEPTH = 2

CHUNK = 64
Q_BLOCK = 128
EPS = 1e-6
N_A = (DEPTH + 1) // 2
N_B = DEPTH - N_A
D_FF = 2816
S5_GROUP = 16
S5_GROUPS = D_MODEL // S5_GROUP
S5_STATE = 64
S5_DT_MIN = 1e-3
S5_DT_MAX = 1e-1
MLA_HEADS = 8
NOPE_DIM = 128
ROPE_DIM = 64
V_DIM = 128
Q_LORA = 256
KV_LORA = 128
ROPE_BASE = 10000.0

kernel_name = "yoco_s5_mla_macaron_trunk"

def rms_norm(x, g):
    xf = x.astype(jnp.float32)
    y = xf * lax.rsqrt(jnp.mean(xf * xf, axis=-1, keepdims=True) + EPS)
    return (y * g.astype(jnp.float32)).astype(x.dtype)

def swiglu(h, w_in, w_out):
    gu = h @ w_in
    gate, up = gu[..., :D_FF], gu[..., D_FF:]
    return (jax.nn.silu(gate) * up) @ w_out

def rope_tables(positions):
    inv_freq = 1.0 / (ROPE_BASE ** (jnp.arange(0, ROPE_DIM, 2, dtype=jnp.float32) / ROPE_DIM))
    ang = positions.astype(jnp.float32)[..., None] * inv_freq
    return jnp.cos(ang), jnp.sin(ang)

def apply_rope(x, cos, sin):
    half = ROPE_DIM // 2
    xf = x.astype(jnp.float32)
    x1, x2 = xf[..., :half], xf[..., half:]
    return jnp.concatenate([x1 * cos - x2 * sin, x1 * sin + x2 * cos], axis=-1).astype(x.dtype)

def s5_mixer(h, lam_re, lam_im, log_step, b_re, b_im, c_re, c_im, d_skip, w_glu):
    bsz, seq, _ = h.shape
    f32 = jnp.float32
    u = h.astype(f32).reshape(bsz, seq, S5_GROUPS, S5_GROUP)
    step = jnp.exp(log_step.astype(f32))[:, None]
    lam = lax.complex(lam_re.astype(f32), lam_im.astype(f32))
    lam_bar = jnp.exp(lam * step)
    b = lax.complex(b_re.astype(f32), b_im.astype(f32))
    b_bar = ((lam_bar - 1.0) / lam)[..., None] * b
    bu = lax.complex(jnp.einsum('gpc,bsgc->bsgp', jnp.real(b_bar), u),
                     jnp.einsum('gpc,bsgc->bsgp', jnp.imag(b_bar), u))
    a = jnp.broadcast_to(lam_bar[None, None], (1, seq, S5_GROUPS, S5_STATE))

    def combine(e1, e2):
        a1, b1 = e1
        a2, b2 = e2
        return a1 * a2, a2 * b1 + b2

    _, states = lax.associative_scan(combine, (a, bu), axis=1)
    y = (jnp.einsum('gcp,bsgp->bsgc', c_re.astype(f32), jnp.real(states))
         - jnp.einsum('gcp,bsgp->bsgc', c_im.astype(f32), jnp.imag(states)))
    y = y.reshape(bsz, seq, D_MODEL) + d_skip.astype(f32) * h.astype(f32)
    y = jax.nn.gelu(y).astype(h.dtype)
    z = y @ w_glu
    return z[..., :D_MODEL] * jax.nn.sigmoid(z[..., D_MODEL:])

def shared_kv(h, cos, sin, kv_in_norm, w_dkv, kv_latent_norm, w_ukv):
    bsz, seq, _ = h.shape
    kv_a = rms_norm(h, kv_in_norm) @ w_dkv
    c_kv = rms_norm(kv_a[..., :KV_LORA], kv_latent_norm)
    k_rope = apply_rope(kv_a[..., KV_LORA:], cos, sin)
    kv = (c_kv @ w_ukv).reshape(bsz, seq, MLA_HEADS, NOPE_DIM + V_DIM)
    k_nope, v = kv[..., :NOPE_DIM], kv[..., NOPE_DIM:]
    k_rope_h = jnp.broadcast_to(k_rope[:, :, None, :], (bsz, seq, MLA_HEADS, ROPE_DIM))
    k = jnp.concatenate([k_nope, k_rope_h], axis=-1)
    return k, v

def mla_attention(h, cos, sin, k, v, w_dq, q_norm, w_uq, w_o):
    bsz, seq, _ = h.shape
    qk_dim = NOPE_DIM + ROPE_DIM
    c_q = rms_norm(h @ w_dq, q_norm)
    q = (c_q @ w_uq).reshape(bsz, seq, MLA_HEADS, qk_dim)
    q = jnp.concatenate([q[..., :NOPE_DIM],
                         apply_rope(q[..., NOPE_DIM:], cos[:, :, None, :], sin[:, :, None, :])], axis=-1)
    scale = 1.0 / math.sqrt(qk_dim)
    n_blk = seq // Q_BLOCK
    q_blocks = q.reshape(bsz, n_blk, Q_BLOCK, MLA_HEADS, qk_dim).transpose(1, 0, 2, 3, 4)
    q_chunk = (jnp.arange(seq, dtype=jnp.int32) // CHUNK).reshape(n_blk, Q_BLOCK)
    k_chunk = jnp.arange(seq, dtype=jnp.int32) // CHUNK
    neg = jnp.finfo(jnp.float32).min

    def attend(args):
        qb, qc = args
        s = jnp.einsum('bqhd,bkhd->bhqk', qb, k).astype(jnp.float32) * scale
        mask = k_chunk[None, :] <= qc[:, None]
        s = jnp.where(mask[None, None], s, neg)
        p = jax.nn.softmax(s, axis=-1).astype(v.dtype)
        return jnp.einsum('bhqk,bkhd->bqhd', p, v)

    o = lax.map(attend, (q_blocks, q_chunk))
    o = o.transpose(1, 0, 2, 3, 4).reshape(bsz, seq, MLA_HEADS * V_DIM)
    return o @ w_o

def setup_inputs(seed: int = 0) -> dict:
    key = jax.random.key(seed)
    ks = jax.random.split(key, 24)
    f32 = jnp.float32

    def nrm(k, shape, fan_in):
        return jax.random.normal(k, shape, f32) * (fan_in ** -0.5)

    def gain(k, shape):
        return 1.0 + 0.02 * jax.random.normal(k, shape, f32)

    x = jax.random.normal(ks[0], (BATCH, SEQ, D_MODEL), f32)
    start = jax.random.randint(ks[1], (BATCH, 1), 0, 4096, dtype=jnp.int32)
    positions = (start + jnp.arange(SEQ, dtype=jnp.int32)[None, :]).astype(jnp.int32)
    norm_gains = gain(ks[2], (DEPTH, 3, D_MODEL))
    ffn_w_in = nrm(ks[3], (DEPTH, 2, D_MODEL, 2 * D_FF), D_MODEL)
    ffn_w_out = nrm(ks[4], (DEPTH, 2, D_FF, D_MODEL), D_FF)
    n_idx = jnp.arange(S5_STATE, dtype=f32)
    s5_lambda_re = -0.5 * jnp.exp(0.05 * jax.random.normal(ks[5], (N_A, S5_GROUPS, S5_STATE), f32))
    s5_lambda_im = math.pi * n_idx + 0.05 * jax.random.normal(ks[6], (N_A, S5_GROUPS, S5_STATE), f32)
    s5_log_step = jax.random.uniform(ks[7], (N_A, S5_GROUPS), f32,
                                     math.log(S5_DT_MIN), math.log(S5_DT_MAX))
    s5_b_re = nrm(ks[8], (N_A, S5_GROUPS, S5_STATE, S5_GROUP), 2 * S5_GROUP)
    s5_b_im = nrm(ks[9], (N_A, S5_GROUPS, S5_STATE, S5_GROUP), 2 * S5_GROUP)
    s5_c_re = nrm(ks[10], (N_A, S5_GROUPS, S5_GROUP, S5_STATE), S5_STATE)
    s5_c_im = nrm(ks[11], (N_A, S5_GROUPS, S5_GROUP, S5_STATE), S5_STATE)
    s5_d = jax.random.normal(ks[12], (N_A, D_MODEL), f32)
    s5_w_glu = nrm(ks[13], (N_A, D_MODEL, 2 * D_MODEL), D_MODEL)
    kv_in_norm = gain(ks[14], (D_MODEL,))
    w_dkv = nrm(ks[15], (D_MODEL, KV_LORA + ROPE_DIM), D_MODEL)
    kv_latent_norm = gain(ks[16], (KV_LORA,))
    w_ukv = nrm(ks[17], (KV_LORA, MLA_HEADS * (NOPE_DIM + V_DIM)), KV_LORA)
    mla_w_dq = nrm(ks[18], (N_B, D_MODEL, Q_LORA), D_MODEL)
    mla_q_norm = gain(ks[19], (N_B, Q_LORA))
    mla_w_uq = nrm(ks[20], (N_B, Q_LORA, MLA_HEADS * (NOPE_DIM + ROPE_DIM)), Q_LORA)
    mla_w_o = nrm(ks[21], (N_B, MLA_HEADS * V_DIM, D_MODEL), MLA_HEADS * V_DIM)
    final_norm = gain(ks[22], (D_MODEL,))
    return {"x": x, "positions": positions, "norm_gains": norm_gains,
            "ffn_w_in": ffn_w_in, "ffn_w_out": ffn_w_out,
            "s5_lambda_re": s5_lambda_re, "s5_lambda_im": s5_lambda_im,
            "s5_log_step": s5_log_step, "s5_b_re": s5_b_re, "s5_b_im": s5_b_im,
            "s5_c_re": s5_c_re, "s5_c_im": s5_c_im, "s5_d": s5_d, "s5_w_glu": s5_w_glu,
            "kv_in_norm": kv_in_norm, "w_dkv": w_dkv, "kv_latent_norm": kv_latent_norm,
            "w_ukv": w_ukv, "mla_w_dq": mla_w_dq, "mla_q_norm": mla_q_norm,
            "mla_w_uq": mla_w_uq, "mla_w_o": mla_w_o, "final_norm": final_norm}

def reference(x, positions, norm_gains, ffn_w_in, ffn_w_out,
              s5_lambda_re, s5_lambda_im, s5_log_step, s5_b_re, s5_b_im,
              s5_c_re, s5_c_im, s5_d, s5_w_glu,
              kv_in_norm, w_dkv, kv_latent_norm, w_ukv,
              mla_w_dq, mla_q_norm, mla_w_uq, mla_w_o, final_norm):
    cos, sin = rope_tables(positions)
    k_shared = None
    v_shared = None
    for l in range(DEPTH):
        g = norm_gains[l]
        x = x + 0.5 * swiglu(rms_norm(x, g[0]), ffn_w_in[l, 0], ffn_w_out[l, 0])
        h = rms_norm(x, g[1])
        if l < N_A:
            x = x + s5_mixer(h, s5_lambda_re[l], s5_lambda_im[l], s5_log_step[l],
                             s5_b_re[l], s5_b_im[l], s5_c_re[l], s5_c_im[l],
                             s5_d[l], s5_w_glu[l])
        else:
            j = l - N_A
            x = x + mla_attention(h, cos, sin, k_shared, v_shared,
                                  mla_w_dq[j], mla_q_norm[j], mla_w_uq[j], mla_w_o[j])
        x = x + 0.5 * swiglu(rms_norm(x, g[2]), ffn_w_in[l, 1], ffn_w_out[l, 1])
        if l == N_A - 1 and N_B > 0:
            k_shared, v_shared = shared_kv(x, cos, sin, kv_in_norm, w_dkv,
                                           kv_latent_norm, w_ukv)
    return rms_norm(x, final_norm)


_drawn_inputs = setup_inputs


def setup_inputs(seed=0):
    import zlib

    import numpy as np

    out = dict(_drawn_inputs(seed))
    spreads = {}
    factors = {'norm_gains': 3.052,
     's5_lambda_re': 8.0,
     's5_b_re': 2.73,
     's5_b_im': 2.693,
     's5_c_re': 2.713,
     's5_c_im': 2.741,
     'kv_in_norm': 8.0,
     'kv_latent_norm': 8.0,
     'mla_q_norm': 8.0,
     'final_norm': 2.821}
    for name, (base, spread) in spreads.items():
        noise = np.random.default_rng([zlib.crc32(name.encode()), seed]).standard_normal(out[name].shape)
        drawn = base * np.exp(spread * noise) if base else spread * noise
        out[name] = __import__('jax').numpy.asarray(drawn.astype(out[name].dtype))
    for name, factor in factors.items():
        out[name] = (out[name] * factor).astype(out[name].dtype)
    return out
```

```python
import numpy as np

import concourse.bass as bass
from concourse import mybir

F32 = mybir.dt.float32
F32R = mybir.dt.float32r
I32 = mybir.dt.int32
ALU = mybir.AluOpType
ACT = mybir.ActivationFunctionType
AX = mybir.AxisListType

P = 128
SEQ = 512
D = 1024
DT = D // P
FF = 2816
FT = FF // P
HEADS = 8
QK_SCALE = float(1.0 / np.sqrt(192.0))
EPS = 1e-6
NEG = -3.0e38

GROUPS, GC, ST = 64, 16, 64
T = 8
STEPS = SEQ // T
GB = 8
BLOCKS = GROUPS // GB
M = T + 1

RING = 4
AHEAD = 3
IN_PACKS = 2 * FT
FFN_PACKS = IN_PACKS + FT
FFN0A = 0
GLU = FFN0A + FFN_PACKS
FFN0B = GLU + 2 * DT
KVD = FFN0B + FFN_PACKS
FFN1A = KVD + 3
DQ = FFN1A + FFN_PACKS
UKV = DQ + 2
UQ = UKV + 2
WO = UQ + 4
FFN1B = WO + DT
N_PACKS = FFN1B + FFN_PACKS
N_LOADS = N_PACKS + AHEAD

F_BASE = {FFN0A: 0, FFN0B: FT, FFN1A: 2 * FT, FFN1B: 3 * FT}
X_BASE = {FFN0A: 0, GLU: DT, FFN0B: 2 * DT, FFN1A: 3 * DT, WO: 4 * DT, FFN1B: 5 * DT}
H_BASE = {FFN0A: 0, FFN0B: DT, KVD: 2 * DT, FFN1A: 3 * DT, DQ: 4 * DT, FFN1B: 5 * DT}
N_IN0A, N_S5, N_IN0B, N_KV, N_LAT, N_DQ, N_CQ, N_IN1B, N_FINAL = range(9)
SUMS = {N_IN0A: 0, N_S5: 1, N_IN0B: 2, N_KV: 3, N_DQ: 4, N_IN1B: 5, N_FINAL: 6}

G_IN0A, G_S5, G_IN0B, G_KV, G_IN1A, G_DQ, G_IN1B, G_FIN = (8 * i for i in range(8))
C_LAT, C_QN, C_SGN, C_SGNR, C_INVF = 64, 65, 67, 68, 69
N_COLS = 70

O_B, O_COS, O_SIN, O_C, O_T = 0, 1024, 1536, 2048, 3072
OPS = 4096


def build(nc, xT, wstream, cols, consts, mask, pos, lam, bcd, dskip, out):
    ops_dram = nc.dram_tensor("s5_ops", [BLOCKS, P, OPS], F32, kind="Internal").ap()
    u_dram = nc.dram_tensor("s5_u", [D, T, STEPS], F32, kind="Internal").ap()
    y_dram = nc.dram_tensor("s5_y", [D, T, STEPS], F32, kind="Internal").ap()

    base = (nc.sbuf_base + 31) // 32 * 32

    def at(name, shape, dt, offset):
        return nc.alloc_sbuf_tensor_at(name, shape, dt, offset=base + offset)

    K = 1024
    o_x, o_h, o_g, o_w, o_raw, o_s = 0, 16 * K, 48 * K, 136 * K, 168 * K, 184 * K
    X = at("x_res", [P, DT, SEQ], F32, o_x)
    H = at("h_split", [P, DT, 2, SEQ], F32R, o_h)
    G = at("g_split", [P, FT, 2, SEQ], F32R, o_g)
    W = at("w_split", [P, RING, 2, 1024], F32R, o_w)
    RAW = at("w_raw", [P, RING, 1024], F32, o_raw)
    RSTD = at("rstd", [P, SEQ], F32, o_s)
    GT = at("gate", [P, SEQ], F32, o_s + 2 * K)
    UT = at("up", [P, SEQ], F32, o_s + 4 * K)
    ACC = at("sq_sum", [P, SEQ], F32, o_s + 6 * K)
    SQ = at("sq", [P, 2, SEQ], F32, o_s + 8 * K)
    CN = at("c_kv", [P, SEQ], F32, o_s + 12 * K)
    KR = at("k_rope", [P, SEQ], F32, o_s + 14 * K)
    COS = at("rope_cos", [P, SEQ], F32, o_s + 16 * K)
    SIN = at("rope_sin", [P, SEQ], F32, o_s + 18 * K)
    o_c = o_s + 20 * K
    COLS = at("cols", [P, N_COLS], F32, o_c)
    ONES = at("ones", [P, P], F32, o_c + 288)
    EYE = at("eye", [P, P], F32, o_c + 800)
    MASK = at("mask_rows", [1, P + 64], F32, o_c + 1312)
    STAT = at("attn_stat", [P, 32], F32, o_c + 2080)
    R8 = at("r8", [P, GROUPS], F32, o_c + 2208)
    assert base + o_c + 2208 + 4 * GROUPS <= nc.sbuf_top

    o_t = o_g + 10 * 4 * K
    t_at = [o_t]

    def tmp(name, shape, dt=F32):
        n = int(np.prod(shape[1:])) * 4
        t = at(name, shape, dt, t_at[0])
        t_at[0] += (n + 31) // 32 * 32
        assert t_at[0] <= o_w
        return t

    LAM = tmp("lam", [P, 3, GROUPS])
    PW = tmp("lam_pow", [P, 2, M, GROUPS])
    PA = tmp("u64_pow", [P, 2, 8, GROUPS])
    PB = tmp("u8_pow", [P, 2, 8, GROUPS])
    EC = tmp("e_coef", [P, 2, GROUPS])
    BC = tmp("bc_in", [P, 2, 4, GB * GC])
    WB = tmp("b_bar", [P, GB * GC])
    XB = tmp("b_bar_swapped", [P, GB * GC])
    CP = tmp("c_pow", [P, GB, M, GC])
    BP = tmp("b_pow", [P, GB, T, GC])
    OUTB = tmp("ops_out", [P, 2048])
    KT = tmp("k_window", [GC, GB, 15, GC])
    DS = tmp("d_skip", [GC, GROUPS])
    DI = tmp("d_eye", [GC, GB, GC])
    TM = tmp("s5_tmp", [P, GB * M * GC])
    ANG = at("ang", [P, SEQ], F32, o_g)
    AN = at("ang_n", [P, SEQ], F32, o_g + 2 * K)
    POS = at("pos", [P, SEQ], I32, o_g + 4 * K)
    S6 = at("s5_small", [P, 24, GROUPS], F32, o_g + 6 * K)

    HN = at("h_norm", [P, DT, T, STEPS], F32, o_h)
    UY = at("u_and_y", [P, GROUPS, STEPS], F32, o_h + 16 * K)
    N_SLOTS = 5
    SLOT = at("op_slots", [P, N_SLOTS, OPS], F32, o_g)
    o_5 = o_g + N_SLOTS * OPS * 4
    XS = at("state", [P, 2, GB, STEPS + 1], F32, o_5)
    ZS = at("state_turned", [P, SEQ], F32, o_5 + 2 * 2080)
    JP = at("swap_halves", [P, P], F32, o_5 + 2 * 2080 + 2 * K)
    YT = at("y_tokens", [P, DT, SEQ], F32, o_h)

    KN = at("k_nope", [P, HEADS, SEQ], F32, o_g)
    VV = at("v", [P, 4, HEADS * P], F32, o_g + 16 * K)
    QN = at("q_nope", [P, HEADS, SEQ], F32, o_g + 32 * K)
    QR = at("q_rope", [P, 4, SEQ], F32, o_g + 48 * K)
    PT = at("probs_t", [P, 2, 4, SEQ], F32, o_g + 56 * K)
    PR = at("probs", [P, 2, 4, SEQ], F32, o_g + 72 * K)
    CS = at("c_kv_split", [P, 2, SEQ], F32R, o_g + 72 * K)
    CQS = at("c_q_split", [P, 2, 2, SEQ], F32R, o_g + 80 * K)


    R2 = at("rstd_latent", [P, SEQ], F32, o_g + (FT - 1) * 4 * K)

    BK = [nc.alloc_psum_tensor(f"bank{i}", [P, SEQ], F32) for i in range(8)]

    def sem(name):
        return nc.alloc_semaphore(name)

    s_raw = [sem(f"pack_loaded{i}") for i in range(RING)]
    s_const, s_xin = sem("const_loaded"), sem("x_loaded")
    s_bc = [sem(f"bc_loaded{i}") for i in range(2)]
    s_opdma, s_jp = sem("ops_stored"), sem("swap_loaded")
    s_slot = [sem(f"slot_loaded{i}") for i in range(N_SLOTS)]
    s_ust = [sem(f"u_stored{i}") for i in range(2)]
    s_uld = [sem(f"u_loaded{i}") for i in range(2)]
    s_yst = [sem(f"y_stored{i}") for i in range(2)]
    s_yld = [sem(f"y_loaded{i}") for i in range(2)]
    s_out = sem("out_stored")
    s_hi, s_lo, s_used = sem("pack_hi"), sem("pack_lo"), sem("pack_used")
    s_h_hi, s_h_lo = sem("h_hi"), sem("h_lo")
    s_sq, s_sum, s_ssq = sem("sq_ready"), sem("sq_added"), sem("sum_of_squares")
    s_rcp, s_rstd = sem("rms_reciprocal"), sem("rstd_ready")
    s_read, s_silu, s_prod = sem("gate_up_read"), sem("silu_done"), sem("gated")
    s_g_hi, s_g_lo = sem("g_hi"), sem("g_lo")
    s_acc, s_x = sem("x_acc"), sem("x_updated")
    s_sig, s_glu = sem("glu_sigmoid"), sem("glu_gated")
    s_ch = sem("dve_step")
    s_expo, s_args, s_trig = sem("step_exponentials"), sem("angles_reduced"), sem("sin_cos")
    s_made, s_turned, s_taps, s_btc = sem("powers_made"), sem("ops_turned"), sem("taps_ready"), sem("b_op_copied")
    s_hn, s_s, s_sc, s_js, s_z, s_jz, s_xs, s_yp, s_y = (sem(n) for n in (
        "h_norm_ready", "step_input", "step_input_copied", "swapped_input", "z_ready", "swapped_z",
        "state_ready", "y_psum", "y_ready"))
    s_zero = sem("state_zeroed")
    s_y_hi, s_y_lo = sem("y_hi"), sem("y_lo")
    s_cn, s_cnsq = sem("latent_scaled"), sem("latent_squared")
    s_mm, s_ev_a, s_ev_v = sem("mid_product"), sem("mid_read_act"), sem("mid_read_dve")
    s_qr = sem("q_turned")
    s_cs_hi, s_cs_lo, s_cq_hi, s_cq_lo, s_cqsq, s_cqsum = (sem(n) for n in (
        "latent_hi", "latent_lo", "cq_hi", "cq_lo", "cq_squared", "cq_squares_added"))
    s_scores, s_max, s_exp, s_p, s_tp, s_pt, s_o, s_o_hi, s_o_lo = (sem(n) for n in (
        "scores", "neg_max", "exp_done", "probs_ready", "probs_turned", "probs_t_copied",
        "o_ready", "o_hi", "o_lo"))

    FFNS = [FFN0A, FFN0B, FFN1A, FFN1B]
    BASE = {FFN0A: 0, FFN0B: 4, FFN1A: 4, FFN1B: 0}
    OPS_STORES = 2 + T

    def col(c):
        return COLS[:, c:c + 1] if isinstance(c, int) else COLS[:, bass.ds(c, 1)]

    def out_bank(stage, d):
        return BK[(BASE[stage] + 4 + d) % 8]

    def gt_part(f, part):
        if isinstance(f, int):
            return G[:, f, part, :]
        return G[:, bass.ds(f, 1), part, :].rearrange("p a n -> p (a n)")

    def in_banks(base, f):
        return BK[base + 2 * (f % 2)], BK[base + 2 * (f % 2) + 1]

    def wait_acc(eng, stage, d):
        if d < DT - 1:
            eng.wait_ge(s_acc, (DT - 1) * FFNS.index(stage) + d + 1)
        else:
            eng.wait_ge(s_used, stage + FFN_PACKS)

    MQ, MSTAT, MK, MCQ, MV, MN, MR, MID = 0, 2, 3, 11, 12, 20, 28, 36
    ENDS = {MQ: DQ + 1, MQ + 1: DQ + 2, MK + 7: UKV + 1, MV + 7: UKV + 2, MN + 3: UQ + 1, MN + 7: UQ + 2,
            MR + 6: UQ + 3, MR + 7: UQ + 4}
    INNER = [m for m in range(MID) if m not in ENDS and m not in (MSTAT, MCQ)]

    def signal(ins, m):
        ins.then_inc(s_used if m in ENDS else s_mm, 1)

    def wait_product(eng, m):
        if m in ENDS:
            eng.wait_ge(s_used, ENDS[m])
        else:
            eng.wait_ge(s_mm, INNER.index(m) + 1)

    def wait_read(eng, m):
        if m < MSTAT:
            eng.wait_ge(s_cq_lo, m + 1)
            eng.wait_ge(s_cqsq, m + 1)
        elif MK <= m < MCQ:
            eng.wait_ge(s_ev_a, m - MK + 1)
        else:
            eng.wait_ge(s_ev_v, [MSTAT, *range(MCQ, MID)].index(m) + 1)

    with nc.Block() as block:

        @block.sync
        def _(sp):
            for k in range(DT):
                sp.dma_start(X[:, k, :], xT[k]).then_inc(s_xin, 16)
            for n in range(RING):
                sp.dma_start(RAW[:, n, :], wstream[n]).then_inc(s_raw[n], 16)
            turns = N_LOADS // RING
            with sp.Fori(1, turns) as i:
                for r in range(RING):
                    sp.wait_ge(s_lo, i * RING + (r - RING + 1))
                    sp.dma_start(RAW[:, r, :], wstream[i * RING + r]).then_inc(s_raw[r], 16)
            for n in range(RING * turns, N_LOADS):
                sp.wait_ge(s_lo, n - RING + 1)
                sp.dma_start(RAW[:, n % RING, :], wstream[n]).then_inc(s_raw[n % RING], 16)
            for k in range(DT):
                sp.wait_ge(s_x, 6 * DT + k + 1)
                sp.dma_start(out[k], X[:, k, :]).then_inc(s_out, 16)
            sp.wait_ge(s_out, 16 * DT)

        @block.gpsimd
        def _(pool):
            pool.dma_start(LAM[:], lam).then_inc(s_const, 16)
            pool.dma_start(COLS[:], cols).then_inc(s_const, 16)
            pool.dma_start(POS[:], pos).then_inc(s_const, 16)
            pool.dma_start(ONES[:], consts[0]).then_inc(s_const, 16)
            pool.dma_start(EYE[:], consts[1]).then_inc(s_const, 16)
            pool.dma_start(MASK[:], mask).then_inc(s_const, 16)
            pool.dma_start(DS[:], dskip).then_inc(s_const, 16)

            def sum_squares(n):
                for k in range(1, DT):
                    pool.wait_ge(s_sq, SUMS[n] * DT + k + 1)
                    if SUMS[n] * (DT - 1) + k > 1:
                        pool.wait_ge(s_sum, SUMS[n] * (DT - 1) + k - 1)
                    nc.gpsimd.tensor_tensor(ACC[:], ACC[:], SQ[:, k % 2, :], ALU.add).then_inc(s_sum, 1)

            def load_bc(k):
                pool.dma_start(BC[:, k % 2], bcd[k]).then_inc(s_bc[k % 2], 16)

            def store_ops(k):
                pool.wait_ge(s_taps, k + 1)
                pool.wait_ge(s_btc, k + 1)
                dst = ops_dram[k]
                pool.dma_start(dst[:, O_B:O_C], OUTB[:]).then_inc(s_opdma, 16)
                pool.dma_start(dst[:, O_C:O_T].rearrange("p (g n) -> p g n", g=GB),
                               CP[:, :, 1:M, :].rearrange("p g m c -> p g (m c)")).then_inc(s_opdma, 16)
                for s in range(T):
                    pool.dma_start(dst[s * GC:(s + 1) * GC, O_T:OPS].rearrange("c (g n) -> c g n", g=GB),
                                   KT[:, :, s:s + T, :].rearrange("c g t d -> c g (t d)")).then_inc(s_opdma, 16)

            load_bc(0)
            sum_squares(N_IN0A)
            for k in range(BLOCKS):
                if k + 1 < BLOCKS:
                    if k >= 1:
                        pool.wait_ge(s_made, k)
                    load_bc(k + 1)
                store_ops(k)
            pool.wait_ge(s_opdma, 16 * OPS_STORES * BLOCKS)
            for k in range(N_SLOTS):
                pool.wait_ge(s_used, FFN0A + IN_PACKS + 4 * k + 4)
                pool.dma_start(SLOT[:, k, :], ops_dram[k]).then_inc(s_slot[k], 16)
            pool.wait_ge(s_used, FFN0A + FFN_PACKS)
            pool.dma_start(JP[:], consts[2]).then_inc(s_jp, 16)
            sum_squares(N_S5)
            for half in range(2):
                pool.wait_ge(s_ust[half], 16 * DT // 2)
                g0 = half * GROUPS // 2
                for t in range(T):
                    r = T - 1 - t
                    pool.dma_start(UY[r * GC:(r + 1) * GC, g0:g0 + GROUPS // 2, :],
                                   u_dram[half * D // 2:(half + 1) * D // 2, t, :].rearrange("(g c) j -> c g j", c=GC)
                                   ).then_inc(s_uld[half], 16)
            for k in range(N_SLOTS, BLOCKS):
                pool.wait_ge(s_yp, k - N_SLOTS + 1)
                pool.dma_start(SLOT[:, k % N_SLOTS, :], ops_dram[k]).then_inc(s_slot[k % N_SLOTS], 16)
            for half in range(2):
                pool.wait_ge(s_y, BLOCKS // 2 * (half + 1))
                g0 = half * GROUPS // 2
                for t in range(T):
                    pool.dma_start(y_dram[half * D // 2:(half + 1) * D // 2, t, :].rearrange("(g c) j -> c g j", c=GC),
                                   UY[t * GC:(t + 1) * GC, g0:g0 + GROUPS // 2, :]).then_inc(s_yst[half], 16)
            for half in range(2):
                pool.wait_ge(s_yst[half], 16 * T)
                for k in range(half * DT // 2, (half + 1) * DT // 2):
                    pool.dma_start(YT[:, k, :], y_dram[k * P:(k + 1) * P].rearrange("p t j -> p (t j)")
                                   ).then_inc(s_yld[half], 16)
            sum_squares(N_IN0B)
            sum_squares(N_KV)
            sum_squares(N_DQ)
            pool.wait_ge(s_cqsq, 2)
            pool.wait_ge(s_ssq, N_DQ + 1)
            nc.gpsimd.tensor_tensor(ACC[:], SQ[:, 0, :], SQ[:, 1, :], ALU.add).then_inc(s_cqsum, 1)
            sum_squares(N_IN1B)
            sum_squares(N_FINAL)

        @block.scalar
        def _(act):
            def split(stage, j, i=None):
                c = stage + j + AHEAD
                r = c % RING
                turn = c // RING + 1
                if i is None:
                    act.wait_ge(s_raw[r], 16 * turn)
                    if c >= RING:
                        act.wait_ge(s_used, c - RING + 1)
                else:
                    act.wait_ge(s_raw[r], i * 16 + 16 * turn)
                    act.wait_ge(s_used, i * 4 + (c - RING + 1))
                nc.scalar.activation(W[:, r, 0, :], RAW[:, r, :], ACT.Copy).then_inc(s_hi, 1)

            def gate(stage, f):
                F = f + F_BASE[stage]
                act.wait_ge(s_read, F + 1)
                nc.scalar.activation(GT[:], GT[:], ACT.Silu).then_inc(s_silu, 1)
                act.wait_ge(s_prod, F + 1)
                nc.scalar.activation(gt_part(f, 0), GT[:], ACT.Copy).then_inc(s_g_hi, 1)

            def h_hi(k, gains, dst):
                nc.scalar.activation(dst[:, k, 0, :], X[:, k, :], ACT.Identity, scale=col(gains + k)).then_inc(s_h_hi, 1)

            def square(n, k):
                if k >= 3:
                    act.wait_ge(s_sum, SUMS[n] * (DT - 1) + k - 2)
                dst = ACC[:] if k == 0 else SQ[:, k % 2, :]
                nc.scalar.activation(dst, X[:, k, :], ACT.Square).then_inc(s_sq, 1)

            def root(n, dst=RSTD):
                act.wait_ge(s_rcp, n + 1)
                nc.scalar.activation(dst[:], dst[:], ACT.Sqrt).then_inc(s_rstd, 1)

            def ffn_in_loop(stage):
                nc.scalar.preload_act_table(ACT.Silu)
                with act.Fori(0, FT // 2 - 1) as i:
                    for a in range(2):
                        split(stage, 4 + 2 * a, i)
                        gate(stage, i * 2 + (1 + a))
                        split(stage, 4 + 2 * a + 1, i)

            def ffn_in(stage, n):
                split(stage, 0)
                split(stage, 1)
                split(stage, 2)
                root(n)
                gate(stage, 0)
                split(stage, 3)
                ffn_in_loop(stage)

            def ffn_out(stage):
                split(stage, IN_PACKS)
                gate(stage, FT - 1)
                split(stage, IN_PACKS + 1)
                with act.Fori(0, FT // 4) as i:
                    for j in range(4):
                        split(stage, IN_PACKS + 2 + j, i)

            act.wait_ge(s_const, 16 * 7)
            nc.scalar.activation(S6[:, 0, :], LAM[:, 2, :], ACT.Exp).then_inc(s_expo, 1)
            act.wait_ge(s_args, 1)
            nc.scalar.activation(S6[:, 7, :], S6[:, 6, :], ACT.Exp).then_inc(s_expo, 1)
            nc.scalar.activation(R8[:], S6[:, 6, :], ACT.Exp, scale=float(T)).then_inc(s_expo, 1)
            act.wait_ge(s_args, 2)
            nc.scalar.activation(S6[:, 4, :], S6[:, 2, :], ACT.Sin).then_inc(s_trig, 1)
            nc.scalar.activation(S6[:, 5, :], S6[:, 3, :], ACT.Sin).then_inc(s_trig, 1)
            act.wait_ge(s_args, 3)
            nc.scalar.activation(SIN[:], ANG[:], ACT.Sin).then_inc(s_trig, 1)
            nc.scalar.activation(COS[:], AN[:], ACT.Sin).then_inc(s_trig, 1)

            act.wait_ge(s_xin, 16 * DT)
            for k in range(DT):
                h_hi(k, G_IN0A, H)
            for k in range(DT):
                square(N_IN0A, k)
            for j in range(-AHEAD, 0):
                split(FFN0A, j)

            for k in range(BLOCKS):
                act.wait_ge(s_turned, k + 1)
                if k >= 1:
                    act.wait_ge(s_opdma, 16 * OPS_STORES * k)
                nc.scalar.activation(OUTB[:, O_B:O_B + 512], BK[2][:], ACT.Copy)
                nc.scalar.activation(OUTB[:, O_B + 512:O_B + 1024], BK[3][:], ACT.Copy).then_inc(s_btc, 1)

            act.wait_ge(s_opdma, 16 * OPS_STORES * BLOCKS)
            ffn_in(FFN0A, N_IN0A)
            ffn_out(FFN0A)

            for k in range(DT):
                act.wait_ge(s_x, X_BASE[FFN0A] + k + 1)
                square(N_S5, k)
            root(N_S5)
            for k in range(DT):
                act.wait_ge(s_hn, k + 1)
                act.dma_start(u_dram[k * P:(k + 1) * P], HN[:, k]).then_inc(s_ust[k // (DT // 2)], 16)

            def copy_s(k):
                act.wait_ge(s_s, k + 1)
                if k >= 2:
                    act.wait_ge(s_z, k - 1)
                nc.scalar.activation(SQ[:, k % 2, :], BK[k % 2][:], ACT.Copy).then_inc(s_sc, 1)

            def gelu(k):
                act.wait_ge(s_yp, k + 1)
                nc.scalar.activation(UY[:, k * GB:(k + 1) * GB, :].rearrange("p g j -> p (g j)"), BK[4 + k % 2][:],
                                     ACT.Gelu_apprx_tanh).then_inc(s_y, 1)

            for k in range(BLOCKS):
                copy_s(k)
                if k >= 1:
                    gelu(k - 1)
            gelu(BLOCKS - 1)
            for k in range(DT):
                act.wait_ge(s_yld[k // (DT // 2)], 16 * DT // 2)
                nc.scalar.activation(G[:, k, 0, :], YT[:, k, :], ACT.Copy).then_inc(s_y_hi, 1)

            def glu(k):
                act.wait_ge(s_used, GLU + 2 * k + 2)
                if k >= 1:
                    act.wait_ge(s_x, X_BASE[GLU] + k)
                nc.scalar.activation(GT[:], in_banks(0, k)[1][:], ACT.Sigmoid).then_inc(s_sig, 1)
                if k >= 1:
                    h_hi(k - 1, G_IN0B, H)
                    square(N_IN0B, k - 1)

            split(GLU, 0)
            split(GLU, 1)
            for f in range(1, DT):
                split(GLU, 2 * f)
                glu(f - 1)
                split(GLU, 2 * f + 1)
            split(FFN0B, 0)
            glu(DT - 1)
            act.wait_ge(s_x, X_BASE[GLU] + DT)
            h_hi(DT - 1, G_IN0B, H)
            square(N_IN0B, DT - 1)
            split(FFN0B, 1)
            split(FFN0B, 2)
            root(N_IN0B)
            gate(FFN0B, 0)
            split(FFN0B, 3)
            ffn_in_loop(FFN0B)
            ffn_out(FFN0B)

            for k in range(DT):
                act.wait_ge(s_x, X_BASE[FFN0B] + k + 1)
                h_hi(k, G_KV, G)
            for k in range(DT):
                h_hi(k, G_IN1A, H)
                square(N_KV, k)
            split(KVD, 0)
            split(KVD, 1)
            split(KVD, 2)
            split(FFN1A, 0)
            root(N_KV)
            act.wait_ge(s_cn, 1)
            nc.scalar.activation(SQ[:, 0, :], CN[:], ACT.Square).then_inc(s_cnsq, 1)
            split(FFN1A, 1)
            split(FFN1A, 2)
            gate(FFN1A, 0)
            split(FFN1A, 3)
            root(N_LAT, R2)
            ffn_in_loop(FFN1A)
            ffn_out(FFN1A)

            for k in range(DT):
                act.wait_ge(s_x, X_BASE[FFN1A] + k + 1)
                h_hi(k, G_DQ, H)
            act.wait_ge(s_cn, 2)
            nc.scalar.activation(CS[:, 0, :], CN[:], ACT.Copy).then_inc(s_cs_hi, 1)
            for k in range(DT):
                square(N_DQ, k)
            split(DQ, 0)
            split(DQ, 1)
            split(UKV, 0)
            for q in range(2):
                wait_product(act, MQ + q)
                nc.scalar.activation(CQS[:, q, 0, :], BK[q][:], ACT.Identity, scale=col(C_QN + q)).then_inc(s_cq_hi, 1)
            act.wait_ge(s_sum, (SUMS[N_DQ] + 1) * (DT - 1))
            for q in range(2):
                act.wait_ge(s_cq_lo, q + 1)
                nc.scalar.activation(SQ[:, q, :], BK[q][:], ACT.Square).then_inc(s_cqsq, 1)
            root(N_DQ)
            for h in range(HEADS):
                wait_product(act, MK + h)
                nc.scalar.activation(KN[:, h, :], BK[(MK + h) % 8][:], ACT.Copy).then_inc(s_ev_a, 1)
            split(UKV, 1)
            split(UQ, 0)
            root(N_CQ, UT)
            split(UQ, 1)
            split(UQ, 2)
            split(UQ, 3)

            def soft(h, t):
                i = 4 * h + t
                n = P * (t + 1)
                act.wait_ge(s_max, i + 1)
                if h >= 2:
                    act.wait_ge(s_tp, i - 7)
                nc.scalar.activation(PR[:, h % 2, t, 0:n], BK[t][:, 0:n], ACT.Exp, bias=STAT[:, 4 + t:5 + t],
                                     scale=QK_SCALE, accum_out=STAT[:, 8 + t:9 + t]).then_inc(s_exp, 1)

            def copy_pt(h, t):
                i = 4 * h + t
                act.wait_ge(s_tp, i + 1)
                if h >= 2:
                    act.wait_ge(s_o, h - 1)
                n = t + 1
                nc.scalar.activation(PT[:, h % 2, 0:n, t * P:(t + 1) * P],
                                     BK[4 + t % 2][:, 0:n * P].rearrange("p (a q) -> p a q", a=n),
                                     ACT.Copy).then_inc(s_pt, 1)

            def o_hi(h):
                act.wait_ge(s_o, h + 1)
                nc.scalar.activation(H[:, h, 0, :], BK[6 + h % 2][:], ACT.Copy).then_inc(s_o_hi, 1)

            for h in range(HEADS + 1):
                for t in range(4):
                    if h < HEADS:
                        soft(h, t)
                for t in range(4):
                    if h >= 1:
                        copy_pt(h - 1, t)
                if h >= 2:
                    o_hi(h - 2)
            o_hi(HEADS - 1)

            for d in range(DT):
                split(WO, d)
                if d >= 1:
                    act.wait_ge(s_x, X_BASE[WO] + d)
                    square(N_IN1B, d - 1)
            act.wait_ge(s_used, WO + DT)
            for k in range(DT):
                act.wait_ge(s_x, X_BASE[WO] + k + 1)
                h_hi(k, G_IN1B, H)
            square(N_IN1B, DT - 1)
            ffn_in(FFN1B, N_IN1B)
            ffn_out(FFN1B)

            for k in range(DT):
                act.wait_ge(s_x, X_BASE[FFN1B] + k + 1)
                square(N_FINAL, k)
            root(N_FINAL)

        @block.vector
        def _(dve):
            chain = [0]

            def link(ins):
                chain[0] += 1
                ins.then_inc(s_ch, 1)
                dve.wait_ge(s_ch, chain[0])

            tt, ts, stt = nc.vector.tensor_tensor, nc.vector.tensor_scalar, nc.vector.scalar_tensor_tensor

            def split(stage, j, i=None):
                c = stage + j + AHEAD
                r = c % RING
                dve.wait_ge(s_hi, c + 1 if i is None else i * 4 + (c + 1))
                tt(W[:, r, 1, :], RAW[:, r, :], W[:, r, 0, :].bitcast(F32), ALU.subtract).then_inc(s_lo, 1)

            def gated(stage, f, par, packs_done):
                F = f + F_BASE[stage]
                gb, ub = in_banks(BASE[stage], par)
                dve.wait_ge(s_used, packs_done)
                if not (isinstance(F, int) and F == 0):
                    dve.wait_ge(s_g_lo, F)
                tt(UT[:], ub[:], RSTD[:], ALU.mult)
                tt(GT[:], gb[:], RSTD[:], ALU.mult).then_inc(s_read, 1)
                dve.wait_ge(s_silu, F + 1)
                tt(GT[:], GT[:], UT[:], ALU.mult).then_inc(s_prod, 1)
                dve.wait_ge(s_g_hi, F + 1)
                tt(gt_part(f, 1), GT[:], gt_part(f, 0).bitcast(F32), ALU.subtract).then_inc(s_g_lo, 1)

            def h_lo(k, gains, dst, base):
                dve.wait_ge(s_h_hi, base + k + 1)
                stt(dst[:, k, 1, :], X[:, k, :], col(gains + k), dst[:, k, 0, :].bitcast(F32),
                    ALU.mult, ALU.subtract).then_inc(s_h_lo, 1)

            def mean_rcp(n, bank, width=D, dst=RSTD):
                dve.wait_ge(s_ssq, n + 1)
                link(ts(dst[:], bank[:], 1.0 / width, EPS, ALU.mult, ALU.add))
                nc.vector.reciprocal(dst[:], dst[:]).then_inc(s_rcp, 1)

            def ffn_in_loop(stage):
                with dve.Fori(0, FT // 2 - 1) as i:
                    for a in range(2):
                        split(stage, 4 + 2 * a, i)
                        gated(stage, i * 2 + (1 + a), (1 + a) % 2, i * 4 + (stage + 4 + 2 * a))
                        split(stage, 4 + 2 * a + 1, i)

            def ffn_in(stage, n):
                split(stage, 0)
                split(stage, 1)
                split(stage, 2)
                mean_rcp(n, BK[(BASE[stage] + 4) % 8])
                dve.wait_ge(s_rstd, n + 1)
                gated(stage, 0, 0, stage + 2)
                split(stage, 3)
                ffn_in_loop(stage)

            def ffn_out(stage):
                split(stage, IN_PACKS)
                gated(stage, FT - 1, 1, stage + IN_PACKS)
                split(stage, IN_PACKS + 1)
                with dve.Fori(0, FT // 4) as i:
                    for j in range(4):
                        split(stage, IN_PACKS + 2 + j, i)

            def add_ffn(stage, d):
                wait_acc(dve, stage, d)
                stt(X[:, d, :], out_bank(stage, d)[:], 0.5, X[:, d, :], ALU.mult, ALU.add).then_inc(s_x, 1)

            def reduced(ang, n, to_sin, to_cos):
                link(ts(n, ang, float(1 / (2 * np.pi)), 12582912.0, ALU.mult, ALU.add))
                link(ts(n, n, -12582912.0, None, ALU.add))
                link(stt(ang, n, -6.28125, ang, ALU.mult, ALU.add))
                c2 = float(np.float32(np.round((2 * np.pi - 6.28125) * 2**21) / 2**21))
                link(stt(ang, n, -c2, ang, ALU.mult, ALU.add))
                link(stt(ang, n, -float(np.float32(2 * np.pi - 6.28125 - c2)), ang, ALU.mult, ALU.add))
                link(ts(to_sin, ang, 3.1415925, -3.1415925, ALU.min, ALU.max))
                link(stt(to_cos, to_sin, -1.0, to_sin, ALU.mult, ALU.min))
                return ts(to_cos, to_cos, float(np.pi / 2), None, ALU.add)

            def cmul(dr, di, ar, ai, br, bi, t1, t2):
                tt(t1, ai, bi, ALU.mult)
                tt(t2, ar, bi, ALU.mult)
                tt(dr, ar, br, ALU.mult)
                link(tt(di, ai, br, ALU.mult))
                tt(dr, dr, t1, ALU.subtract)
                link(tt(di, di, t2, ALU.add))

            dve.wait_ge(s_const, 16 * 7)
            dve.wait_ge(s_expo, 1)
            link(tt(S6[:, 6, :], LAM[:, 0, :], S6[:, 0, :], ALU.mult))
            tt(S6[:, 1, :], LAM[:, 1, :], S6[:, 0, :], ALU.mult).then_inc(s_args, 1)
            dve.wait_ge(s_args, 1)
            reduced(S6[:, 1, :], S6[:, 8, :], S6[:, 2, :], S6[:, 3, :]).then_inc(s_args, 1)
            link(nc.vector.tensor_copy(ANG[:], POS[:]))
            link(ts(ANG[:], ANG[:], col(C_INVF), None, ALU.mult))
            reduced(ANG[:], UT[:], ANG[:], AN[:]).then_inc(s_args, 1)
            dve.wait_ge(s_trig, 4)
            link(ts(SIN[:], SIN[:], col(C_SGNR), None, ALU.mult))

            dve.wait_ge(s_xin, 16 * DT)
            for k in range(DT):
                h_lo(k, G_IN0A, H, H_BASE[FFN0A])
            for j in range(-AHEAD, 0):
                split(FFN0A, j)

            dve.wait_ge(s_expo, 3)
            t1, t2 = TM[:, 0:256], TM[:, 256:512]

            nc.vector.memset(PW[:, 0, 0, :], 1.0)
            nc.vector.memset(PW[:, 1, 0, :], 0.0)
            nc.vector.memset(PA[:, 0, 0, :], 1.0)
            nc.vector.memset(PA[:, 1, 0, :], 0.0)
            nc.vector.memset(PB[:, 0, 0, :], 1.0)
            nc.vector.memset(PB[:, 1, 0, :], 0.0)
            nc.vector.memset(KT[:, :, 0:T - 1, :], 0.0)
            link(ts(S6[:, 4, :], S6[:, 4, :], col(C_SGN), None, ALU.mult))
            tt(PW[:, 0, 1, :], S6[:, 7, :], S6[:, 5, :], ALU.mult)
            link(tt(PW[:, 1, 1, :], S6[:, 7, :], S6[:, 4, :], ALU.mult))

            def sq6(dst, src):
                cmul(dst[0], dst[1], src[0], src[1], src[0], src[1], t1[:, 0:GROUPS], t2[:, 0:GROUPS])

            u1 = (S6[:, 5, :], S6[:, 4, :])
            u2 = (S6[:, 9, :], S6[:, 10, :])
            u4 = (S6[:, 11, :], S6[:, 12, :])
            sq6(u2, u1)
            sq6(u4, u2)
            sq6((PB[:, 0, 1, :], PB[:, 1, 1, :]), u4)

            def powers(tab, top):
                m = 1
                while m < top:
                    q = min(m, top - m)
                    bc = [tab[:, ri, m:m + 1, :].broadcast_to([P, q, GROUPS]) for ri in range(2)]
                    v1, v2 = (t[:, 0:q * GROUPS].rearrange("p (q g) -> p q g", q=q) for t in (t1, t2))
                    cmul(tab[:, 0, m + 1:m + 1 + q, :], tab[:, 1, m + 1:m + 1 + q, :],
                         tab[:, 0, 1:1 + q, :], tab[:, 1, 1:1 + q, :], bc[0], bc[1], v1, v2)
                    m += q

            powers(PW, T)
            powers(PB, 7)
            sq6((PA[:, 0, 1, :], PA[:, 1, 1, :]), (PB[:, 0, 4, :], PB[:, 1, 4, :]))
            powers(PA, 7)

            lr, li = LAM[:, 0, :], S6[:, 13, :]
            nr, ni = S6[:, 14, :], PW[:, 1, 1, :]
            ts(li, LAM[:, 1, :], col(C_SGN), None, ALU.mult)
            link(ts(nr, PW[:, 0, 1, :], -1.0, None, ALU.add))
            tt(S6[:, 15, :], lr, lr, ALU.mult)
            tt(S6[:, 16, :], li, li, ALU.mult)
            tt(S6[:, 17, :], nr, lr, ALU.mult)
            tt(S6[:, 18, :], ni, li, ALU.mult)
            tt(S6[:, 19, :], ni, lr, ALU.mult)
            link(tt(S6[:, 20, :], nr, li, ALU.mult))
            tt(S6[:, 15, :], S6[:, 15, :], S6[:, 16, :], ALU.add)
            tt(S6[:, 17, :], S6[:, 17, :], S6[:, 18, :], ALU.add)
            link(tt(S6[:, 19, :], S6[:, 19, :], S6[:, 20, :], ALU.subtract))
            link(nc.vector.reciprocal(S6[:, 15, :], S6[:, 15, :]))
            tt(EC[:, 0, :], S6[:, 17, :], S6[:, 15, :], ALU.mult)
            link(tt(EC[:, 1, :], S6[:, 19, :], S6[:, 15, :], ALU.mult))

            for k in range(BLOCKS):
                g0, g1 = k * GB, (k + 1) * GB

                def chan(ap):
                    return ap.rearrange("p (g c) -> p g c", g=GB)

                wb, xb, cu, cv = (chan(BC[:, k % 2, q, :]) for q in range(4))
                er, ei = (EC[:, ri, g0:g1].unsqueeze(2).broadcast_to([P, GB, GC]) for ri in range(2))
                a1, a2 = chan(TM[:, 0:GB * GC]), chan(TM[:, 128:128 + GB * GC])
                dve.wait_ge(s_bc[k % 2], 16 * (k // 2 + 1))
                if k >= 1:
                    dve.wait_ge(s_turned, k)
                    dve.wait_ge(s_opdma, 16 * OPS_STORES * k)
                ts(BC[:, k % 2, 2:4, :], BC[:, k % 2, 2:4, :], col(C_SGN), None, ALU.mult)
                tt(a1, xb, ei, ALU.mult)
                tt(a2, wb, ei, ALU.mult)
                tt(chan(WB[:]), wb, er, ALU.mult)
                link(tt(chan(XB[:]), xb, er, ALU.mult))
                tt(chan(WB[:]), chan(WB[:]), a1, ALU.subtract)
                link(tt(chan(XB[:]), chan(XB[:]), a2, ALU.add))

                def power(tab, ri, m0, m1):
                    n = m1 - m0
                    return (tab[:, ri, m0:m1, g0:g1].rearrange("p m g -> p g m").unsqueeze(3)
                            .broadcast_to([P, GB, n, GC]))

                def spread(ap, n):
                    return ap.unsqueeze(2).broadcast_to([P, GB, n, GC])

                tmc = TM[:].rearrange("p (g m c) -> p g m c", g=GB, m=M)
                tmb = TM[:, 0:1024].rearrange("p (g m c) -> p g m c", g=GB, m=T)
                tt(CP[:], spread(cu, M), power(PW, 0, 0, M), ALU.mult)
                link(tt(tmc, spread(cv, M), power(PW, 1, 0, M), ALU.mult))
                tt(BP[:], spread(chan(WB[:]), T), power(PW, 0, 0, T), ALU.mult)
                link(tt(CP[:], CP[:], tmc, ALU.subtract))
                link(tt(tmb, spread(chan(XB[:]), T), power(PW, 1, 0, T), ALU.mult))
                tt(BP[:], BP[:], tmb, ALU.subtract).then_inc(s_made, 1)
                dve.wait_ge(s_made, k + 1)
                ar, ai = (PA[:, ri, :, g0:g1].rearrange("p a g -> p g a").unsqueeze(3).broadcast_to([P, GB, 8, 8])
                          for ri in range(2))
                br, bi = (PB[:, ri, :, g0:g1].rearrange("p b g -> p g b").unsqueeze(2).broadcast_to([P, GB, 8, 8])
                          for ri in range(2))
                ct, st, v1, v2 = (ap.rearrange("p (g a b) -> p g a b", g=GB, a=8) for ap in (
                    OUTB[:, O_COS:O_COS + 512], OUTB[:, O_SIN:O_SIN + 512], TM[:, 0:512], TM[:, 512:1024]))
                cmul(ct, st, ar, ai, br, bi, v1, v2)
                tt(DI[:], DS[:, g0:g1].unsqueeze(2).broadcast_to([GC, GB, GC]),
                   EYE[0:GC, 0:GC].unsqueeze(1).broadcast_to([GC, GB, GC]), ALU.mult)
                dve.wait_ge(s_turned, k + 1)
                for q in range(2):
                    ins = nc.vector.tensor_copy(KT[:, 4 * q:4 * q + 4, T - 1:, :].rearrange("c g t d -> c g (t d)"),
                                                BK[q][0:GC, :].rearrange("c (g n) -> c g n", g=4))
                link(ins)
                tt(KT[:, :, T - 1, :], KT[:, :, T - 1, :], DI[:], ALU.add).then_inc(s_taps, 1)

            ffn_in(FFN0A, N_IN0A)
            ffn_out(FFN0A)

            for d in range(DT):
                add_ffn(FFN0A, d)
            mean_rcp(N_S5, BK[4])
            dve.wait_ge(s_rstd, N_S5 + 1)
            for k in range(DT):
                stt(HN[:, k].rearrange("p t j -> p j t"), X[:, k, :].rearrange("p (j t) -> p j t", t=T),
                    col(G_S5 + k), RSTD[:].rearrange("p (j t) -> p j t", t=T), ALU.mult, ALU.mult).then_inc(s_hn, 1)
            nc.vector.memset(XS[:, :, :, 0:1], 0.0).then_inc(s_zero, 1)
            for k in range(BLOCKS):
                ops = SLOT[:, k % N_SLOTS]
                cosb, sinb = ops[:, O_COS:O_COS + 512], ops[:, O_SIN:O_SIN + 512]
                dve.wait_ge(s_sc, k + 1)
                if k >= 1:
                    dve.wait_ge(s_xs, k)
                tt(GT[:], SQ[:, k % 2, :], cosb, ALU.mult)
                dve.wait_ge(s_js, k + 1)
                link(tt(UT[:], BK[2 + k % 2][:], sinb, ALU.mult))
                link(tt(GT[:], GT[:], UT[:], ALU.add))
                for g in range(GB):
                    ins = nc.vector.tensor_tensor_scan(
                        ZS[:, g * STEPS:(g + 1) * STEPS], R8[:, k * GB + g:k * GB + g + 1].broadcast_to([P, STEPS]),
                        GT[:, g * STEPS:(g + 1) * STEPS], 0.0, ALU.mult, ALU.add)
                ins.then_inc(s_z, 1)
                dve.wait_ge(s_z, k + 1)
                tt(GT[:], ZS[:], cosb, ALU.mult)
                dve.wait_ge(s_jz, k + 1)
                link(tt(UT[:], BK[6 + k % 2][:], sinb, ALU.mult))
                if k >= 2:
                    dve.wait_ge(s_yp, k - 1)
                tt(XS[:, k % 2, :, 1:], GT[:].rearrange("p (g j) -> p g j", g=GB),
                   UT[:].rearrange("p (g j) -> p g j", g=GB), ALU.subtract).then_inc(s_xs, 1)
            for k in range(DT):
                dve.wait_ge(s_y_hi, k + 1)
                tt(G[:, k, 1, :], YT[:, k, :], G[:, k, 0, :].bitcast(F32), ALU.subtract).then_inc(s_y_lo, 1)

            def glu(k):
                dve.wait_ge(s_sig, k + 1)
                dve.wait_ge(s_x, X_BASE[GLU] + k)
                tt(UT[:], in_banks(0, k)[0][:], GT[:], ALU.mult).then_inc(s_glu, 1)
                dve.wait_ge(s_glu, k + 1)
                xk = X[:, k, :].rearrange("p (j t) -> p t j", t=T)
                tt(xk, xk, UT[:].rearrange("p (t j) -> p t j", t=T), ALU.add).then_inc(s_x, 1)
                if k >= 1:
                    h_lo(k - 1, G_IN0B, H, H_BASE[FFN0B])

            split(GLU, 0)
            split(GLU, 1)
            for f in range(1, DT):
                split(GLU, 2 * f)
                glu(f - 1)
                split(GLU, 2 * f + 1)
            split(FFN0B, 0)
            glu(DT - 1)
            h_lo(DT - 1, G_IN0B, H, H_BASE[FFN0B])
            split(FFN0B, 1)
            split(FFN0B, 2)
            mean_rcp(N_IN0B, BK[0])
            dve.wait_ge(s_rstd, N_IN0B + 1)
            gated(FFN0B, 0, 0, FFN0B + 2)
            split(FFN0B, 3)
            ffn_in_loop(FFN0B)
            ffn_out(FFN0B)

            for d in range(DT):
                add_ffn(FFN0B, d)
                if d >= 1:
                    h_lo(d - 1, G_KV, G, H_BASE[KVD])
            h_lo(DT - 1, G_KV, G, H_BASE[KVD])
            for k in range(DT):
                h_lo(k, G_IN1A, H, H_BASE[FFN1A])
            split(KVD, 0)
            split(KVD, 1)
            split(KVD, 2)
            split(FFN1A, 0)
            mean_rcp(N_KV, BK[3])
            dve.wait_ge(s_rstd, N_KV + 1)
            tt(KR[:], BK[1][:], RSTD[:], ALU.mult)
            tt(UT[:], BK[2][:], RSTD[:], ALU.mult)
            tt(CN[:], BK[0][:], RSTD[:], ALU.mult).then_inc(s_cn, 1)
            dve.wait_ge(s_cn, 1)
            tt(KR[:], KR[:], COS[:], ALU.mult)
            link(tt(UT[:], UT[:], SIN[:], ALU.mult))
            link(tt(KR[:], KR[:], UT[:], ALU.add))
            split(FFN1A, 1)
            split(FFN1A, 2)
            gated(FFN1A, 0, 0, FFN1A + 2)
            split(FFN1A, 3)
            mean_rcp(N_LAT, BK[3], P, R2)
            dve.wait_ge(s_rstd, N_LAT + 1)
            stt(CN[:], CN[:], col(C_LAT), R2[:], ALU.mult, ALU.mult).then_inc(s_cn, 1)
            ffn_in_loop(FFN1A)
            ffn_out(FFN1A)

            for d in range(DT):
                add_ffn(FFN1A, d)
                if d >= 1:
                    h_lo(d - 1, G_DQ, H, H_BASE[DQ])
            h_lo(DT - 1, G_DQ, H, H_BASE[DQ])
            dve.wait_ge(s_cs_hi, 1)
            tt(CS[:, 1, :], CN[:], CS[:, 0, :].bitcast(F32), ALU.subtract).then_inc(s_cs_lo, 1)
            split(DQ, 0)
            split(DQ, 1)
            split(UKV, 0)
            for q in range(2):
                dve.wait_ge(s_cq_hi, q + 1)
                stt(CQS[:, q, 1, :], BK[q][:], col(C_QN + q), CQS[:, q, 0, :].bitcast(F32),
                    ALU.mult, ALU.subtract).then_inc(s_cq_lo, 1)
            dve.wait_ge(s_ssq, N_DQ + 1)
            ts(RSTD[:], BK[MSTAT % 8][:], 1.0 / D, EPS, ALU.mult, ALU.add).then_inc(s_ev_v, 1)
            dve.wait_ge(s_ev_v, 1)
            nc.vector.reciprocal(RSTD[:], RSTD[:]).then_inc(s_rcp, 1)
            dve.wait_ge(s_rstd, N_DQ + 1)
            dve.wait_ge(s_ssq, N_CQ + 1)
            ts(UT[:], BK[MCQ % 8][:], 1.0 / 256, None, ALU.mult).then_inc(s_ev_v, 1)
            dve.wait_ge(s_ev_v, 2)
            link(tt(UT[:], UT[:], RSTD[:], ALU.mult))
            link(tt(UT[:], UT[:], RSTD[:], ALU.mult))
            link(ts(UT[:], UT[:], EPS, None, ALU.add))
            nc.vector.reciprocal(UT[:], UT[:]).then_inc(s_rcp, 1)
            for m in range(8):
                wait_product(dve, MV + m)
                nc.vector.tensor_copy(VV[:, m // 2, (m % 2) * 512:(m % 2 + 1) * 512], BK[(MV + m) % 8][:]).then_inc(s_ev_v, 1)
            split(UKV, 1)
            split(UQ, 0)
            dve.wait_ge(s_rstd, N_CQ + 1)
            link(tt(UT[:], UT[:], RSTD[:], ALU.mult))
            tt(COS[:], COS[:], UT[:], ALU.mult)
            tt(SIN[:], SIN[:], UT[:], ALU.mult)
            for h in range(HEADS):
                if h == 4:
                    split(UQ, 1)
                wait_product(dve, MN + h)
                tt(QN[:, h, :], BK[(MN + h) % 8][:], UT[:], ALU.mult).then_inc(s_ev_v, 1)
            split(UQ, 2)
            split(UQ, 3)
            for q in range(4):
                ea, eb = MR + 2 * q, MR + 2 * q + 1
                wait_product(dve, ea)
                tt(QR[:, q, :], BK[ea % 8][:], COS[:], ALU.mult).then_inc(s_ev_v, 1)
                wait_product(dve, eb)
                tt(GT[:], BK[eb % 8][:], SIN[:], ALU.mult).then_inc(s_ev_v, 1)
                wait_read(dve, eb)
                tt(QR[:, q, :], QR[:, q, :], GT[:], ALU.add).then_inc(s_qr, 1)
                dve.wait_ge(s_qr, q + 1)

            def top(h, t):
                i = 4 * h + t
                dve.wait_ge(s_scores, i + 1)
                link(nc.vector.reduce_max(STAT[:, t:t + 1], BK[t][:, 0:P * (t + 1)], AX.X))
                ts(STAT[:, 4 + t:5 + t], STAT[:, t:t + 1], -QK_SCALE, None, ALU.mult).then_inc(s_max, 1)

            def scale(h, t):
                i = 4 * h + t
                n = P * (t + 1)
                dve.wait_ge(s_exp, i + 1)
                link(nc.vector.reciprocal(STAT[:, 12 + t:13 + t], STAT[:, 8 + t:9 + t]))
                ts(PR[:, h % 2, t, 0:n], PR[:, h % 2, t, 0:n], STAT[:, 12 + t:13 + t], None, ALU.mult).then_inc(s_p, 1)
                dve.wait_ge(s_p, i + 1)

            def o_lo(h):
                dve.wait_ge(s_o_hi, h + 1)
                tt(H[:, h, 1, :], BK[6 + h % 2][:], H[:, h, 0, :].bitcast(F32), ALU.subtract).then_inc(s_o_lo, 1)

            for h in range(HEADS):
                for t in range(4):
                    top(h, t)
                    if t >= 1:
                        scale(h, t - 1)
                scale(h, 3)
                if h >= 2:
                    o_lo(h - 2)
            o_lo(HEADS - 2)
            o_lo(HEADS - 1)

            def add_wo(d):
                dve.wait_ge(s_used, WO + d + 1)
                tt(X[:, d, :], X[:, d, :], BK[d][:], ALU.add).then_inc(s_x, 1)

            for d in range(DT):
                split(WO, d)
                if d >= 1:
                    add_wo(d - 1)
            add_wo(DT - 1)
            for k in range(DT):
                h_lo(k, G_IN1B, H, H_BASE[FFN1B])
            ffn_in(FFN1B, N_IN1B)
            ffn_out(FFN1B)

            for d in range(DT):
                add_ffn(FFN1B, d)
            mean_rcp(N_FINAL, BK[4])
            dve.wait_ge(s_rstd, N_FINAL + 1)
            for k in range(DT):
                stt(X[:, k, :], X[:, k, :], col(G_FIN + k), RSTD[:], ALU.mult, ALU.mult).then_inc(s_x, 1)

        @block.tensor
        def _(pe):
            mm = nc.tensor.matmul

            def three(bank, hi, lo, x_hi, x_lo, start, cols=None):
                mm(bank, hi, x_hi, start=start, stop=True, skip_group_check=True)
                mm(bank, hi, x_lo, start=False, stop=True, skip_group_check=True)
                return mm(bank, lo, x_hi, start=False, stop=True, skip_group_check=True)

            def tile(c, k):
                r = c % RING
                return W[:, r, 0, k * P:(k + 1) * P], W[:, r, 1, k * P:(k + 1) * P]

            def pack(n):
                pe.wait_ge(s_lo, n + 1)

            def column(c, bank, src, wait=None):
                for k in range(DT):
                    if wait:
                        wait(k)
                    last = three(bank[:], *tile(c, k), src[:, k, 0, :], src[:, k, 1, :], k == 0)
                last.then_inc(s_used, 1)

            def stat(n, bank):
                pe.wait_ge(s_sum, (SUMS[n] + 1) * (DT - 1))
                mm(bank[:], ONES[:], ACC[:], start=True, stop=True).then_inc(s_ssq, 1)

            def first_pair(stage, base, src, wait):
                banks = in_banks(base, 0)
                for k in range(DT):
                    wait(k)
                    for q in range(2):
                        if k == 0:
                            pack(stage + q)
                        last = three(banks[q][:], *tile(stage + q, k), src[:, k, 0, :], src[:, k, 1, :], k == 0)
                        if k == DT - 1:
                            last.then_inc(s_used, 1)

            def in_tile(stage, f, par, base, src, i=None):
                for q in range(2):
                    c = stage + f * 2 + q
                    pack(c if i is None else i * 4 + c)
                    column(c, in_banks(base, par)[q], src)

            def ffn_in(stage, src, wait, between=None, after=None):
                base = BASE[stage]
                first_pair(stage, base, src, wait)
                if between:
                    between()
                in_tile(stage, 1, 1, base, src)
                if after:
                    after()
                with pe.Fori(0, FT // 2 - 1) as i:
                    for a in range(2):
                        pe.wait_ge(s_read, i * 2 + (F_BASE[stage] + a + 1))
                        in_tile(stage, 2 + a, a, base, src, i)

            def ffn_out(stage):
                F = F_BASE[stage]

                def row(j, c, n, x_hi, x_lo, last_row=False):
                    pack(n)
                    for d in range(DT):
                        if j == 0 and d in (4, 6):
                            pe.wait_ge(s_read, F + FT - 1 + (d == 6))
                        last = three(out_bank(stage, d)[:], *tile(c, d), x_hi, x_lo, j == 0)
                        if last_row and d < DT - 1:
                            last.then_inc(s_acc, 1)
                    last.then_inc(s_used, 1)

                for j in range(2):
                    pe.wait_ge(s_g_lo, F + j + 1)
                    row(j, stage + IN_PACKS + j, stage + IN_PACKS + j, G[:, j, 0, :], G[:, j, 1, :])
                pe.wait_ge(s_g_lo, F + FT - 2)
                with pe.Fori(0, FT // 4 - 1) as i:
                    for a in range(4):
                        f = i * 4 + (2 + a)
                        c = stage + IN_PACKS + 2 + a
                        row(2 + a, c, i * 4 + c, gt_part(f, 0), gt_part(f, 1))
                pe.wait_ge(s_g_lo, F + FT)
                for j in range(FT - 4, FT):
                    n = stage + IN_PACKS + j
                    row(j, n, n, G[:, j, 0, :], G[:, j, 1, :], j == FT - 1)

            pe.wait_ge(s_const, 16 * 7)
            for k in range(BLOCKS):
                pe.wait_ge(s_made, k + 1)
                if k >= 1:
                    pe.wait_ge(s_taps, k)
                    pe.wait_ge(s_btc, k)
                for g in range(GB):
                    mm(BK[g // 4][0:GC, (g % 4) * P:(g % 4 + 1) * P], WB[:, g * GC:(g + 1) * GC],
                       CP[:, g, 0:T, :].rearrange("p m c -> p (m c)"), start=(g % 4 == 0), stop=True,
                       skip_group_check=True)
                for g in range(GB):
                    last = nc.tensor.transpose(BK[2 + g // 4][:, (g % 4) * P:(g % 4 + 1) * P],
                                               BP[:, g].rearrange("p m c -> p (m c)"), EYE[:])
                last.then_inc(s_turned, 1)

            pe.wait_ge(s_taps, BLOCKS)
            pe.wait_ge(s_btc, BLOCKS)
            ffn_in(FFN0A, H, lambda k: pe.wait_ge(s_h_lo, H_BASE[FFN0A] + k + 1), between=lambda: stat(N_IN0A, BK[4]))
            ffn_out(FFN0A)

            pe.wait_ge(s_x, X_BASE[FFN0A] + DT)
            stat(N_S5, BK[4])

            def group(ap, g, n=P):
                return ap[:, g * n:(g + 1) * n]

            def step_input(k):
                ops = SLOT[:, k % N_SLOTS]
                if k % 4 == 0:
                    pe.wait_ge(s_uld[k // 4], 16 * T)
                pe.wait_ge(s_slot[k % N_SLOTS], 16 * (k // N_SLOTS + 1))
                if k >= 2:
                    pe.wait_ge(s_sc, k - 1)
                for g in range(GB):
                    last = mm(group(BK[k % 2], g, STEPS), group(ops[:, O_B:O_B + 1024], g), UY[:, k * GB + g, :],
                              start=(g == 0), stop=True, skip_group_check=True)
                last.then_inc(s_s, 1)

            def block_out(k):
                ops = SLOT[:, k % N_SLOTS]
                pe.wait_ge(s_sc, k + 1)
                mm(BK[2 + k % 2][:], JP[:], SQ[:, k % 2, :], start=True, stop=True).then_inc(s_js, 1)
                if k >= 2:
                    pe.wait_ge(s_y, k - 1)
                for g in range(GB):
                    mm(group(BK[4 + k % 2], g, STEPS), group(ops[:, O_T:OPS], g), UY[:, k * GB + g, :],
                       start=(g == 0), stop=True, skip_group_check=True)
                pe.wait_ge(s_z, k + 1)
                mm(BK[6 + k % 2][:], JP[:], ZS[:], start=True, stop=True).then_inc(s_jz, 1)
                pe.wait_ge(s_xs, k + 1)
                for g in range(GB):
                    last = mm(group(BK[4 + k % 2], g, STEPS), group(ops[:, O_C:O_T], g), XS[:, k % 2, g, 0:STEPS],
                              start=False, stop=True, skip_group_check=True)
                last.then_inc(s_yp, 1)

            pe.wait_ge(s_jp, 16)
            pe.wait_ge(s_zero, 1)
            step_input(0)
            for k in range(BLOCKS):
                if k + 1 < BLOCKS:
                    step_input(k + 1)
                block_out(k)

            first_pair(GLU, 0, G, lambda k: pe.wait_ge(s_y_lo, k + 1))
            for f in range(1, DT):
                if f >= 2:
                    pe.wait_ge(s_glu, f - 1)
                in_tile(GLU, f, f % 2, 0, G)

            ffn_in(FFN0B, H, lambda k: pe.wait_ge(s_h_lo, H_BASE[FFN0B] + k + 1), between=lambda: stat(N_IN0B, BK[0]))
            ffn_out(FFN0B)
            for q in range(3):
                pack(KVD + q)
                column(KVD + q, BK[q], G,
                       (lambda k: (pe.wait_ge(s_h_lo, H_BASE[KVD] + k + 1), pe.wait_ge(s_x, X_BASE[FFN0B] + 1 + k))) if q == 0 else None)
            stat(N_KV, BK[3])

            def latent_stat():
                pe.wait_ge(s_cnsq, 1)
                pe.wait_ge(s_rcp, N_KV + 1)
                mm(BK[3][:], ONES[:], SQ[:, 0, :], start=True, stop=True).then_inc(s_ssq, 1)

            ffn_in(FFN1A, H, lambda k: pe.wait_ge(s_h_lo, H_BASE[FFN1A] + k + 1), after=latent_stat)
            ffn_out(FFN1A)

            def free(m):
                if m >= 8:
                    wait_read(pe, m - 8)
                return BK[m % 8]

            def product(m, c, tiles, src):
                b = free(m)
                for q, k in enumerate(tiles):
                    last = three(b[:], *tile(c, k), src[q][0], src[q][1], q == 0)
                signal(last, m)

            for q in range(2):
                pack(DQ + q)
                for k in range(DT):
                    if q == 0:
                        pe.wait_ge(s_h_lo, H_BASE[DQ] + k + 1)
                    last = three(BK[q][:], *tile(DQ + q, k), H[:, k, 0, :], H[:, k, 1, :], k == 0)
                signal(last, MQ + q)
            pe.wait_ge(s_sum, (SUMS[N_DQ] + 1) * (DT - 1))
            mm(BK[MSTAT][:], ONES[:], ACC[:], start=True, stop=True).then_inc(s_ssq, 1)
            pe.wait_ge(s_cs_lo, 1)
            pack(UKV)
            for h in range(HEADS):
                product(MK + h, UKV, [h], [(CS[:, 0, :], CS[:, 1, :])])
            pe.wait_ge(s_cqsum, 1)
            free(MCQ)
            mm(BK[MCQ % 8][:], ONES[:], ACC[:], start=True, stop=True).then_inc(s_ssq, 1)
            pack(UKV + 1)
            for m in range(8):
                t, half = m // 2, m % 2
                b = free(MV + m)
                r = (UKV + 1) % RING
                tok = slice(t * P, (t + 1) * P)
                w_hi, w_lo = (W[:, r, q, half * 512:(half + 1) * 512] for q in range(2))
                mm(b[:], CS[:, 0, tok], w_hi, start=True, stop=True, skip_group_check=True)
                mm(b[:], CS[:, 0, tok], w_lo, start=False, stop=True, skip_group_check=True)
                signal(mm(b[:], CS[:, 1, tok], w_hi, start=False, stop=True, skip_group_check=True), MV + m)
            pe.wait_ge(s_cq_lo, 2)
            cq = [(CQS[:, q, 0, :], CQS[:, q, 1, :]) for q in range(2)]
            for h in range(HEADS):
                if h % 4 == 0:
                    pack(UQ + h // 4)
                product(MN + h, UQ + h // 4, [2 * (h % 4), 2 * (h % 4) + 1], cq)
            pack(UQ + 3)
            for q in range(4):
                for side in range(2):
                    product(MR + 2 * q + side, UQ + 2 + side, [2 * q, 2 * q + 1], cq)

            wait_read(pe, MCQ - 1)
            wait_read(pe, MID - 1)
            pe.wait_ge(s_qr, 4)

            def scores(h, t):
                if h >= 1:
                    pe.wait_ge(s_exp, 4 * (h - 1) + t + 1)
                n = P * (t + 1)
                q0 = 64 * (h % 2)
                mm(BK[t][:, 0:n], QN[:, h, t * P:(t + 1) * P], KN[:, h, 0:n], start=True, stop=True, skip_group_check=True)
                mm(BK[t][:, 0:n], QR[q0:q0 + 64, h // 2, t * P:(t + 1) * P], KR[q0:q0 + 64, 0:n],
                   start=False, stop=True, skip_group_check=True)
                mm(BK[t][:, n - 64:n], MASK[0:1, 0:P], MASK[0:1, P:P + 64], start=False, stop=True,
                   skip_group_check=True).then_inc(s_scores, 1)

            def turn(h, t):
                i = 4 * h + t
                pe.wait_ge(s_p, i + 1)
                if i >= 2:
                    pe.wait_ge(s_pt, i - 1)
                for a in range(t + 1):
                    last = nc.tensor.transpose(BK[4 + t % 2][:, a * P:(a + 1) * P],
                                               PR[:, h % 2, t, a * P:(a + 1) * P], EYE[:])
                last.then_inc(s_tp, 1)

            def values(h):
                if h >= 2:
                    pe.wait_ge(s_o_lo, h - 1)
                pe.wait_ge(s_pt, 4 * h + 4)
                for a in range(4):
                    last = mm(BK[6 + h % 2][:, a * P:], VV[:, a, h * P:(h + 1) * P], PT[:, h % 2, a, a * P:],
                              start=(a == 0), stop=True, skip_group_check=True)
                last.then_inc(s_o, 1)

            for h in range(HEADS + 1):
                if h < HEADS:
                    for t in range(4):
                        scores(h, t)
                if h >= 1:
                    for t in range(4):
                        turn(h - 1, t)
                    values(h - 1)

            for d in range(DT):
                pack(WO + d)
                if d in (4, 6, 7):
                    pe.wait_ge(s_o_lo, HEADS)
                column(WO + d, BK[d], H, (lambda k: pe.wait_ge(s_o_lo, k + 1)) if d == 0 else None)

            ffn_in(FFN1B, H, lambda k: pe.wait_ge(s_h_lo, H_BASE[FFN1B] + k + 1), between=lambda: stat(N_IN1B, BK[4]))
            ffn_out(FFN1B)
            pe.wait_ge(s_x, X_BASE[FFN1B] + DT)
            stat(N_FINAL, BK[4])

    return nc


def column_packs(w):
    k, n = w.shape
    return w.reshape(k // P, P, n // P, P).transpose(2, 1, 0, 3).reshape(n // P, P, k)


def weight_stream(ffn_w_in, ffn_w_out, s5_w_glu, w_dkv, w_ukv, mla_w_dq, mla_w_uq, mla_w_o):
    s = np.zeros((N_LOADS, P, 1024), np.float32)

    def gated(at, w, n):
        packs = column_packs(w)
        s[at:at + 2 * n:2], s[at + 1:at + 2 * n:2] = packs[:n], packs[n:]

    for at, layer, i in ((FFN0A, 0, 0), (FFN0B, 0, 1), (FFN1A, 1, 0), (FFN1B, 1, 1)):
        gated(at, ffn_w_in[layer, i], FT)
        s[at + IN_PACKS:at + FFN_PACKS] = ffn_w_out[layer, i].reshape(FT, P, D)
    gated(GLU, s5_w_glu[0], DT)
    s[KVD] = column_packs(w_dkv[:, :P])[0]
    r = w_dkv[:, P:]
    x = np.concatenate([r[:, 32:], r[:, :32]], 1)
    s[KVD + 1] = column_packs(np.concatenate([r, r], 1))[0]
    s[KVD + 2] = column_packs(np.concatenate([x, x], 1))[0]
    ukv = w_ukv.reshape(P, HEADS, 2, P)
    s[UKV], s[UKV + 1] = ukv[:, :, 0].reshape(P, 1024), ukv[:, :, 1].reshape(P, 1024)
    s[DQ:DQ + 2] = column_packs(mla_w_dq[0])
    uq = mla_w_uq[0].reshape(2, P, HEADS, 192)
    nope = uq[..., :P].transpose(1, 2, 0, 3).reshape(P, 2, 1024)
    s[UQ], s[UQ + 1] = nope[:, 0], nope[:, 1]
    rope = uq[..., P:]
    swap = np.concatenate([rope[..., 32:], rope[..., :32]], -1)
    for q, part in enumerate((rope, swap)):
        s[UQ + 2 + q] = part.reshape(2, P, 4, 2, 64).transpose(1, 2, 0, 3, 4).reshape(P, 1024)
    s[WO:WO + DT] = column_packs(mla_w_o[0])
    return s


def kernel(**inputs):
    import concourse.bacc as bacc
    from concourse.bass_utils import run_bass_kernel_spmd

    a = {k: np.asarray(v) for k, v in inputs.items()}
    f = np.float32

    def columns(v):
        return v.reshape(-1, P).T

    g = a["norm_gains"]
    half, quarter = np.repeat([1.0, -1.0], 64), np.tile(np.repeat([-1.0, 1.0], 32), 2)
    inv_freq = (1.0 / (f(10000.0) ** (np.arange(0, 64, 2, dtype=f) / f(64)))).astype(f)
    cols = np.concatenate([columns(v) for v in (
        g[0, 0], g[0, 1], g[0, 2], a["kv_in_norm"], g[1, 0], g[1, 1], g[1, 2], a["final_norm"],
        a["kv_latent_norm"], a["mla_q_norm"][0], half.astype(f), quarter.astype(f), np.tile(inv_freq, 4))], 1)
    eye = np.eye(P, dtype=f)
    consts = np.stack([np.ones((P, P), f), eye, np.roll(eye, 64, 0)])
    mask = np.concatenate([np.repeat([1.0, 0.0], 64), np.full(64, NEG)]).astype(f)[None]

    def states(v):
        return np.concatenate([v.T, v.T], 0)

    lam = np.stack([states(a["s5_lambda_re"][0]), states(a["s5_lambda_im"][0]),
                    np.broadcast_to(a["s5_log_step"][0], (P, GROUPS))], 1)
    b_re, b_im = (a[n][0].transpose(1, 0, 2) for n in ("s5_b_re", "s5_b_im"))
    c_re, c_im = (a[n][0].transpose(2, 0, 1) for n in ("s5_c_re", "s5_c_im"))
    bcd = np.stack([np.concatenate(v, 0) for v in ((b_re, b_im), (b_im, b_re), (c_re, c_im), (c_im, c_re))], 1)
    bcd = bcd.reshape(P, 4, BLOCKS, GB * GC).transpose(2, 0, 1, 3)
    arrays = {
        "xT": a["x"][0].T.reshape(DT, P, SEQ),
        "wstream": weight_stream(*(a[n] for n in ("ffn_w_in", "ffn_w_out", "s5_w_glu", "w_dkv", "w_ukv",
                                                  "mla_w_dq", "mla_w_uq", "mla_w_o"))),
        "cols": cols, "consts": consts, "mask": mask,
        "pos": np.broadcast_to(a["positions"], (P, SEQ)),
        "lam": lam, "bcd": bcd, "dskip": a["s5_d"][0].reshape(GROUPS, GC).T,
    }
    arrays = {k: np.ascontiguousarray(v) for k, v in arrays.items()}

    nc = bacc.Bacc("TRN2", target_bir_lowering=False, num_devices=1)
    aps = {k: nc.dram_tensor(k, v.shape, mybir.dt.from_np(v.dtype), kind="ExternalInput").ap()
           for k, v in arrays.items()}
    out = nc.dram_tensor("out", (DT, P, SEQ), F32, kind="ExternalOutput").ap()
    build(nc, out=out, **aps)
    r = run_bass_kernel_spmd(nc, [arrays], core_ids=[0])
    return r.results[0]["out"].reshape(D, SEQ).T[None]
```

```python
import numpy as np

import concourse.bass as bass
from concourse import mybir

F32 = mybir.dt.float32
F32R = mybir.dt.float32r
I32 = mybir.dt.int32
ALU = mybir.AluOpType
ACT = mybir.ActivationFunctionType
AX = mybir.AxisListType

P = 128
SEQ = 512
D = 1024
DT = D // P
FF = 2816
FT = FF // P
HEADS = 8
QK_SCALE = float(1.0 / np.sqrt(192.0))
EPS = 1e-6
NEG = -3.0e38

GROUPS, GC, ST = 64, 16, 64
T = 8
STEPS = SEQ // T
GB = 8
BLOCKS = GROUPS // GB
M = T + 1

RING = 4
AHEAD = 3
FFN_PACKS = 3 * FT
HALF = FT // 2
FFN0A1 = 0
FFN0A2 = FFN0A1 + 3 * HALF
GLU = FFN0A2 + 3 * HALF
FFN0B = GLU + 2 * DT
KVD = FFN0B + FFN_PACKS
FFN1A = KVD + 3
DQ = FFN1A + FFN_PACKS
UKV = DQ + 2
UQ = UKV + 2
WO = UQ + 4
FFN1B = WO + DT
N_PACKS = FFN1B + FFN_PACKS
N_LOADS = N_PACKS + AHEAD

TILES = {FFN0A1: HALF, FFN0A2: HALF, FFN0B: FT, FFN1A: FT, FFN1B: FT}
F_BASE = {FFN0A1: 0, FFN0A2: HALF, FFN0B: FT, FFN1A: 2 * FT, FFN1B: 3 * FT}
X_BASE = {s: DT * i for i, s in enumerate((FFN0A1, FFN0A2, GLU, FFN0B, FFN1A, WO, FFN1B))}
H_BASE = {FFN0A1: 0, FFN0B: DT, KVD: 2 * DT, FFN1A: 3 * DT, DQ: 4 * DT, FFN1B: 5 * DT}
BLOCK_BASE = {FFN0A1: 0, FFN0A2: BLOCKS // 2}
N_IN0A, N_S5, N_IN0B, N_KV, N_LAT, N_DQ, N_CQ, N_IN1B, N_FINAL = range(9)
SUMS = {N_IN0A: 0, N_S5: 1, N_IN0B: 2, N_KV: 3, N_DQ: 4, N_IN1B: 5, N_FINAL: 6}

G_IN0A, G_S5, G_IN0B, G_KV, G_IN1A, G_DQ, G_IN1B, G_FIN = (8 * i for i in range(8))
C_LAT, C_QN, C_SGN, C_SGNR, C_INVF = 64, 65, 67, 68, 69
N_COLS = 70

O_B, O_COS, O_SIN, O_C, O_T = 0, 1024, 1536, 2048, 3072
OPS = 4096


def build(nc, xT, wstream, cols, consts, mask, pos, lam, bcd, dskip, out):
    ops_dram = nc.dram_tensor("s5_ops", [BLOCKS, P, OPS], F32, kind="Internal").ap()
    u_dram = nc.dram_tensor("s5_u", [D, T, STEPS], F32, kind="Internal").ap()
    y_dram = nc.dram_tensor("s5_y", [D, T, STEPS], F32, kind="Internal").ap()

    base = (nc.sbuf_base + 31) // 32 * 32

    def at(name, shape, dt, offset):
        return nc.alloc_sbuf_tensor_at(name, shape, dt, offset=base + offset)

    K = 1024
    o_x, o_h, o_g, o_w, o_raw, o_s = 0, 16 * K, 48 * K, 136 * K, 168 * K, 184 * K
    X = at("x_res", [P, DT, SEQ], F32, o_x)
    H = at("h_split", [P, DT, 2, SEQ], F32R, o_h)
    G = at("g_split", [P, FT, 2, SEQ], F32R, o_g)
    W = at("w_split", [P, RING, 2, 1024], F32R, o_w)
    RAW = at("w_raw", [P, RING, 1024], F32, o_raw)
    RSTD = at("rstd", [P, SEQ], F32, o_s)
    GT = at("gate", [P, SEQ], F32, o_s + 2 * K)
    UT = at("up", [P, SEQ], F32, o_s + 4 * K)
    ACC = at("sq_sum", [P, SEQ], F32, o_s + 6 * K)
    SQ = at("sq", [P, 2, SEQ], F32, o_s + 8 * K)
    CN = at("c_kv", [P, SEQ], F32, o_s + 12 * K)
    KR = at("k_rope", [P, SEQ], F32, o_s + 14 * K)
    COS = at("rope_cos", [P, SEQ], F32, o_s + 16 * K)
    SIN = at("rope_sin", [P, SEQ], F32, o_s + 18 * K)
    o_c = o_s + 20 * K
    COLS = at("cols", [P, N_COLS], F32, o_c)
    ONES = at("ones", [P, P], F32, o_c + 288)
    EYE = at("eye", [P, P], F32, o_c + 800)
    MASK = at("mask_rows", [1, P + 64], F32, o_c + 1312)
    STAT = at("attn_stat", [P, 32], F32, o_c + 2080)
    R8 = at("r8", [P, GROUPS], F32, o_c + 2208)
    assert base + o_c + 2208 + 4 * GROUPS <= nc.sbuf_top

    t_at = [o_g + HALF * 4 * K]

    def tmp(name, shape, dt=F32):
        t = at(name, shape, dt, t_at[0])
        t_at[0] += (int(np.prod(shape[1:])) * 4 + 31) // 32 * 32
        assert t_at[0] <= o_w
        return t

    LAM = tmp("lam", [P, 3, GROUPS])
    PW = tmp("lam_pow", [P, 2, M, GROUPS])
    PWS = tmp("lam_pow_signed", [P, 2, M, GROUPS])
    PA = tmp("u64_pow", [P, 2, 8, GROUPS])
    PB = tmp("u8_pow", [P, 2, 8, GROUPS])
    EC = tmp("e_coef", [P, 2, GROUPS])
    BC = tmp("bc_in", [P, 4, GB * GC])
    CP = tmp("c_pow", [P, GB, M, GC])
    BP = tmp("b_pow", [P, GB, T, GC])
    OUTB = tmp("ops_out", [P, 2048])
    DS = tmp("d_skip", [GC, GROUPS])
    DI = tmp("d_eye", [GC, GB, GC])
    TM = tmp("s5_tmp", [P, GB * M * GC])
    KT = at("k_window", [GC, GB, 15, GC], F32, o_s + 6 * K)
    WB = at("b_bar", [P, GB * GC], F32, o_s + 14 * K)
    XB = at("b_bar_swapped", [P, GB * GC], F32, o_s + 14 * K + 512)
    S6 = at("s5_small", [P, 24, GROUPS], F32, o_g + HALF * 4 * K - 24 * GROUPS * 4)
    POS = at("pos", [P, SEQ], I32, o_s + 14 * K)

    HN = at("h_norm", [P, DT, T, STEPS], F32, o_h)
    UY = at("u_and_y", [P, GROUPS, STEPS], F32, o_h + 16 * K)
    N_SLOTS = 5
    SLOT = at("op_slots", [P, N_SLOTS, OPS], F32, o_g)
    o_5 = o_g + N_SLOTS * OPS * 4
    XS = at("state", [P, 2, GB, STEPS + 1], F32, o_5)
    ZS = at("state_turned", [P, SEQ], F32, o_5 + 2 * 2080)
    JP = at("swap_halves", [P, P], F32, o_5 + 2 * 2080 + 2 * K)
    YT = at("y_tokens", [P, DT, SEQ], F32, o_h)

    KN = at("k_nope", [P, HEADS, SEQ], F32, o_g)
    VV = at("v", [P, 4, HEADS * P], F32, o_g + 16 * K)
    QN = at("q_nope", [P, HEADS, SEQ], F32, o_g + 32 * K)
    QR = at("q_rope", [P, 4, SEQ], F32, o_g + 48 * K)
    PT = at("probs_t", [P, 2, 4, SEQ], F32, o_g + 56 * K)
    PR = at("probs", [P, 2, 4, SEQ], F32, o_g + 72 * K)
    CS = at("c_kv_split", [P, 2, SEQ], F32R, o_g + 72 * K)
    CQS = at("c_q_split", [P, 2, 2, SEQ], F32R, o_g + 80 * K)


    R2 = at("rstd_latent", [P, SEQ], F32, o_g + (FT - 1) * 4 * K)

    BK = [nc.alloc_psum_tensor(f"bank{i}", [P, SEQ], F32) for i in range(8)]

    def sem(name):
        return nc.alloc_semaphore(name)

    s_raw = [sem(f"pack_loaded{i}") for i in range(RING)]
    s_const, s_xin = sem("const_loaded"), sem("x_loaded")
    s_bc, s_cpst, s_pos = sem("bc_loaded"), sem("c_op_stored"), sem("positions_loaded")
    s_opdma, s_jp = sem("ops_stored"), sem("swap_loaded")
    s_slot = [sem(f"slot_loaded{i}") for i in range(N_SLOTS)]
    s_ust = [sem(f"u_stored{i}") for i in range(2)]
    s_uld = [sem(f"u_loaded{i}") for i in range(2)]
    s_yst = [sem(f"y_stored{i}") for i in range(2)]
    s_yld = [sem(f"y_loaded{i}") for i in range(2)]
    s_out = sem("out_stored")
    s_hi, s_lo, s_used = sem("pack_hi"), sem("pack_lo"), sem("pack_used")
    s_h_hi, s_h_lo = sem("h_hi"), sem("h_lo")
    s_sq, s_sum, s_ssq = sem("sq_ready"), sem("sq_added"), sem("sum_of_squares")
    s_rcp, s_rstd = sem("rms_reciprocal"), sem("rstd_ready")
    s_read, s_silu, s_prod = sem("gate_up_read"), sem("silu_done"), sem("gated")
    s_g_hi, s_g_lo = sem("g_hi"), sem("g_lo")
    s_acc, s_x = sem("x_acc"), sem("x_updated")
    s_sig, s_glu = sem("glu_sigmoid"), sem("glu_gated")
    s_ch = sem("dve_step")
    s_expo, s_args, s_trig = sem("step_exponentials"), sem("angles_reduced"), sem("sin_cos")
    s_cp = sem("c_and_b_steps")
    s_phase, s_window, s_eb = sem("phase_steps"), sem("taps_in_window"), sem("e_times_b")
    s_small, s_tables, s_bbar = sem("coefficients_ready"), sem("power_tables_ready"), sem("b_bar_ready")
    s_ang, s_rope, s_pch = sem("rope_angles_reduced"), sem("rope_tables_ready"), sem("pool_step")
    s_made, s_turned, s_taps, s_btc = sem("powers_made"), sem("ops_turned"), sem("taps_ready"), sem("b_op_copied")
    s_hn, s_s, s_sc, s_js, s_z, s_jz, s_xs, s_yp, s_y = (sem(n) for n in (
        "h_norm_ready", "step_input", "step_input_copied", "swapped_input", "z_ready", "swapped_z",
        "state_ready", "y_psum", "y_ready"))
    s_zero = sem("state_zeroed")
    s_y_hi, s_y_lo = sem("y_hi"), sem("y_lo")
    s_cn, s_cnsq = sem("latent_scaled"), sem("latent_squared")
    s_mm, s_ev_a, s_ev_v = sem("mid_product"), sem("mid_read_act"), sem("mid_read_dve")
    s_qr = sem("q_turned")
    s_cs_hi, s_cs_lo, s_cq_hi, s_cq_lo, s_cqsq, s_cqsum = (sem(n) for n in (
        "latent_hi", "latent_lo", "cq_hi", "cq_lo", "cq_squared", "cq_squares_added"))
    s_scores, s_max, s_exp, s_p, s_tp, s_pt, s_o, s_o_hi, s_o_lo = (sem(n) for n in (
        "scores", "neg_max", "exp_done", "probs_ready", "probs_turned", "probs_t_copied",
        "o_ready", "o_hi", "o_lo"))

    FFNS = [FFN0A1, FFN0A2, FFN0B, FFN1A, FFN1B]
    BASE = {FFN0A1: 0, FFN0A2: 4, FFN0B: 4, FFN1A: 4, FFN1B: 0}
    OPS_STORES = 1 + T

    def in_packs(stage):
        return 2 * TILES[stage]

    def block_groups(k):
        return slice(k * GB, (k + 1) * GB) if isinstance(k, int) else bass.ds(k * GB, GB)

    def col(c):
        return COLS[:, c:c + 1] if isinstance(c, int) else COLS[:, bass.ds(c, 1)]

    def out_bank(stage, d):
        last = d ^ 2 if TILES[stage] % 2 and d >= 4 else d
        return BK[(BASE[stage] + 4 + last) % 8]

    def gt_part(f, part):
        if isinstance(f, int):
            return G[:, f, part, :]
        return G[:, bass.ds(f, 1), part, :].rearrange("p a n -> p (a n)")

    def in_banks(base, f):
        return BK[base + 2 * (f % 2)], BK[base + 2 * (f % 2) + 1]

    def wait_acc(eng, stage, d):
        if d < DT - 1:
            eng.wait_ge(s_acc, (DT - 1) * FFNS.index(stage) + d + 1)
        else:
            eng.wait_ge(s_used, stage + 3 * TILES[stage])

    MQ, MSTAT, MK, MCQ, MV, MN, MR, MID = 0, 2, 3, 11, 12, 20, 28, 36
    ENDS = {MQ: DQ + 1, MQ + 1: DQ + 2, MK + 7: UKV + 1, MV + 7: UKV + 2, MN + 3: UQ + 1, MN + 7: UQ + 2,
            MR + 6: UQ + 3, MR + 7: UQ + 4}
    INNER = [m for m in range(MID) if m not in ENDS and m not in (MSTAT, MCQ)]

    def signal(ins, m):
        ins.then_inc(s_used if m in ENDS else s_mm, 1)

    def wait_product(eng, m):
        if m in ENDS:
            eng.wait_ge(s_used, ENDS[m])
        else:
            eng.wait_ge(s_mm, INNER.index(m) + 1)

    def wait_read(eng, m):
        if m < MSTAT:
            eng.wait_ge(s_cq_lo, m + 1)
            eng.wait_ge(s_cqsq, m + 1)
        elif MK <= m < MCQ:
            eng.wait_ge(s_ev_a, m - MK + 1)
        else:
            eng.wait_ge(s_ev_v, [MSTAT, *range(MCQ, MID)].index(m) + 1)

    CONSTS = 6

    def cmul(tt, link, dr, di, ar, ai, br, bi, t1, t2):
        tt(t1, ai, bi, ALU.mult)
        tt(t2, ar, bi, ALU.mult)
        tt(dr, ar, br, ALU.mult)
        link(tt(di, ai, br, ALU.mult))
        tt(dr, dr, t1, ALU.subtract)
        link(tt(di, di, t2, ALU.add))

    def powers(tt, link, tab, top, t1, t2):
        m = 1
        while m < top:
            q = min(m, top - m)
            bc = [tab[:, ri, m:m + 1, :].broadcast_to([P, q, GROUPS]) for ri in range(2)]
            v1, v2 = (t[:, 0:q * GROUPS].rearrange("p (q g) -> p q g", q=q) for t in (t1, t2))
            cmul(tt, link, tab[:, 0, m + 1:m + 1 + q, :], tab[:, 1, m + 1:m + 1 + q, :],
                 tab[:, 0, 1:1 + q, :], tab[:, 1, 1:1 + q, :], bc[0], bc[1], v1, v2)
            m += q

    def reduced(ts, tt, link, ang, n, to_cos):
        link(ts(n, ang, float(1 / (2 * np.pi)), 12582912.0, ALU.mult, ALU.add))
        link(ts(n, n, -12582912.0, None, ALU.add))
        c1 = 6.28125
        c2 = float(np.float32(np.round((2 * np.pi - c1) * 2**21) / 2**21))
        for c in (c1, c2, float(np.float32(2 * np.pi - c1 - c2))):
            link(ts(to_cos, n, -c, None, ALU.mult))
            link(tt(ang, ang, to_cos, ALU.add))
        link(ts(ang, ang, 3.1415925, -3.1415925, ALU.min, ALU.max))
        link(ts(to_cos, ang, 0.0, -2.0, ALU.max, ALU.mult))
        link(tt(to_cos, to_cos, ang, ALU.add))
        return ts(to_cos, to_cos, float(np.pi / 2), None, ALU.add)

    with nc.Block() as block:

        @block.sync
        def _(sp):
            for k in range(DT):
                sp.dma_start(X[:, k, :], xT[k]).then_inc(s_xin, 16)
            for n in range(RING):
                sp.dma_start(RAW[:, n, :], wstream[n]).then_inc(s_raw[n], 16)
            turns = N_LOADS // RING
            with sp.Fori(1, turns) as i:
                for r in range(RING):
                    sp.wait_ge(s_lo, i * RING + (r - RING + 1))
                    sp.dma_start(RAW[:, r, :], wstream[i * RING + r]).then_inc(s_raw[r], 16)
            for n in range(RING * turns, N_LOADS):
                sp.wait_ge(s_lo, n - RING + 1)
                sp.dma_start(RAW[:, n % RING, :], wstream[n]).then_inc(s_raw[n % RING], 16)
            for k in range(DT):
                sp.wait_ge(s_x, 7 * DT + k + 1)
                sp.dma_start(out[k], X[:, k, :]).then_inc(s_out, 16)
            sp.wait_ge(s_out, 16 * DT)

        @block.gpsimd
        def _(pool):
            chain = [0]

            def link(ins):
                chain[0] += 1
                ins.then_inc(s_pch, 1)
                pool.wait_ge(s_pch, chain[0])

            tt, ts = nc.gpsimd.tensor_tensor, nc.gpsimd.tensor_scalar

            def sum_squares(n):
                for k in range(1, DT):
                    pool.wait_ge(s_sq, SUMS[n] * DT + k + 1)
                    if SUMS[n] * (DT - 1) + k > 1:
                        pool.wait_ge(s_sum, SUMS[n] * (DT - 1) + k - 1)
                    nc.gpsimd.tensor_tensor(ACC[:], ACC[:], SQ[:, k % 2, :], ALU.add).then_inc(s_sum, 1)

            def make_powers(k):
                first = isinstance(k, int)

                def chan(ap):
                    return ap.rearrange("p (g c) -> p g c", g=GB)

                def power(tab, ri, n):
                    return (tab[:, ri, 0:n, block_groups(k)].rearrange("p m g -> p g m").unsqueeze(3)
                            .broadcast_to([P, GB, n, GC]))

                def spread(ap, n):
                    return chan(ap).unsqueeze(2).broadcast_to([P, GB, n, GC])

                tmc = TM[:].rearrange("p (g m c) -> p g m c", g=GB, m=M)
                tmb = TM[:, 0:GB * T * GC].rearrange("p (g m c) -> p g m c", g=GB, m=T)
                pool.dma_start(BC[:], bcd[k]).then_inc(s_bc, 16)
                pool.wait_ge(s_bc, k * 16 + 16)
                tt(tmc, spread(BC[:, 3, :], M), power(PWS, 1, M), ALU.mult)
                if not first:
                    pool.wait_ge(s_turned, k)
                    pool.wait_ge(s_cpst, k * 16)
                tt(CP[:], spread(BC[:, 2, :], M), power(PWS, 0, M), ALU.mult).then_inc(s_cp, 1)
                pool.wait_ge(s_cp, k * 3 + 1)
                tt(CP[:], CP[:], tmc, ALU.subtract).then_inc(s_cp, 1)
                pool.wait_ge(s_bbar, k + 1)
                pool.wait_ge(s_cp, k * 3 + 2)
                tt(BP[:], spread(WB[:], T), power(PW, 0, T), ALU.mult)
                tt(tmb, spread(XB[:], T), power(PW, 1, T), ALU.mult).then_inc(s_cp, 1)
                pool.wait_ge(s_cp, k * 3 + 3)
                tt(BP[:], BP[:], tmb, ALU.subtract).then_inc(s_made, 1)
                pool.wait_ge(s_made, k + 1)
                pool.dma_start(ops_dram[k][:, O_C:O_T].rearrange("p (g n) -> p g n", g=GB),
                               CP[:, :, 1:M, :].rearrange("p g m c -> p g (m c)")).then_inc(s_cpst, 16)

            for q, v in ((0, 1.0), (1, 0.0)):
                nc.gpsimd.memset(PW[:, q, 0, :], v)
            pool.wait_ge(s_expo, 3)
            pool.wait_ge(s_small, 1)
            tt(PW[:, 0, 1, :], S6[:, 7, :], S6[:, 5, :], ALU.mult)
            link(tt(PW[:, 1, 1, :], S6[:, 7, :], S6[:, 4, :], ALU.mult))
            powers(tt, link, PW, T, TM[:, 0:256], TM[:, 256:512])
            link(ts(PWS[:].rearrange("p a m g -> p (a m g)"), PW[:].rearrange("p a m g -> p (a m g)"),
                    col(C_SGN), None, ALU.mult))
            lr, li, nr, ni = LAM[:, 0, :], S6[:, 13, :], S6[:, 14, :], PW[:, 1, 1, :]
            link(ts(nr, PW[:, 0, 1, :], -1.0, None, ALU.add))
            tt(S6[:, 17, :], nr, lr, ALU.mult)
            tt(S6[:, 18, :], ni, li, ALU.mult)
            tt(S6[:, 19, :], ni, lr, ALU.mult)
            link(tt(S6[:, 20, :], nr, li, ALU.mult))
            tt(S6[:, 17, :], S6[:, 17, :], S6[:, 18, :], ALU.add)
            link(tt(S6[:, 19, :], S6[:, 19, :], S6[:, 20, :], ALU.subtract))
            tt(EC[:, 0, :], S6[:, 17, :], S6[:, 15, :], ALU.mult)
            tt(EC[:, 1, :], S6[:, 19, :], S6[:, 15, :], ALU.mult).then_inc(s_tables, 1)
            sum_squares(N_IN0A)
            make_powers(0)
            with pool.Fori(1, BLOCKS) as k:
                make_powers(k)

            pool.wait_ge(s_opdma, 16 * OPS_STORES * BLOCKS)
            pool.wait_ge(s_cpst, 16 * BLOCKS)
            pool.dma_start(POS[:], pos).then_inc(s_pos, 16)
            pool.dma_start(JP[:], consts[2]).then_inc(s_jp, 16)
            for k in (3, 4, 0, 1, 2):
                if k < 3:
                    pool.wait_ge(s_used, FFN0A2 + 2 * HALF + min(4 * k + 4, HALF))
                pool.dma_start(SLOT[:, k, :], ops_dram[k]).then_inc(s_slot[k], 16)
            sum_squares(N_S5)
            for half in range(2):
                pool.wait_ge(s_ust[half], 16 * DT // 2)
                g0 = half * GROUPS // 2
                for t in range(T):
                    r = T - 1 - t
                    pool.dma_start(UY[r * GC:(r + 1) * GC, g0:g0 + GROUPS // 2, :],
                                   u_dram[half * D // 2:(half + 1) * D // 2, t, :].rearrange("(g c) j -> c g j", c=GC)
                                   ).then_inc(s_uld[half], 16)
            for k in range(N_SLOTS, BLOCKS):
                pool.wait_ge(s_yp, k - N_SLOTS + 1)
                pool.dma_start(SLOT[:, k % N_SLOTS, :], ops_dram[k]).then_inc(s_slot[k % N_SLOTS], 16)
            for half in range(2):
                pool.wait_ge(s_y, BLOCKS // 2 * (half + 1))
                g0 = half * GROUPS // 2
                for t in range(T):
                    pool.dma_start(y_dram[half * D // 2:(half + 1) * D // 2, t, :].rearrange("(g c) j -> c g j", c=GC),
                                   UY[t * GC:(t + 1) * GC, g0:g0 + GROUPS // 2, :]).then_inc(s_yst[half], 16)
            for half in range(2):
                pool.wait_ge(s_yst[half], 16 * T)
                for k in range(half * DT // 2, (half + 1) * DT // 2):
                    pool.dma_start(YT[:, k, :], y_dram[k * P:(k + 1) * P].rearrange("p t j -> p (t j)")
                                   ).then_inc(s_yld[half], 16)
            sum_squares(N_IN0B)

            pool.wait_ge(s_pos, 16)
            link(nc.gpsimd.tensor_copy(SIN[:], POS[:]))
            link(ts(SIN[:], SIN[:], col(C_INVF), None, ALU.mult))
            reduced(ts, tt, link, SIN[:], CN[:], COS[:]).then_inc(s_ang, 1)
            pool.wait_ge(s_trig, 4)
            ts(SIN[:], SIN[:], col(C_SGNR), None, ALU.mult).then_inc(s_rope, 1)

            sum_squares(N_KV)
            sum_squares(N_DQ)
            pool.wait_ge(s_cqsq, 2)
            pool.wait_ge(s_ssq, N_DQ + 1)
            nc.gpsimd.tensor_tensor(ACC[:], SQ[:, 0, :], SQ[:, 1, :], ALU.add).then_inc(s_cqsum, 1)
            sum_squares(N_IN1B)
            sum_squares(N_FINAL)

        @block.scalar
        def _(act):
            def split(stage, j, i=None):
                c = stage + j + AHEAD
                r = c % RING
                turn = c // RING + 1
                if i is None:
                    act.wait_ge(s_raw[r], 16 * turn)
                    if c >= RING:
                        act.wait_ge(s_used, c - RING + 1)
                else:
                    act.wait_ge(s_raw[r], i * 16 + 16 * turn)
                    act.wait_ge(s_used, i * 4 + (c - RING + 1))
                nc.scalar.activation(W[:, r, 0, :], RAW[:, r, :], ACT.Copy).then_inc(s_hi, 1)

            def gate(stage, f):
                F = f + F_BASE[stage]
                act.wait_ge(s_read, F + 1)
                nc.scalar.activation(GT[:], GT[:], ACT.Silu).then_inc(s_silu, 1)
                act.wait_ge(s_prod, F + 1)
                nc.scalar.activation(gt_part(f, 0), GT[:], ACT.Copy).then_inc(s_g_hi, 1)

            def h_hi(k, gains, dst):
                nc.scalar.activation(dst[:, k, 0, :], X[:, k, :], ACT.Identity, scale=col(gains + k)).then_inc(s_h_hi, 1)

            def square(n, k):
                if k >= 3:
                    act.wait_ge(s_sum, SUMS[n] * (DT - 1) + k - 2)
                dst = ACC[:] if k == 0 else SQ[:, k % 2, :]
                nc.scalar.activation(dst, X[:, k, :], ACT.Square).then_inc(s_sq, 1)

            def root(n, dst=RSTD):
                act.wait_ge(s_rcp, n + 1)
                nc.scalar.activation(dst[:], dst[:], ACT.Sqrt).then_inc(s_rstd, 1)

            def copy_b_op(stage, k):
                act.wait_ge(s_turned, k + 1)
                if not (isinstance(k, int) and k == 0):
                    act.wait_ge(s_opdma, k * (16 * OPS_STORES))
                b = (BASE[stage] + 6) % 8
                for q in range(2):
                    ins = nc.scalar.activation(OUTB[:, O_B + 512 * q:O_B + 512 * (q + 1)], BK[b + q][:], ACT.Copy)
                ins.then_inc(s_btc, 1)

            def store_ops(k):
                act.wait_ge(s_taps, k + 1)
                act.wait_ge(s_btc, k + 1)
                dst = ops_dram[k]
                act.dma_start(dst[:, O_B:O_C], OUTB[:]).then_inc(s_opdma, 16)
                for s in range(T):
                    act.dma_start(dst[s * GC:(s + 1) * GC, O_T:OPS].rearrange("c (g n) -> c g n", g=GB),
                                  KT[:, :, s:s + T, :].rearrange("c g t d -> c g (t d)")).then_inc(s_opdma, 16)

            def ffn_in_turn(stage, i):
                for a in range(2):
                    split(stage, 4 + 2 * a, i)
                    gate(stage, i * 2 + (1 + a))
                    if a == 1 and stage in BLOCK_BASE:
                        copy_b_op(stage, i + BLOCK_BASE[stage])
                    split(stage, 4 + 2 * a + 1, i)
                if stage in BLOCK_BASE:
                    store_ops(i + BLOCK_BASE[stage])

            def ffn_in_loop(stage):
                n = TILES[stage]
                nc.scalar.preload_act_table(ACT.Silu)
                first = int(stage == FFN0A1)
                if first:
                    ffn_in_turn(stage, 0)
                with act.Fori(first, n // 2 - 1) as i:
                    ffn_in_turn(stage, i)
                if n % 2:
                    split(stage, 2 * n - 2)
                    gate(stage, n - 2)
                    split(stage, 2 * n - 1)

            def ffn_in(stage, n=None):
                split(stage, 0)
                split(stage, 1)
                split(stage, 2)
                if n is not None:
                    root(n)
                gate(stage, 0)
                split(stage, 3)
                ffn_in_loop(stage)

            def ffn_out(stage, between=None):
                n = TILES[stage]
                split(stage, 2 * n)
                gate(stage, n - 1)
                if between:
                    between()
                split(stage, 2 * n + 1)
                with act.Fori(0, (n - 2) // 4) as i:
                    for j in range(4):
                        split(stage, 2 * n + 2 + j, i)
                for j in range(2 + (n - 2) // 4 * 4, n):
                    split(stage, 2 * n + j)

            act.dma_start(LAM[:], lam).then_inc(s_const, 16)
            act.dma_start(COLS[:], cols).then_inc(s_const, 16)
            act.dma_start(ONES[:], consts[0]).then_inc(s_const, 16)
            act.dma_start(EYE[:], consts[1]).then_inc(s_const, 16)
            act.dma_start(MASK[:], mask).then_inc(s_const, 16)
            act.dma_start(DS[:], dskip).then_inc(s_const, 16)

            act.wait_ge(s_const, 16 * CONSTS)
            nc.scalar.activation(S6[:, 0, :], LAM[:, 2, :], ACT.Exp).then_inc(s_expo, 1)
            act.wait_ge(s_args, 1)
            nc.scalar.activation(S6[:, 7, :], S6[:, 6, :], ACT.Exp).then_inc(s_expo, 1)
            nc.scalar.activation(R8[:], S6[:, 6, :], ACT.Exp, scale=float(T)).then_inc(s_expo, 1)
            act.wait_ge(s_args, 2)
            nc.scalar.activation(S6[:, 4, :], S6[:, 1, :], ACT.Sin).then_inc(s_trig, 1)
            nc.scalar.activation(S6[:, 5, :], S6[:, 3, :], ACT.Sin).then_inc(s_trig, 1)

            act.wait_ge(s_xin, 16 * DT)
            for k in range(DT):
                h_hi(k, G_IN0A, H)
                if k < AHEAD:
                    split(FFN0A1, k - AHEAD)
            for k in range(DT):
                square(N_IN0A, k)

            ffn_in(FFN0A1, N_IN0A)
            ffn_out(FFN0A1)
            ffn_in(FFN0A2)
            ffn_out(FFN0A2)

            act.wait_ge(s_opdma, 16 * OPS_STORES * BLOCKS)
            for k in range(DT):
                act.wait_ge(s_x, X_BASE[FFN0A2] + k + 1)
                square(N_S5, k)
            root(N_S5)
            for k in range(DT):
                act.wait_ge(s_hn, k + 1)
                act.dma_start(u_dram[k * P:(k + 1) * P], HN[:, k]).then_inc(s_ust[k // (DT // 2)], 16)

            def copy_s(k):
                act.wait_ge(s_s, k + 1)
                if k >= 2:
                    act.wait_ge(s_z, k - 1)
                nc.scalar.activation(SQ[:, k % 2, :], BK[k % 2][:], ACT.Copy).then_inc(s_sc, 1)

            def gelu(k):
                act.wait_ge(s_yp, k + 1)
                nc.scalar.activation(UY[:, k * GB:(k + 1) * GB, :].rearrange("p g j -> p (g j)"), BK[4 + k % 2][:],
                                     ACT.Gelu_apprx_tanh).then_inc(s_y, 1)

            for k in range(BLOCKS):
                copy_s(k)
                if k >= 1:
                    gelu(k - 1)
            gelu(BLOCKS - 1)
            for k in range(DT):
                act.wait_ge(s_yld[k // (DT // 2)], 16 * DT // 2)
                nc.scalar.activation(G[:, k, 0, :], YT[:, k, :], ACT.Copy).then_inc(s_y_hi, 1)

            def glu(k):
                act.wait_ge(s_used, GLU + 2 * k + 2)
                if k >= 1:
                    act.wait_ge(s_x, X_BASE[GLU] + k)
                nc.scalar.activation(GT[:], in_banks(0, k)[1][:], ACT.Sigmoid).then_inc(s_sig, 1)
                if k >= 1:
                    h_hi(k - 1, G_IN0B, H)
                    square(N_IN0B, k - 1)

            split(GLU, 0)
            split(GLU, 1)
            for f in range(1, DT):
                split(GLU, 2 * f)
                glu(f - 1)
                split(GLU, 2 * f + 1)
            split(FFN0B, 0)
            glu(DT - 1)
            act.wait_ge(s_x, X_BASE[GLU] + DT)
            h_hi(DT - 1, G_IN0B, H)
            square(N_IN0B, DT - 1)
            split(FFN0B, 1)
            split(FFN0B, 2)
            root(N_IN0B)
            gate(FFN0B, 0)
            split(FFN0B, 3)
            ffn_in_loop(FFN0B)

            def rope_tables():
                act.wait_ge(s_ang, 1)
                nc.scalar.activation(SIN[:], SIN[:], ACT.Sin).then_inc(s_trig, 1)
                nc.scalar.activation(COS[:], COS[:], ACT.Sin).then_inc(s_trig, 1)

            ffn_out(FFN0B, rope_tables)

            for k in range(DT):
                act.wait_ge(s_x, X_BASE[FFN0B] + k + 1)
                h_hi(k, G_KV, G)
            for k in range(DT):
                h_hi(k, G_IN1A, H)
                square(N_KV, k)
            split(KVD, 0)
            split(KVD, 1)
            split(KVD, 2)
            split(FFN1A, 0)
            root(N_KV)
            act.wait_ge(s_cn, 1)
            nc.scalar.activation(SQ[:, 0, :], CN[:], ACT.Square).then_inc(s_cnsq, 1)
            split(FFN1A, 1)
            split(FFN1A, 2)
            gate(FFN1A, 0)
            split(FFN1A, 3)
            root(N_LAT, R2)
            ffn_in_loop(FFN1A)
            ffn_out(FFN1A)

            for k in range(DT):
                act.wait_ge(s_x, X_BASE[FFN1A] + k + 1)
                h_hi(k, G_DQ, H)
            act.wait_ge(s_cn, 2)
            nc.scalar.activation(CS[:, 0, :], CN[:], ACT.Copy).then_inc(s_cs_hi, 1)
            for k in range(DT):
                square(N_DQ, k)
            split(DQ, 0)
            split(DQ, 1)
            split(UKV, 0)
            for q in range(2):
                wait_product(act, MQ + q)
                nc.scalar.activation(CQS[:, q, 0, :], BK[q][:], ACT.Identity, scale=col(C_QN + q)).then_inc(s_cq_hi, 1)
            act.wait_ge(s_sum, (SUMS[N_DQ] + 1) * (DT - 1))
            for q in range(2):
                act.wait_ge(s_cq_lo, q + 1)
                nc.scalar.activation(SQ[:, q, :], BK[q][:], ACT.Square).then_inc(s_cqsq, 1)
            root(N_DQ)
            for h in range(HEADS):
                wait_product(act, MK + h)
                nc.scalar.activation(KN[:, h, :], BK[(MK + h) % 8][:], ACT.Copy).then_inc(s_ev_a, 1)
            split(UKV, 1)
            split(UQ, 0)
            root(N_CQ, UT)
            split(UQ, 1)
            split(UQ, 2)
            split(UQ, 3)

            def soft(h, t):
                i = 4 * h + t
                n = P * (t + 1)
                act.wait_ge(s_max, i + 1)
                if h >= 2:
                    act.wait_ge(s_tp, i - 7)
                nc.scalar.activation(PR[:, h % 2, t, 0:n], BK[t][:, 0:n], ACT.Exp, bias=STAT[:, 4 + t:5 + t],
                                     scale=QK_SCALE, accum_out=STAT[:, 8 + t:9 + t]).then_inc(s_exp, 1)

            def copy_pt(h, t):
                i = 4 * h + t
                act.wait_ge(s_tp, i + 1)
                if h >= 2:
                    act.wait_ge(s_o, h - 1)
                n = t + 1
                nc.scalar.activation(PT[:, h % 2, 0:n, t * P:(t + 1) * P],
                                     BK[4 + t % 2][:, 0:n * P].rearrange("p (a q) -> p a q", a=n),
                                     ACT.Copy).then_inc(s_pt, 1)

            def o_hi(h):
                act.wait_ge(s_o, h + 1)
                nc.scalar.activation(H[:, h, 0, :], BK[6 + h % 2][:], ACT.Copy).then_inc(s_o_hi, 1)

            for h in range(HEADS + 1):
                for t in range(4):
                    if h < HEADS:
                        soft(h, t)
                for t in range(4):
                    if h >= 1:
                        copy_pt(h - 1, t)
                if h >= 2:
                    o_hi(h - 2)
            o_hi(HEADS - 1)

            for d in range(DT):
                split(WO, d)
                if d >= 1:
                    act.wait_ge(s_x, X_BASE[WO] + d)
                    square(N_IN1B, d - 1)
            act.wait_ge(s_used, WO + DT)
            for k in range(DT):
                act.wait_ge(s_x, X_BASE[WO] + k + 1)
                h_hi(k, G_IN1B, H)
            square(N_IN1B, DT - 1)
            ffn_in(FFN1B, N_IN1B)
            ffn_out(FFN1B)

            for k in range(DT):
                act.wait_ge(s_x, X_BASE[FFN1B] + k + 1)
                square(N_FINAL, k)
            root(N_FINAL)

        @block.vector
        def _(dve):
            chain = [0]

            def link(ins):
                chain[0] += 1
                ins.then_inc(s_ch, 1)
                dve.wait_ge(s_ch, chain[0])

            tt, ts, stt = nc.vector.tensor_tensor, nc.vector.tensor_scalar, nc.vector.scalar_tensor_tensor

            def split(stage, j, i=None):
                c = stage + j + AHEAD
                r = c % RING
                dve.wait_ge(s_hi, c + 1 if i is None else i * 4 + (c + 1))
                tt(W[:, r, 1, :], RAW[:, r, :], W[:, r, 0, :].bitcast(F32), ALU.subtract).then_inc(s_lo, 1)

            def gated(stage, f, par, packs_done):
                F = f + F_BASE[stage]
                gb, ub = in_banks(BASE[stage], par)
                dve.wait_ge(s_used, packs_done)
                if not (isinstance(F, int) and F == 0):
                    dve.wait_ge(s_g_lo, F)
                tt(UT[:], ub[:], RSTD[:], ALU.mult)
                tt(GT[:], gb[:], RSTD[:], ALU.mult).then_inc(s_read, 1)
                dve.wait_ge(s_silu, F + 1)
                tt(GT[:], GT[:], UT[:], ALU.mult).then_inc(s_prod, 1)
                dve.wait_ge(s_g_hi, F + 1)
                tt(gt_part(f, 1), GT[:], gt_part(f, 0).bitcast(F32), ALU.subtract).then_inc(s_g_lo, 1)

            def h_lo(k, gains, dst, base):
                dve.wait_ge(s_h_hi, base + k + 1)
                stt(dst[:, k, 1, :], X[:, k, :], col(gains + k), dst[:, k, 0, :].bitcast(F32),
                    ALU.mult, ALU.subtract).then_inc(s_h_lo, 1)

            def mean_rcp(n, bank, width=D, dst=RSTD):
                dve.wait_ge(s_ssq, n + 1)
                link(ts(dst[:], bank[:], 1.0 / width, EPS, ALU.mult, ALU.add))
                nc.vector.reciprocal(dst[:], dst[:]).then_inc(s_rcp, 1)

            def block_tables(stage, k, F):
                if not (isinstance(k, int) and k == 0):
                    dve.wait_ge(s_opdma, k * (16 * OPS_STORES))
                dve.wait_ge(s_g_lo, F + 1)
                gs = block_groups(k)
                ar, ai = (PA[:, ri, :, gs].rearrange("p a g -> p g a").unsqueeze(3).broadcast_to([P, GB, 8, 8])
                          for ri in range(2))
                br, bi = (PB[:, ri, :, gs].rearrange("p b g -> p g b").unsqueeze(2).broadcast_to([P, GB, 8, 8])
                          for ri in range(2))
                ct, st, v1, v2 = (ap.rearrange("p (g a b) -> p g a b", g=GB, a=8) for ap in (
                    OUTB[:, O_COS:O_COS + 512], OUTB[:, O_SIN:O_SIN + 512], GT[:], UT[:]))
                tt(DI[:], DS[:, gs].unsqueeze(2).broadcast_to([GC, GB, GC]),
                   EYE[0:GC, 0:GC].unsqueeze(1).broadcast_to([GC, GB, GC]), ALU.mult)
                tt(v1, ai, bi, ALU.mult)
                tt(v2, ar, bi, ALU.mult)
                tt(ct, ar, br, ALU.mult)
                tt(st, ai, br, ALU.mult).then_inc(s_phase, 1)
                dve.wait_ge(s_phase, k * 2 + 1)
                tt(ct, ct, v1, ALU.subtract)
                tt(st, st, v2, ALU.add).then_inc(s_phase, 1)
                dve.wait_ge(s_phase, k * 2 + 2)

            def block_taps(stage, k):
                b = (BASE[stage] + 4) % 8
                dve.wait_ge(s_turned, k + 1)
                if isinstance(k, int):
                    nc.vector.memset(KT[:, :, 0:T - 1, :], 0.0)
                for q in range(2):
                    ins = nc.vector.tensor_copy(KT[:, 4 * q:4 * q + 4, T - 1:, :].rearrange("c g t d -> c g (t d)"),
                                                BK[b + q][0:GC, :].rearrange("c (g n) -> c g n", g=4))
                ins.then_inc(s_window, 1)
                dve.wait_ge(s_window, k + 1)
                tt(KT[:, :, T - 1, :], KT[:, :, T - 1, :], DI[:], ALU.add).then_inc(s_taps, 1)

            def block_b_bar(k, F):

                def chan(ap):
                    return ap.rearrange("p (g c) -> p g c", g=GB)

                wb, xb = chan(BC[:, 0, :]), chan(BC[:, 1, :])
                er, ei = (EC[:, ri, block_groups(k)].unsqueeze(2).broadcast_to([P, GB, GC]) for ri in range(2))
                a1, a2 = chan(GT[:, 0:GB * GC]), chan(GT[:, GB * GC:2 * GB * GC])
                dve.wait_ge(s_bc, k * 16 + 16)
                if isinstance(k, int) and k == 0:
                    dve.wait_ge(s_tables, 1)
                else:
                    dve.wait_ge(s_made, k)
                dve.wait_ge(s_g_lo, F + 1)
                tt(a1, xb, ei, ALU.mult)
                tt(a2, wb, ei, ALU.mult)
                tt(chan(WB[:]), wb, er, ALU.mult)
                tt(chan(XB[:]), xb, er, ALU.mult).then_inc(s_eb, 1)
                dve.wait_ge(s_eb, k + 1)
                tt(chan(WB[:]), chan(WB[:]), a1, ALU.subtract)
                tt(chan(XB[:]), chan(XB[:]), a2, ALU.add).then_inc(s_bbar, 1)
                dve.wait_ge(s_bbar, k + 1)

            def ffn_in_turn(stage, i, last=False):
                for a in range(2):
                    f = i * 2 + (1 + a)
                    split(stage, 4 + 2 * a, i)
                    gated(stage, f, (1 + a) % 2, i * 4 + (stage + 4 + 2 * a))
                    split(stage, 4 + 2 * a + 1, i)
                    if stage in BLOCK_BASE:
                        k = i + BLOCK_BASE[stage]
                        if a == 0:
                            block_tables(stage, k, f + F_BASE[stage])
                        else:
                            block_taps(stage, k)
                            if not last:
                                block_b_bar(k + 1, f + F_BASE[stage])

            def ffn_in_loop(stage):
                n = TILES[stage]
                first, last = int(stage == FFN0A1), int(stage == FFN0A2)
                if first:
                    ffn_in_turn(stage, 0)
                with dve.Fori(first, n // 2 - 1 - last) as i:
                    ffn_in_turn(stage, i)
                if last:
                    ffn_in_turn(stage, n // 2 - 2, True)
                if n % 2:
                    split(stage, 2 * n - 2)
                    gated(stage, n - 2, (n - 2) % 2, stage + 2 * n - 2)
                    split(stage, 2 * n - 1)

            def ffn_in(stage, n=None):
                split(stage, 0)
                split(stage, 1)
                split(stage, 2)
                if n is not None:
                    mean_rcp(n, BK[(BASE[stage] + 4) % 8])
                    dve.wait_ge(s_rstd, n + 1)
                gated(stage, 0, 0, stage + 2)
                split(stage, 3)
                if stage == FFN0A1:
                    block_b_bar(0, 0)
                ffn_in_loop(stage)

            def ffn_out(stage):
                n = TILES[stage]
                split(stage, 2 * n)
                gated(stage, n - 1, (n - 1) % 2, stage + 2 * n)
                split(stage, 2 * n + 1)
                with dve.Fori(0, (n - 2) // 4) as i:
                    for j in range(4):
                        split(stage, 2 * n + 2 + j, i)
                for j in range(2 + (n - 2) // 4 * 4, n):
                    split(stage, 2 * n + j)

            def add_ffn(stage, d):
                wait_acc(dve, stage, d)
                stt(X[:, d, :], out_bank(stage, d)[:], 0.5, X[:, d, :], ALU.mult, ALU.add).then_inc(s_x, 1)

            dve.wait_ge(s_const, 16 * CONSTS)
            dve.wait_ge(s_expo, 1)
            link(tt(S6[:, 6, :], LAM[:, 0, :], S6[:, 0, :], ALU.mult))
            tt(S6[:, 1, :], LAM[:, 1, :], S6[:, 0, :], ALU.mult).then_inc(s_args, 1)
            dve.wait_ge(s_args, 1)
            reduced(ts, tt, link, S6[:, 1, :], S6[:, 8, :], S6[:, 3, :]).then_inc(s_args, 1)
            ts(S6[:, 13, :], LAM[:, 1, :], col(C_SGN), None, ALU.mult)
            tt(S6[:, 15, :], LAM[:, 0, :], LAM[:, 0, :], ALU.mult)
            link(tt(S6[:, 16, :], LAM[:, 1, :], LAM[:, 1, :], ALU.mult))
            link(tt(S6[:, 15, :], S6[:, 15, :], S6[:, 16, :], ALU.add))
            link(nc.vector.reciprocal(S6[:, 15, :], S6[:, 15, :]))
            dve.wait_ge(s_trig, 2)
            ts(S6[:, 4, :], S6[:, 4, :], col(C_SGN), None, ALU.mult).then_inc(s_small, 1)

            dve.wait_ge(s_xin, 16 * DT)
            for k in range(DT):
                h_lo(k, G_IN0A, H, H_BASE[FFN0A1])
                if k < AHEAD:
                    split(FFN0A1, k - AHEAD)

            for tab in (PA, PB):
                nc.vector.memset(tab[:, 0, 0, :], 1.0)
                nc.vector.memset(tab[:, 1, 0, :], 0.0)
            t1, t2 = GT[:, 0:256], GT[:, 256:512]

            def squared(dst, src):
                cmul(tt, link, dst[0], dst[1], src[0], src[1], src[0], src[1], t1[:, 0:GROUPS], t2[:, 0:GROUPS])

            dve.wait_ge(s_small, 1)
            u1, u2, u4 = (S6[:, 5, :], S6[:, 4, :]), (S6[:, 9, :], S6[:, 10, :]), (S6[:, 11, :], S6[:, 12, :])
            squared(u2, u1)
            squared(u4, u2)
            squared((PB[:, 0, 1, :], PB[:, 1, 1, :]), u4)
            powers(tt, link, PB, 7, t1, t2)
            squared((PA[:, 0, 1, :], PA[:, 1, 1, :]), (PB[:, 0, 4, :], PB[:, 1, 4, :]))
            powers(tt, link, PA, 7, t1, t2)

            ffn_in(FFN0A1, N_IN0A)
            ffn_out(FFN0A1)
            for d in range(DT):
                add_ffn(FFN0A1, d)
            ffn_in(FFN0A2)
            ffn_out(FFN0A2)

            for d in range(DT):
                add_ffn(FFN0A2, d)
            mean_rcp(N_S5, BK[4])
            dve.wait_ge(s_rstd, N_S5 + 1)
            for k in range(DT):
                stt(HN[:, k].rearrange("p t j -> p j t"), X[:, k, :].rearrange("p (j t) -> p j t", t=T),
                    col(G_S5 + k), RSTD[:].rearrange("p (j t) -> p j t", t=T), ALU.mult, ALU.mult).then_inc(s_hn, 1)
            nc.vector.memset(XS[:, :, :, 0:1], 0.0).then_inc(s_zero, 1)
            for k in range(BLOCKS):
                ops = SLOT[:, k % N_SLOTS]
                cosb, sinb = ops[:, O_COS:O_COS + 512], ops[:, O_SIN:O_SIN + 512]
                dve.wait_ge(s_sc, k + 1)
                if k >= 1:
                    dve.wait_ge(s_xs, k)
                tt(GT[:], SQ[:, k % 2, :], cosb, ALU.mult)
                dve.wait_ge(s_js, k + 1)
                link(tt(UT[:], BK[2 + k % 2][:], sinb, ALU.mult))
                link(tt(GT[:], GT[:], UT[:], ALU.add))
                for g in range(GB):
                    ins = nc.vector.tensor_tensor_scan(
                        ZS[:, g * STEPS:(g + 1) * STEPS], R8[:, k * GB + g:k * GB + g + 1].broadcast_to([P, STEPS]),
                        GT[:, g * STEPS:(g + 1) * STEPS], 0.0, ALU.mult, ALU.add)
                ins.then_inc(s_z, 1)
                dve.wait_ge(s_z, k + 1)
                tt(GT[:], ZS[:], cosb, ALU.mult)
                dve.wait_ge(s_jz, k + 1)
                link(tt(UT[:], BK[6 + k % 2][:], sinb, ALU.mult))
                if k >= 2:
                    dve.wait_ge(s_yp, k - 1)
                tt(XS[:, k % 2, :, 1:], GT[:].rearrange("p (g j) -> p g j", g=GB),
                   UT[:].rearrange("p (g j) -> p g j", g=GB), ALU.subtract).then_inc(s_xs, 1)
            for k in range(DT):
                dve.wait_ge(s_y_hi, k + 1)
                tt(G[:, k, 1, :], YT[:, k, :], G[:, k, 0, :].bitcast(F32), ALU.subtract).then_inc(s_y_lo, 1)

            def glu(k):
                dve.wait_ge(s_sig, k + 1)
                dve.wait_ge(s_x, X_BASE[GLU] + k)
                tt(UT[:], in_banks(0, k)[0][:], GT[:], ALU.mult).then_inc(s_glu, 1)
                dve.wait_ge(s_glu, k + 1)
                xk = X[:, k, :].rearrange("p (j t) -> p t j", t=T)
                tt(xk, xk, UT[:].rearrange("p (t j) -> p t j", t=T), ALU.add).then_inc(s_x, 1)
                if k >= 1:
                    h_lo(k - 1, G_IN0B, H, H_BASE[FFN0B])

            split(GLU, 0)
            split(GLU, 1)
            for f in range(1, DT):
                split(GLU, 2 * f)
                glu(f - 1)
                split(GLU, 2 * f + 1)
            split(FFN0B, 0)
            glu(DT - 1)
            h_lo(DT - 1, G_IN0B, H, H_BASE[FFN0B])
            split(FFN0B, 1)
            split(FFN0B, 2)
            mean_rcp(N_IN0B, BK[0])
            dve.wait_ge(s_rstd, N_IN0B + 1)
            gated(FFN0B, 0, 0, FFN0B + 2)
            split(FFN0B, 3)
            ffn_in_loop(FFN0B)
            ffn_out(FFN0B)

            for d in range(DT):
                add_ffn(FFN0B, d)
                if d >= 1:
                    h_lo(d - 1, G_KV, G, H_BASE[KVD])
            h_lo(DT - 1, G_KV, G, H_BASE[KVD])
            for k in range(DT):
                h_lo(k, G_IN1A, H, H_BASE[FFN1A])
            split(KVD, 0)
            split(KVD, 1)
            split(KVD, 2)
            split(FFN1A, 0)
            mean_rcp(N_KV, BK[3])
            dve.wait_ge(s_rstd, N_KV + 1)
            dve.wait_ge(s_rope, 1)
            tt(KR[:], BK[1][:], RSTD[:], ALU.mult)
            tt(UT[:], BK[2][:], RSTD[:], ALU.mult)
            tt(CN[:], BK[0][:], RSTD[:], ALU.mult).then_inc(s_cn, 1)
            dve.wait_ge(s_cn, 1)
            tt(KR[:], KR[:], COS[:], ALU.mult)
            link(tt(UT[:], UT[:], SIN[:], ALU.mult))
            link(tt(KR[:], KR[:], UT[:], ALU.add))
            split(FFN1A, 1)
            split(FFN1A, 2)
            gated(FFN1A, 0, 0, FFN1A + 2)
            split(FFN1A, 3)
            mean_rcp(N_LAT, BK[3], P, R2)
            dve.wait_ge(s_rstd, N_LAT + 1)
            stt(CN[:], CN[:], col(C_LAT), R2[:], ALU.mult, ALU.mult).then_inc(s_cn, 1)
            ffn_in_loop(FFN1A)
            ffn_out(FFN1A)

            for d in range(DT):
                add_ffn(FFN1A, d)
                if d >= 1:
                    h_lo(d - 1, G_DQ, H, H_BASE[DQ])
            h_lo(DT - 1, G_DQ, H, H_BASE[DQ])
            dve.wait_ge(s_cs_hi, 1)
            tt(CS[:, 1, :], CN[:], CS[:, 0, :].bitcast(F32), ALU.subtract).then_inc(s_cs_lo, 1)
            split(DQ, 0)
            split(DQ, 1)
            split(UKV, 0)
            for q in range(2):
                dve.wait_ge(s_cq_hi, q + 1)
                stt(CQS[:, q, 1, :], BK[q][:], col(C_QN + q), CQS[:, q, 0, :].bitcast(F32),
                    ALU.mult, ALU.subtract).then_inc(s_cq_lo, 1)
            dve.wait_ge(s_ssq, N_DQ + 1)
            ts(RSTD[:], BK[MSTAT % 8][:], 1.0 / D, EPS, ALU.mult, ALU.add).then_inc(s_ev_v, 1)
            dve.wait_ge(s_ev_v, 1)
            nc.vector.reciprocal(RSTD[:], RSTD[:]).then_inc(s_rcp, 1)
            dve.wait_ge(s_rstd, N_DQ + 1)
            dve.wait_ge(s_ssq, N_CQ + 1)
            ts(UT[:], BK[MCQ % 8][:], 1.0 / 256, None, ALU.mult).then_inc(s_ev_v, 1)
            dve.wait_ge(s_ev_v, 2)
            link(tt(UT[:], UT[:], RSTD[:], ALU.mult))
            link(tt(UT[:], UT[:], RSTD[:], ALU.mult))
            link(ts(UT[:], UT[:], EPS, None, ALU.add))
            nc.vector.reciprocal(UT[:], UT[:]).then_inc(s_rcp, 1)
            for m in range(8):
                wait_product(dve, MV + m)
                nc.vector.tensor_copy(VV[:, m // 2, (m % 2) * 512:(m % 2 + 1) * 512], BK[(MV + m) % 8][:]).then_inc(s_ev_v, 1)
            split(UKV, 1)
            split(UQ, 0)
            dve.wait_ge(s_rstd, N_CQ + 1)
            link(tt(UT[:], UT[:], RSTD[:], ALU.mult))
            tt(COS[:], COS[:], UT[:], ALU.mult)
            tt(SIN[:], SIN[:], UT[:], ALU.mult)
            for h in range(HEADS):
                if h == 4:
                    split(UQ, 1)
                wait_product(dve, MN + h)
                tt(QN[:, h, :], BK[(MN + h) % 8][:], UT[:], ALU.mult).then_inc(s_ev_v, 1)
            split(UQ, 2)
            split(UQ, 3)
            for q in range(4):
                ea, eb = MR + 2 * q, MR + 2 * q + 1
                wait_product(dve, ea)
                tt(QR[:, q, :], BK[ea % 8][:], COS[:], ALU.mult).then_inc(s_ev_v, 1)
                wait_product(dve, eb)
                tt(GT[:], BK[eb % 8][:], SIN[:], ALU.mult).then_inc(s_ev_v, 1)
                wait_read(dve, eb)
                tt(QR[:, q, :], QR[:, q, :], GT[:], ALU.add).then_inc(s_qr, 1)
                dve.wait_ge(s_qr, q + 1)

            def top(h, t):
                i = 4 * h + t
                dve.wait_ge(s_scores, i + 1)
                link(nc.vector.reduce_max(STAT[:, t:t + 1], BK[t][:, 0:P * (t + 1)], AX.X))
                ts(STAT[:, 4 + t:5 + t], STAT[:, t:t + 1], -QK_SCALE, None, ALU.mult).then_inc(s_max, 1)

            def scale(h, t):
                i = 4 * h + t
                n = P * (t + 1)
                dve.wait_ge(s_exp, i + 1)
                link(nc.vector.reciprocal(STAT[:, 12 + t:13 + t], STAT[:, 8 + t:9 + t]))
                ts(PR[:, h % 2, t, 0:n], PR[:, h % 2, t, 0:n], STAT[:, 12 + t:13 + t], None, ALU.mult).then_inc(s_p, 1)
                dve.wait_ge(s_p, i + 1)

            def o_lo(h):
                dve.wait_ge(s_o_hi, h + 1)
                tt(H[:, h, 1, :], BK[6 + h % 2][:], H[:, h, 0, :].bitcast(F32), ALU.subtract).then_inc(s_o_lo, 1)

            for h in range(HEADS):
                for t in range(4):
                    top(h, t)
                    if t >= 1:
                        scale(h, t - 1)
                scale(h, 3)
                if h >= 2:
                    o_lo(h - 2)
            o_lo(HEADS - 2)
            o_lo(HEADS - 1)

            def add_wo(d):
                dve.wait_ge(s_used, WO + d + 1)
                tt(X[:, d, :], X[:, d, :], BK[d][:], ALU.add).then_inc(s_x, 1)

            for d in range(DT):
                split(WO, d)
                if d >= 1:
                    add_wo(d - 1)
            add_wo(DT - 1)
            for k in range(DT):
                h_lo(k, G_IN1B, H, H_BASE[FFN1B])
            ffn_in(FFN1B, N_IN1B)
            ffn_out(FFN1B)

            for d in range(DT):
                add_ffn(FFN1B, d)
            mean_rcp(N_FINAL, BK[4])
            dve.wait_ge(s_rstd, N_FINAL + 1)
            for k in range(DT):
                stt(X[:, k, :], X[:, k, :], col(G_FIN + k), RSTD[:], ALU.mult, ALU.mult).then_inc(s_x, 1)

        @block.tensor
        def _(pe):
            mm = nc.tensor.matmul

            def three(bank, hi, lo, x_hi, x_lo, start, cols=None):
                mm(bank, hi, x_hi, start=start, stop=True, skip_group_check=True)
                mm(bank, hi, x_lo, start=False, stop=True, skip_group_check=True)
                return mm(bank, lo, x_hi, start=False, stop=True, skip_group_check=True)

            def tile(c, k):
                r = c % RING
                return W[:, r, 0, k * P:(k + 1) * P], W[:, r, 1, k * P:(k + 1) * P]

            def pack(n):
                pe.wait_ge(s_lo, n + 1)

            def column(c, bank, src, wait=None):
                for k in range(DT):
                    if wait:
                        wait(k)
                    last = three(bank[:], *tile(c, k), src[:, k, 0, :], src[:, k, 1, :], k == 0)
                last.then_inc(s_used, 1)

            def stat(n, bank):
                pe.wait_ge(s_sum, (SUMS[n] + 1) * (DT - 1))
                mm(bank[:], ONES[:], ACC[:], start=True, stop=True).then_inc(s_ssq, 1)

            def first_pair(stage, base, src, wait):
                banks = in_banks(base, 0)
                for k in range(DT):
                    wait(k)
                    for q in range(2):
                        if k == 0:
                            pack(stage + q)
                        last = three(banks[q][:], *tile(stage + q, k), src[:, k, 0, :], src[:, k, 1, :], k == 0)
                        if k == DT - 1:
                            last.then_inc(s_used, 1)

            def in_tile(stage, f, par, base, src, i=None):
                for q in range(2):
                    c = stage + f * 2 + q
                    pack(c if i is None else i * 4 + c)
                    column(c, in_banks(base, par)[q], src)

            def turn_block(stage, k):
                b = (BASE[stage] + 4) % 8
                pe.wait_ge(s_made, k + 1)
                if isinstance(k, int):
                    pe.wait_ge(s_rcp, N_IN0A + 1)
                else:
                    pe.wait_ge(s_taps, k)
                    pe.wait_ge(s_btc, k)
                for g in range(GB):
                    mm(BK[b + g // 4][0:GC, (g % 4) * P:(g % 4 + 1) * P], BP[:, g, 0, :],
                       CP[:, g, 0:T, :].rearrange("p m c -> p (m c)"), start=(g % 4 == 0), stop=True,
                       skip_group_check=True)
                for g in range(GB):
                    last = nc.tensor.transpose(BK[b + 2 + g // 4][:, (g % 4) * P:(g % 4 + 1) * P],
                                               BP[:, g].rearrange("p m c -> p (m c)"), EYE[:])
                last.then_inc(s_turned, 1)

            def ffn_in_turn(stage, i, src):
                for a in range(2):
                    pe.wait_ge(s_read, i * 2 + (F_BASE[stage] + a + 1))
                    in_tile(stage, 2 + a, a, BASE[stage], src, i)
                    if a == 0 and stage in BLOCK_BASE:
                        turn_block(stage, i + BLOCK_BASE[stage])

            def ffn_in(stage, src, wait, between=None, after=None):
                base, n = BASE[stage], TILES[stage]
                first_pair(stage, base, src, wait)
                if between:
                    between()
                in_tile(stage, 1, 1, base, src)
                if after:
                    after()
                first = int(stage == FFN0A1)
                if first:
                    ffn_in_turn(stage, 0, src)
                with pe.Fori(first, n // 2 - 1) as i:
                    ffn_in_turn(stage, i, src)
                if n % 2:
                    pe.wait_ge(s_read, F_BASE[stage] + n - 2)
                    in_tile(stage, n - 1, (n - 1) % 2, base, src)

            def ffn_out(stage):
                F, n = F_BASE[stage], TILES[stage]

                def row(j, c, at, x_hi, x_lo, last_row=False):
                    pack(at)
                    for d in range(DT):
                        if j == 0 and d in (4, 6):
                            pe.wait_ge(s_read, F + n - 1 + (d == 6))
                        last = three(out_bank(stage, d)[:], *tile(c, d), x_hi, x_lo, j == 0)
                        if last_row and d < DT - 1:
                            last.then_inc(s_acc, 1)
                    last.then_inc(s_used, 1)

                if stage in BLOCK_BASE:
                    pe.wait_ge(s_taps, BLOCK_BASE[stage] + BLOCKS // 2)
                    pe.wait_ge(s_btc, BLOCK_BASE[stage] + BLOCKS // 2)
                for j in range(2):
                    pe.wait_ge(s_g_lo, F + j + 1)
                    row(j, stage + 2 * n + j, stage + 2 * n + j, G[:, j, 0, :], G[:, j, 1, :])
                pe.wait_ge(s_g_lo, F + n - 2)
                turns = (n - 5) // 4
                with pe.Fori(0, turns) as i:
                    for a in range(4):
                        c = stage + 2 * n + 2 + a
                        f = i * 4 + (2 + a)
                        row(2 + a, c, i * 4 + c, gt_part(f, 0), gt_part(f, 1))
                pe.wait_ge(s_g_lo, F + n)
                for j in range(2 + 4 * turns, n):
                    at = stage + 2 * n + j
                    row(j, at, at, G[:, j, 0, :], G[:, j, 1, :], j == n - 1)

            pe.wait_ge(s_const, 16 * CONSTS)
            ffn_in(FFN0A1, H, lambda k: pe.wait_ge(s_h_lo, H_BASE[FFN0A1] + k + 1), between=lambda: stat(N_IN0A, BK[4]))
            ffn_out(FFN0A1)

            def second_half(k):
                if k == 0:
                    pe.wait_ge(s_x, X_BASE[FFN0A1] + 2)

            ffn_in(FFN0A2, H, second_half, between=lambda: pe.wait_ge(s_x, X_BASE[FFN0A1] + DT))
            ffn_out(FFN0A2)

            pe.wait_ge(s_x, X_BASE[FFN0A2] + DT)
            stat(N_S5, BK[4])

            def group(ap, g, n=P):
                return ap[:, g * n:(g + 1) * n]

            def step_input(k):
                ops = SLOT[:, k % N_SLOTS]
                if k % 4 == 0:
                    pe.wait_ge(s_uld[k // 4], 16 * T)
                pe.wait_ge(s_slot[k % N_SLOTS], 16 * (k // N_SLOTS + 1))
                if k >= 2:
                    pe.wait_ge(s_sc, k - 1)
                for g in range(GB):
                    last = mm(group(BK[k % 2], g, STEPS), group(ops[:, O_B:O_B + 1024], g), UY[:, k * GB + g, :],
                              start=(g == 0), stop=True, skip_group_check=True)
                last.then_inc(s_s, 1)

            def block_out(k):
                ops = SLOT[:, k % N_SLOTS]
                pe.wait_ge(s_sc, k + 1)
                mm(BK[2 + k % 2][:], JP[:], SQ[:, k % 2, :], start=True, stop=True).then_inc(s_js, 1)
                if k >= 2:
                    pe.wait_ge(s_y, k - 1)
                for g in range(GB):
                    mm(group(BK[4 + k % 2], g, STEPS), group(ops[:, O_T:OPS], g), UY[:, k * GB + g, :],
                       start=(g == 0), stop=True, skip_group_check=True)
                pe.wait_ge(s_z, k + 1)
                mm(BK[6 + k % 2][:], JP[:], ZS[:], start=True, stop=True).then_inc(s_jz, 1)
                pe.wait_ge(s_xs, k + 1)
                for g in range(GB):
                    last = mm(group(BK[4 + k % 2], g, STEPS), group(ops[:, O_C:O_T], g), XS[:, k % 2, g, 0:STEPS],
                              start=False, stop=True, skip_group_check=True)
                last.then_inc(s_yp, 1)

            pe.wait_ge(s_jp, 16)
            pe.wait_ge(s_zero, 1)
            step_input(0)
            for k in range(BLOCKS):
                if k + 1 < BLOCKS:
                    step_input(k + 1)
                block_out(k)

            first_pair(GLU, 0, G, lambda k: pe.wait_ge(s_y_lo, k + 1))
            for f in range(1, DT):
                if f >= 2:
                    pe.wait_ge(s_glu, f - 1)
                in_tile(GLU, f, f % 2, 0, G)

            ffn_in(FFN0B, H, lambda k: pe.wait_ge(s_h_lo, H_BASE[FFN0B] + k + 1), between=lambda: stat(N_IN0B, BK[0]))
            ffn_out(FFN0B)
            for q in range(3):
                pack(KVD + q)
                column(KVD + q, BK[q], G,
                       (lambda k: (pe.wait_ge(s_h_lo, H_BASE[KVD] + k + 1), pe.wait_ge(s_x, X_BASE[FFN0B] + 1 + k))) if q == 0 else None)
            stat(N_KV, BK[3])

            def latent_stat():
                pe.wait_ge(s_cnsq, 1)
                pe.wait_ge(s_rcp, N_KV + 1)
                mm(BK[3][:], ONES[:], SQ[:, 0, :], start=True, stop=True).then_inc(s_ssq, 1)

            ffn_in(FFN1A, H, lambda k: pe.wait_ge(s_h_lo, H_BASE[FFN1A] + k + 1), after=latent_stat)
            ffn_out(FFN1A)

            def free(m):
                if m >= 8:
                    wait_read(pe, m - 8)
                return BK[m % 8]

            def product(m, c, tiles, src):
                b = free(m)
                for q, k in enumerate(tiles):
                    last = three(b[:], *tile(c, k), src[q][0], src[q][1], q == 0)
                signal(last, m)

            for q in range(2):
                pack(DQ + q)
                for k in range(DT):
                    if q == 0:
                        pe.wait_ge(s_h_lo, H_BASE[DQ] + k + 1)
                    last = three(BK[q][:], *tile(DQ + q, k), H[:, k, 0, :], H[:, k, 1, :], k == 0)
                signal(last, MQ + q)
            pe.wait_ge(s_sum, (SUMS[N_DQ] + 1) * (DT - 1))
            mm(BK[MSTAT][:], ONES[:], ACC[:], start=True, stop=True).then_inc(s_ssq, 1)
            pe.wait_ge(s_cs_lo, 1)
            pack(UKV)
            for h in range(HEADS):
                product(MK + h, UKV, [h], [(CS[:, 0, :], CS[:, 1, :])])
            pe.wait_ge(s_cqsum, 1)
            free(MCQ)
            mm(BK[MCQ % 8][:], ONES[:], ACC[:], start=True, stop=True).then_inc(s_ssq, 1)
            pack(UKV + 1)
            for m in range(8):
                t, half = m // 2, m % 2
                b = free(MV + m)
                r = (UKV + 1) % RING
                tok = slice(t * P, (t + 1) * P)
                w_hi, w_lo = (W[:, r, q, half * 512:(half + 1) * 512] for q in range(2))
                mm(b[:], CS[:, 0, tok], w_hi, start=True, stop=True, skip_group_check=True)
                mm(b[:], CS[:, 0, tok], w_lo, start=False, stop=True, skip_group_check=True)
                signal(mm(b[:], CS[:, 1, tok], w_hi, start=False, stop=True, skip_group_check=True), MV + m)
            pe.wait_ge(s_cq_lo, 2)
            cq = [(CQS[:, q, 0, :], CQS[:, q, 1, :]) for q in range(2)]
            for h in range(HEADS):
                if h % 4 == 0:
                    pack(UQ + h // 4)
                product(MN + h, UQ + h // 4, [2 * (h % 4), 2 * (h % 4) + 1], cq)
            pack(UQ + 3)
            for q in range(4):
                for side in range(2):
                    product(MR + 2 * q + side, UQ + 2 + side, [2 * q, 2 * q + 1], cq)

            wait_read(pe, MCQ - 1)
            wait_read(pe, MID - 1)
            pe.wait_ge(s_qr, 4)

            def scores(h, t):
                if h >= 1:
                    pe.wait_ge(s_exp, 4 * (h - 1) + t + 1)
                n = P * (t + 1)
                q0 = 64 * (h % 2)
                mm(BK[t][:, 0:n], QN[:, h, t * P:(t + 1) * P], KN[:, h, 0:n], start=True, stop=True, skip_group_check=True)
                mm(BK[t][:, 0:n], QR[q0:q0 + 64, h // 2, t * P:(t + 1) * P], KR[q0:q0 + 64, 0:n],
                   start=False, stop=True, skip_group_check=True)
                mm(BK[t][:, n - 64:n], MASK[0:1, 0:P], MASK[0:1, P:P + 64], start=False, stop=True,
                   skip_group_check=True).then_inc(s_scores, 1)

            def turn(h, t):
                i = 4 * h + t
                pe.wait_ge(s_p, i + 1)
                if i >= 2:
                    pe.wait_ge(s_pt, i - 1)
                for a in range(t + 1):
                    last = nc.tensor.transpose(BK[4 + t % 2][:, a * P:(a + 1) * P],
                                               PR[:, h % 2, t, a * P:(a + 1) * P], EYE[:])
                last.then_inc(s_tp, 1)

            def values(h):
                if h >= 2:
                    pe.wait_ge(s_o_lo, h - 1)
                pe.wait_ge(s_pt, 4 * h + 4)
                for a in range(4):
                    last = mm(BK[6 + h % 2][:, a * P:], VV[:, a, h * P:(h + 1) * P], PT[:, h % 2, a, a * P:],
                              start=(a == 0), stop=True, skip_group_check=True)
                last.then_inc(s_o, 1)

            for h in range(HEADS + 1):
                if h < HEADS:
                    for t in range(4):
                        scores(h, t)
                if h >= 1:
                    for t in range(4):
                        turn(h - 1, t)
                    values(h - 1)

            for d in range(DT):
                pack(WO + d)
                if d in (4, 6, 7):
                    pe.wait_ge(s_o_lo, HEADS)
                column(WO + d, BK[d], H, (lambda k: pe.wait_ge(s_o_lo, k + 1)) if d == 0 else None)

            ffn_in(FFN1B, H, lambda k: pe.wait_ge(s_h_lo, H_BASE[FFN1B] + k + 1), between=lambda: stat(N_IN1B, BK[4]))
            ffn_out(FFN1B)
            pe.wait_ge(s_x, X_BASE[FFN1B] + DT)
            stat(N_FINAL, BK[4])

    return nc


def column_packs(w):
    k, n = w.shape
    return w.reshape(k // P, P, n // P, P).transpose(2, 1, 0, 3).reshape(n // P, P, k)


def weight_stream(ffn_w_in, ffn_w_out, s5_w_glu, w_dkv, w_ukv, mla_w_dq, mla_w_uq, mla_w_o):
    s = np.zeros((N_LOADS, P, 1024), np.float32)

    def gated(at, w, f0, f1):
        packs = column_packs(w)
        up, n = len(packs) // 2, f1 - f0
        s[at:at + 2 * n:2], s[at + 1:at + 2 * n:2] = packs[f0:f1], packs[up + f0:up + f1]

    for at, layer, i, f0, f1 in ((FFN0A1, 0, 0, 0, HALF), (FFN0A2, 0, 0, HALF, FT), (FFN0B, 0, 1, 0, FT),
                                 (FFN1A, 1, 0, 0, FT), (FFN1B, 1, 1, 0, FT)):
        n = f1 - f0
        gated(at, ffn_w_in[layer, i], f0, f1)
        s[at + 2 * n:at + 3 * n] = ffn_w_out[layer, i].reshape(FT, P, D)[f0:f1]
    gated(GLU, s5_w_glu[0], 0, DT)
    s[KVD] = column_packs(w_dkv[:, :P])[0]
    r = w_dkv[:, P:]
    x = np.concatenate([r[:, 32:], r[:, :32]], 1)
    s[KVD + 1] = column_packs(np.concatenate([r, r], 1))[0]
    s[KVD + 2] = column_packs(np.concatenate([x, x], 1))[0]
    ukv = w_ukv.reshape(P, HEADS, 2, P)
    s[UKV], s[UKV + 1] = ukv[:, :, 0].reshape(P, 1024), ukv[:, :, 1].reshape(P, 1024)
    s[DQ:DQ + 2] = column_packs(mla_w_dq[0])
    uq = mla_w_uq[0].reshape(2, P, HEADS, 192)
    nope = uq[..., :P].transpose(1, 2, 0, 3).reshape(P, 2, 1024)
    s[UQ], s[UQ + 1] = nope[:, 0], nope[:, 1]
    rope = uq[..., P:]
    swap = np.concatenate([rope[..., 32:], rope[..., :32]], -1)
    for q, part in enumerate((rope, swap)):
        s[UQ + 2 + q] = part.reshape(2, P, 4, 2, 64).transpose(1, 2, 0, 3, 4).reshape(P, 1024)
    s[WO:WO + DT] = column_packs(mla_w_o[0])
    return s


def kernel(**inputs):
    import concourse.bacc as bacc
    from concourse.bass_utils import run_bass_kernel_spmd

    a = {k: np.asarray(v) for k, v in inputs.items()}
    f = np.float32

    def columns(v):
        return v.reshape(-1, P).T

    g = a["norm_gains"]
    half, quarter = np.repeat([1.0, -1.0], 64), np.tile(np.repeat([-1.0, 1.0], 32), 2)
    inv_freq = (1.0 / (10000.0 ** (np.arange(0, 64, 2) / 64)).astype(f)).astype(f)
    cols = np.concatenate([columns(v) for v in (
        g[0, 0], g[0, 1], g[0, 2], a["kv_in_norm"], g[1, 0], g[1, 1], g[1, 2], a["final_norm"],
        a["kv_latent_norm"], a["mla_q_norm"][0], half.astype(f), quarter.astype(f), np.tile(inv_freq, 4))], 1)
    eye = np.eye(P, dtype=f)
    consts = np.stack([np.ones((P, P), f), eye, np.roll(eye, 64, 0)])
    mask = np.concatenate([np.repeat([1.0, 0.0], 64), np.full(64, NEG)]).astype(f)[None]

    def states(v):
        return np.concatenate([v.T, v.T], 0)

    lam = np.stack([states(a["s5_lambda_re"][0]), states(a["s5_lambda_im"][0]),
                    np.broadcast_to(a["s5_log_step"][0], (P, GROUPS))], 1)
    b_re, b_im = (a[n][0].transpose(1, 0, 2) for n in ("s5_b_re", "s5_b_im"))
    c_re, c_im = (a[n][0].transpose(2, 0, 1) for n in ("s5_c_re", "s5_c_im"))
    bcd = np.stack([np.concatenate(v, 0) for v in ((b_re, b_im), (b_im, b_re), (c_re, c_im), (c_im, c_re))], 1)
    bcd = bcd.reshape(P, 4, BLOCKS, GB * GC).transpose(2, 0, 1, 3)
    arrays = {
        "xT": a["x"][0].T.reshape(DT, P, SEQ),
        "wstream": weight_stream(*(a[n] for n in ("ffn_w_in", "ffn_w_out", "s5_w_glu", "w_dkv", "w_ukv",
                                                  "mla_w_dq", "mla_w_uq", "mla_w_o"))),
        "cols": cols, "consts": consts, "mask": mask,
        "pos": np.broadcast_to(a["positions"], (P, SEQ)),
        "lam": lam, "bcd": bcd, "dskip": a["s5_d"][0].reshape(GROUPS, GC).T,
    }
    arrays = {k: np.ascontiguousarray(v) for k, v in arrays.items()}

    nc = bacc.Bacc("TRN2", target_bir_lowering=False, num_devices=1)
    aps = {k: nc.dram_tensor(k, v.shape, mybir.dt.from_np(v.dtype), kind="ExternalInput").ap()
           for k, v in arrays.items()}
    out = nc.dram_tensor("out", (DT, P, SEQ), F32, kind="ExternalOutput").ap()
    build(nc, out=out, **aps)
    r = run_bass_kernel_spmd(nc, [arrays], core_ids=[0])
    return r.results[0]["out"].reshape(D, SEQ).T[None]
```

```python
import numpy as np

import concourse.bass as bass
from concourse import mybir

F32 = mybir.dt.float32
F32R = mybir.dt.float32r
I32 = mybir.dt.int32
ALU = mybir.AluOpType
ACT = mybir.ActivationFunctionType
AX = mybir.AxisListType

P = 128
SEQ = 512
D = 1024
DT = D // P
FF = 2816
FT = FF // P
HEADS = 8
QK_SCALE = float(1.0 / np.sqrt(192.0))
EPS = 1e-6
NEG = -3.0e38

GROUPS, GC, ST = 64, 16, 64
T = 8
STEPS = SEQ // T
GB = 8
BLOCKS = GROUPS // GB
QUARTERS = 4
QG = GROUPS // QUARTERS
QD = D // QUARTERS
QK = DT // QUARTERS
M = T + 1

RING = 4
AHEAD = 3
FFN_PACKS = 3 * FT
HALF = FT // 2
FFN0A1 = 0
FFN0A2 = FFN0A1 + 3 * HALF
GLU = FFN0A2 + 3 * HALF
FFN0B = GLU + 2 * DT
KVD = FFN0B + FFN_PACKS
FFN1A = KVD + 3
DQ = FFN1A + FFN_PACKS
UKV = DQ + 2
UQ = UKV + 2
WO = UQ + 4
FFN1B = WO + DT
N_PACKS = FFN1B + FFN_PACKS
N_LOADS = N_PACKS + AHEAD

TILES = {FFN0A1: HALF, FFN0A2: HALF, FFN0B: FT, FFN1A: FT, FFN1B: FT}
F_BASE = {FFN0A1: 0, FFN0A2: HALF, FFN0B: FT, FFN1A: 2 * FT, FFN1B: 3 * FT}
X_BASE = {s: DT * i for i, s in enumerate((FFN0A1, FFN0A2, GLU, FFN0B, FFN1A, WO, FFN1B))}
H_BASE = {FFN0A1: 0, FFN0B: DT, KVD: 2 * DT, FFN1A: 3 * DT, DQ: 4 * DT, FFN1B: 5 * DT}
BLOCK_BASE = {FFN0A1: 0, FFN0A2: BLOCKS // 2}
BLOCK_TURN = {FFN0A1: 1, FFN0A2: 0}
N_IN0A, N_S5, N_IN0B, N_KV, N_LAT, N_DQ, N_CQ, N_IN1B, N_FINAL = range(9)
SUMS = {N_IN0A: 0, N_IN0B: 1, N_KV: 2, N_DQ: 3, N_IN1B: 4}
PE_SUMS = {N_S5: 0, N_FINAL: 1}
POOL_TILES = 3

G_IN0A, G_S5, G_IN0B, G_KV, G_IN1A, G_DQ, G_IN1B, G_FIN = (8 * i for i in range(8))
C_LAT, C_QN, C_SGN, C_SGNR, C_INVF = 64, 65, 67, 68, 69
N_COLS = 70

O_B, O_COS, O_SIN, O_C, O_T = 0, 1024, 1536, 2048, 3072
OPS = 4096


def build(nc, xT, wstream, cols, consts, mask, pos, lam, bcd, dskip, out):
    ops_dram = nc.dram_tensor("s5_ops", [BLOCKS, P, OPS], F32, kind="Internal").ap()
    u_dram = nc.dram_tensor("s5_u", [D, T, STEPS], F32, kind="Internal").ap()
    y_dram = nc.dram_tensor("s5_y", [D, T, STEPS], F32, kind="Internal").ap()

    base = (nc.sbuf_base + 31) // 32 * 32

    def at(name, shape, dt, offset):
        return nc.alloc_sbuf_tensor_at(name, shape, dt, offset=base + offset)

    K = 1024
    o_x, o_h, o_g, o_w, o_raw, o_s = 0, 16 * K, 48 * K, 136 * K, 168 * K, 184 * K
    X = at("x_res", [P, DT, SEQ], F32, o_x)
    H = at("h_split", [P, DT, 2, SEQ], F32R, o_h)
    G = at("g_split", [P, FT, 2, SEQ], F32R, o_g)
    W = at("w_split", [P, RING, 2, 1024], F32R, o_w)
    RAW = at("w_raw", [P, RING, 1024], F32, o_raw)
    RSTD = at("rstd", [P, SEQ], F32, o_s)
    GT = at("gate", [P, SEQ], F32, o_s + 2 * K)
    UT = at("up", [P, SEQ], F32, o_s + 4 * K)
    ACC = at("sq_sum", [P, SEQ], F32, o_s + 6 * K)
    SQ = at("sq", [P, 2, SEQ], F32, o_s + 8 * K)
    CN = at("c_kv", [P, SEQ], F32, o_s + 12 * K)
    KR = at("k_rope", [P, SEQ], F32, o_s + 14 * K)
    COS = at("rope_cos", [P, SEQ], F32, o_s + 16 * K)
    SIN = at("rope_sin", [P, SEQ], F32, o_s + 18 * K)
    o_c = o_s + 20 * K
    COLS = at("cols", [P, N_COLS], F32, o_c)
    ONES = at("ones", [P, P], F32, o_c + 288)
    EYE = at("eye", [P, P], F32, o_c + 800)
    MASK = at("mask_rows", [1, P + 64], F32, o_c + 1312)
    STAT = at("attn_stat", [P, 32], F32, o_c + 2080)
    R8 = at("r8", [P, GROUPS], F32, o_c + 2208)
    assert base + o_c + 2208 + 4 * GROUPS <= nc.sbuf_top

    t_at = [o_g + HALF * 4 * K]

    def tmp(name, shape, dt=F32):
        t = at(name, shape, dt, t_at[0])
        t_at[0] += (int(np.prod(shape[1:])) * 4 + 31) // 32 * 32
        assert t_at[0] <= o_w
        return t

    LAM = tmp("lam", [P, 3, GROUPS])
    PW = tmp("lam_pow", [P, 2, M, GROUPS])
    PWS = tmp("lam_pow_signed", [P, 2, M, GROUPS])
    PA = tmp("u64_pow", [P, 2, 8, GROUPS])
    PB = tmp("u8_pow", [P, 2, 8, GROUPS])
    EC = tmp("e_coef", [P, 2, GROUPS])
    BC = tmp("bc_in", [P, 4, GB * GC])
    CP = tmp("c_pow", [P, GB, M, GC])
    BP = tmp("b_pow", [P, GB, T, GC])
    OUTB = tmp("ops_out", [P, 2048])
    DS = tmp("d_skip", [GC, GROUPS])
    DI = tmp("d_eye", [GC, GB, GC])
    TM = tmp("s5_tmp", [P, GB * M * GC])
    KT = at("k_window", [GC, GB, 15, GC], F32, o_s + 6 * K)
    WB = at("b_bar", [P, GB * GC], F32, o_s + 14 * K)
    XB = at("b_bar_swapped", [P, GB * GC], F32, o_s + 14 * K + 512)
    S6 = at("s5_small", [P, 24, GROUPS], F32, o_g + HALF * 4 * K - 24 * GROUPS * 4)
    POS = at("pos", [P, SEQ], I32, o_s + 14 * K)

    HN = at("h_norm", [P, DT, T, STEPS], F32, o_h)
    UY = at("u_and_y", [P, GROUPS, STEPS], F32, o_h + 16 * K)
    N_SLOTS = 5
    SLOT = at("op_slots", [P, N_SLOTS, OPS], F32, o_g)
    o_5 = o_g + N_SLOTS * OPS * 4
    XS = at("state", [P, 2, GB, STEPS + 1], F32, o_5)
    ZS = [at("state_turned0", [P, SEQ], F32, o_5 + 2 * 2080), at("state_turned1", [P, SEQ], F32, o_s + 6 * K)]
    IC = [at(f"input_cos{i}", [P, SEQ], F32, o_s + o) for i, o in enumerate((2 * K, 16 * K))]
    ZC = [at(f"state_cos{i}", [P, SEQ], F32, o_s + o) for i, o in enumerate((12 * K, 18 * K))]
    JP = at("swap_halves", [P, P], F32, o_5 + 2 * 2080 + 2 * K)
    SQ8 = at("squares", [P, DT, SEQ], F32, o_h)
    YT = at("y_tokens", [P, DT, SEQ], F32, o_h)

    KN = at("k_nope", [P, HEADS, SEQ], F32, o_g)
    VV = at("v", [P, 4, HEADS * P], F32, o_g + 16 * K)
    QN = at("q_nope", [P, HEADS, SEQ], F32, o_g + 32 * K)
    QR = at("q_rope", [P, 4, SEQ], F32, o_g + 48 * K)
    PT = at("probs_t", [P, 2, 4, SEQ], F32, o_g + 56 * K)
    PR = at("probs", [P, 2, 4, SEQ], F32, o_g + 72 * K)
    CS = at("c_kv_split", [P, 2, SEQ], F32R, o_g + 72 * K)
    CQS = at("c_q_split", [P, 2, 2, SEQ], F32R, o_g + 80 * K)
    R2 = at("rstd_latent", [P, SEQ], F32, o_g + (FT - 1) * 4 * K)

    BK = [nc.alloc_psum_tensor(f"bank{i}", [P, SEQ], F32) for i in range(8)]

    def sem(name):
        return nc.alloc_semaphore(name)

    s_raw = [sem(f"pack_loaded{i}") for i in range(RING)]
    s_const, s_early = sem("const_loaded"), sem("lambda_and_columns_loaded")
    s_xin = [sem(f"x_loaded{i}") for i in range(DT)]
    s_bc, s_cpst, s_pos = sem("bc_loaded"), sem("c_op_stored"), sem("positions_loaded")
    s_opdma, s_jp = sem("ops_stored"), sem("swap_loaded")
    s_slot = [sem(f"slot_loaded{i}") for i in range(N_SLOTS)]
    s_again = [sem(f"slot_loaded_again{i}") for i in range(BLOCKS - N_SLOTS)]
    s_ust = [sem(f"u_stored{i}") for i in range(QUARTERS)]
    s_uld = [sem(f"u_loaded{i}") for i in range(QUARTERS)]
    s_yst = [sem(f"y_stored{i}") for i in range(QUARTERS)]
    s_yld = [sem(f"y_loaded{i}") for i in range(QUARTERS)]
    s_out = sem("out_stored")
    s_hi, s_lo, s_used = sem("pack_hi"), sem("pack_lo"), sem("pack_used")
    s_h_hi, s_h_lo = sem("h_hi"), sem("h_lo")
    s_sq, s_sum, s_ssq = sem("sq_ready"), sem("sq_added"), sem("sum_of_squares")
    s_rcp, s_rstd = sem("rms_reciprocal"), sem("rstd_ready")
    s_read, s_silu, s_prod = sem("gate_up_read"), sem("silu_done"), sem("gated")
    s_g_hi, s_g_lo = sem("g_hi"), sem("g_lo")
    s_acc, s_x = sem("x_acc"), sem("x_updated")
    s_sig, s_glu = sem("glu_sigmoid"), sem("glu_gated")
    s_ch = sem("dve_step")
    s_expo, s_args, s_trig = sem("step_exponentials"), sem("angles_reduced"), sem("sin_cos")
    s_cp = sem("c_and_b_steps")
    s_phase, s_window, s_eb = sem("phase_steps"), sem("taps_in_window"), sem("e_times_b")
    s_small, s_tables, s_bbar = sem("coefficients_ready"), sem("power_tables_ready"), sem("b_bar_ready")
    s_ang, s_rope, s_pch = sem("rope_angles_reduced"), sem("rope_tables_ready"), sem("pool_step")
    s_made, s_turned, s_taps, s_btc = sem("powers_made"), sem("ops_turned"), sem("taps_ready"), sem("b_op_copied")
    s_hn, s_s, s_sc, s_js, s_z, s_jz, s_xs, s_yp, s_y = (sem(n) for n in (
        "h_norm_ready", "step_input", "step_input_copied", "swapped_input", "z_ready", "swapped_z",
        "state_ready", "y_psum", "y_ready"))
    s_ic, s_zc = sem("input_cos_ready"), sem("state_cos_ready")
    s_warm = sem("zeros_for_warming_up")
    s_sq8, s_gained, s_fin_v, s_fin_p = (sem(n) for n in (
        "wide_squares_ready", "x_times_gain", "final_by_dve", "final_by_pool"))
    s_zero = sem("state_zeroed")
    s_y_hi, s_y_lo = sem("y_hi"), sem("y_lo")
    s_cn, s_cnsq = sem("latent_scaled"), sem("latent_squared")
    s_mm, s_ev_a, s_ev_v = sem("mid_product"), sem("mid_read_act"), sem("mid_read_dve")
    s_qr = sem("q_turned")
    s_cs_hi, s_cs_lo, s_cq_hi, s_cq_lo, s_cqsq, s_cqsum = (sem(n) for n in (
        "latent_hi", "latent_lo", "cq_hi", "cq_lo", "cq_squared", "cq_squares_added"))
    s_scores, s_max, s_exp, s_p, s_tp, s_pt, s_o, s_o_hi, s_o_lo = (sem(n) for n in (
        "scores", "neg_max", "exp_done", "probs_ready", "probs_turned", "probs_t_copied",
        "o_ready", "o_hi", "o_lo"))

    FFNS = [FFN0A1, FFN0A2, FFN0B, FFN1A, FFN1B]
    BASE = {FFN0A1: 0, FFN0A2: 4, FFN0B: 4, FFN1A: 4, FFN1B: 0}
    OPS_STORES = 1 + T

    def block_groups(k):
        return slice(k * GB, (k + 1) * GB) if isinstance(k, int) else bass.ds(k * GB, GB)

    def col(c):
        return COLS[:, c:c + 1] if isinstance(c, int) else COLS[:, bass.ds(c, 1)]

    def out_bank(stage, d):
        last = d ^ 2 if TILES[stage] % 2 and d >= 4 else d
        return BK[(BASE[stage] + 4 + last) % 8]

    def gt_part(f, part):
        if isinstance(f, int):
            return G[:, f, part, :]
        return G[:, bass.ds(f, 1), part, :].rearrange("p a n -> p (a n)")

    def in_banks(base, f):
        return BK[base + 2 * (f % 2)], BK[base + 2 * (f % 2) + 1]

    def wait_acc(eng, stage, d):
        if d < DT - 1:
            eng.wait_ge(s_acc, (DT - 1) * FFNS.index(stage) + d + 1)
        else:
            eng.wait_ge(s_used, stage + 3 * TILES[stage])

    MQ, MSTAT, MK, MCQ, MV, MN, MR, MID = 0, 2, 3, 11, 12, 20, 28, 36
    ENDS = {MQ: DQ + 1, MQ + 1: DQ + 2, MK + 7: UKV + 1, MV + 7: UKV + 2, MN + 3: UQ + 1, MN + 7: UQ + 2,
            MR + 6: UQ + 3, MR + 7: UQ + 4}
    INNER = [m for m in range(MID) if m not in ENDS and m not in (MSTAT, MCQ)]

    def signal(ins, m):
        ins.then_inc(s_used if m in ENDS else s_mm, 1)

    def wait_product(eng, m):
        if m in ENDS:
            eng.wait_ge(s_used, ENDS[m])
        else:
            eng.wait_ge(s_mm, INNER.index(m) + 1)

    def wait_read(eng, m):
        if m < MSTAT:
            eng.wait_ge(s_cq_lo, m + 1)
            eng.wait_ge(s_cqsq, m + 1)
        elif MK <= m < MCQ:
            eng.wait_ge(s_ev_a, m - MK + 1)
        else:
            eng.wait_ge(s_ev_v, [MSTAT, *range(MCQ, MID)].index(m) + 1)

    CONSTS = 4

    def in_turns(eng, stage, turn):
        end = TILES[stage] // 2 - 1
        if stage == FFN0A1:
            turn(stage, 0)
            turn(stage, 1, 0)
            with eng.Fori(2, end) as i:
                turn(stage, i, i + (-1))
        elif stage == FFN0A2:
            with eng.Fori(0, end - 1) as i:
                turn(stage, i, i + BLOCKS // 2)
            turn(stage, end - 1, BLOCKS - 1)
        else:
            with eng.Fori(0, end) as i:
                turn(stage, i)

    def cmul(tt, link, dr, di, ar, ai, br, bi, t1, t2):
        tt(t1, ai, bi, ALU.mult)
        tt(t2, ar, bi, ALU.mult)
        tt(dr, ar, br, ALU.mult)
        link(tt(di, ai, br, ALU.mult))
        tt(dr, dr, t1, ALU.subtract)
        link(tt(di, di, t2, ALU.add))

    def powers(tt, link, tab, top, t1, t2):
        m = 1
        while m < top:
            q = min(m, top - m)
            bc = [tab[:, ri, m:m + 1, :].broadcast_to([P, q, GROUPS]) for ri in range(2)]
            v1, v2 = (t[:, 0:q * GROUPS].rearrange("p (q g) -> p q g", q=q) for t in (t1, t2))
            cmul(tt, link, tab[:, 0, m + 1:m + 1 + q, :], tab[:, 1, m + 1:m + 1 + q, :],
                 tab[:, 0, 1:1 + q, :], tab[:, 1, 1:1 + q, :], bc[0], bc[1], v1, v2)
            m += q

    def reduced(ts, tt, link, ang, n, to_cos):
        link(ts(n, ang, float(1 / (2 * np.pi)), 12582912.0, ALU.mult, ALU.add))
        link(ts(n, n, -12582912.0, None, ALU.add))
        c1 = 6.28125
        c2 = float(np.float32(np.round((2 * np.pi - c1) * 2**21) / 2**21))
        for c in (c1, c2, float(np.float32(2 * np.pi - c1 - c2))):
            link(ts(to_cos, n, -c, None, ALU.mult))
            link(tt(ang, ang, to_cos, ALU.add))
        link(ts(ang, ang, 3.1415925, -3.1415925, ALU.min, ALU.max))
        link(ts(to_cos, ang, 0.0, -2.0, ALU.max, ALU.mult))
        link(tt(to_cos, to_cos, ang, ALU.add))
        return ts(to_cos, to_cos, float(np.pi / 2), None, ALU.add)

    with nc.Block() as block:

        @block.sync
        def _(sp):
            sp.dma_start(LAM[:], lam).then_inc(s_early, 16)
            sp.dma_start(COLS[:], cols).then_inc(s_early, 16)
            for k in range(DT):
                sp.dma_start(X[:, k, :], xT[k]).then_inc(s_xin[k], 16)
                if k < RING:
                    sp.dma_start(RAW[:, k, :], wstream[k]).then_inc(s_raw[k], 16)

            def store_ops(k):
                sp.wait_ge(s_taps, k + 1)
                sp.wait_ge(s_btc, k + 1)
                dst = ops_dram[k]
                sp.dma_start(dst[:, O_B:O_C], OUTB[:]).then_inc(s_opdma, 16)
                for s in range(T):
                    sp.dma_start(dst[s * GC:(s + 1) * GC, O_T:OPS].rearrange("c (g n) -> c g n", g=GB),
                                 KT[:, :, s:s + T, :].rearrange("c g t d -> c g (t d)")).then_inc(s_opdma, 16)

            def load_packs(first, end, after=None, block=None):
                with sp.Fori(first, end) as i:
                    for r in range(RING):
                        sp.wait_ge(s_lo, i * RING + (r - RING + 1))
                        sp.dma_start(RAW[:, r, :], wstream[i * RING + r]).then_inc(s_raw[r], 16)
                        if r == after:
                            store_ops(i + block)

            turns = N_LOADS // RING
            before = (GLU + AHEAD + RING - 1) // RING
            at = 1
            for stage, block in BLOCK_BASE.items():
                turn, slot = divmod(stage + 8 + 2 * AHEAD + 4 * BLOCK_TURN[stage], RING)
                load_packs(at, turn)
                at = turn + BLOCKS // 2
                load_packs(turn, at, slot, block - turn)
            load_packs(at, before)
            for q in range(QUARTERS):
                sp.wait_ge(s_ust[q], 16 * QK)
                for t in range(T):
                    r = T - 1 - t
                    sp.dma_start(UY[r * GC:(r + 1) * GC, q * QG:(q + 1) * QG, :],
                                 u_dram[q * QD:(q + 1) * QD, t, :].rearrange("(g c) j -> c g j", c=GC)
                                 ).then_inc(s_uld[q], 16)
            for k in range(N_SLOTS, BLOCKS):
                sp.wait_ge(s_yp, k - N_SLOTS + 1)
                sp.dma_start(SLOT[:, k % N_SLOTS, :], ops_dram[k]).then_inc(s_again[k - N_SLOTS], 16)
            for q in range(QUARTERS):
                sp.wait_ge(s_y, BLOCKS // QUARTERS * (q + 1))
                for t in range(T):
                    sp.dma_start(y_dram[q * QD:(q + 1) * QD, t, :].rearrange("(g c) j -> c g j", c=GC),
                                 UY[t * GC:(t + 1) * GC, q * QG:(q + 1) * QG, :]).then_inc(s_yst[q], 16)
                sp.wait_ge(s_yst[q], 16 * T)
                for k in range(q * QK, (q + 1) * QK):
                    sp.dma_start(YT[:, k, :], y_dram[k * P:(k + 1) * P].rearrange("p t j -> p (t j)")
                                 ).then_inc(s_yld[q], 16)
            load_packs(before, turns)
            for n in range(RING * turns, N_LOADS):
                sp.wait_ge(s_lo, n - RING + 1)
                sp.dma_start(RAW[:, n % RING, :], wstream[n]).then_inc(s_raw[n % RING], 16)
            tiles = [(k, s_fin_v, k + 1) for k in range(DT - POOL_TILES)]
            for q in range(POOL_TILES):
                tiles.insert(3 * q + 2, (DT - POOL_TILES + q, s_fin_p, q + 1))
            for k, done, count in tiles:
                sp.wait_ge(done, count)
                sp.dma_start(out[k], X[:, k, :]).then_inc(s_out, 16)
            sp.wait_ge(s_out, 16 * DT)

        @block.gpsimd
        def _(pool):
            chain = [0]

            def link(ins):
                chain[0] += 1
                ins.then_inc(s_pch, 1)
                pool.wait_ge(s_pch, chain[0])

            tt, ts = nc.gpsimd.tensor_tensor, nc.gpsimd.tensor_scalar

            def sum_squares(n):
                for k in range(1, DT):
                    pool.wait_ge(s_sq, SUMS[n] * DT + k + 1)
                    if SUMS[n] * (DT - 1) + k > 1:
                        pool.wait_ge(s_sum, SUMS[n] * (DT - 1) + k - 1)
                    nc.gpsimd.tensor_tensor(ACC[:], ACC[:], SQ[:, k % 2, :], ALU.add).then_inc(s_sum, 1)

            def make_powers(k):
                first = isinstance(k, int)

                def chan(ap):
                    return ap.rearrange("p (g c) -> p g c", g=GB)

                def power(tab, ri, n):
                    return (tab[:, ri, 0:n, block_groups(k)].rearrange("p m g -> p g m").unsqueeze(3)
                            .broadcast_to([P, GB, n, GC]))

                def spread(ap, n):
                    return chan(ap).unsqueeze(2).broadcast_to([P, GB, n, GC])

                tmc = TM[:].rearrange("p (g m c) -> p g m c", g=GB, m=M)
                tmb = TM[:, 0:GB * T * GC].rearrange("p (g m c) -> p g m c", g=GB, m=T)
                if not first:
                    pool.dma_start(BC[:], bcd[k]).then_inc(s_bc, 16)
                pool.wait_ge(s_bc, k * 16 + 16)
                tt(tmc, spread(BC[:, 3, :], M), power(PWS, 1, M), ALU.mult)
                if not first:
                    pool.wait_ge(s_turned, k)
                    pool.wait_ge(s_cpst, k * 16)
                tt(CP[:], spread(BC[:, 2, :], M), power(PWS, 0, M), ALU.mult).then_inc(s_cp, 1)
                pool.wait_ge(s_cp, k * 3 + 1)
                tt(CP[:], CP[:], tmc, ALU.subtract).then_inc(s_cp, 1)
                pool.wait_ge(s_bbar, k + 1)
                pool.wait_ge(s_cp, k * 3 + 2)
                tt(BP[:], spread(WB[:], T), power(PW, 0, T), ALU.mult)
                tt(tmb, spread(XB[:], T), power(PW, 1, T), ALU.mult).then_inc(s_cp, 1)
                pool.wait_ge(s_cp, k * 3 + 3)
                tt(BP[:], BP[:], tmb, ALU.subtract).then_inc(s_made, 1)
                pool.wait_ge(s_made, k + 1)
                pool.dma_start(ops_dram[k][:, O_C:O_T].rearrange("p (g n) -> p g n", g=GB),
                               CP[:, :, 1:M, :].rearrange("p g m c -> p g (m c)")).then_inc(s_cpst, 16)

            nc.gpsimd.memset(RSTD[:], 0.0).then_inc(s_warm, 1)
            pool.dma_start(ONES[:], consts[0]).then_inc(s_const, 16)
            pool.dma_start(EYE[:], consts[1]).then_inc(s_const, 16)
            pool.dma_start(MASK[:], mask).then_inc(s_const, 16)
            pool.dma_start(DS[:], dskip).then_inc(s_const, 16)
            pool.dma_start(BC[:], bcd[0]).then_inc(s_bc, 16)
            sum_squares(N_IN0A)

            for q, v in ((0, 1.0), (1, 0.0)):
                nc.gpsimd.memset(PW[:, q, 0, :], v)
            pool.wait_ge(s_small, 1)
            powers(tt, link, PW, T, TM[:, 0:256], TM[:, 256:512])
            link(tt(PWS[:].rearrange("p a m g -> p (a m g)"), PW[:].rearrange("p a m g -> p (a m g)"),
                    col(C_SGN).broadcast_to([P, 2 * M * GROUPS]), ALU.mult))
            make_powers(0)
            with pool.Fori(1, BLOCKS) as k:
                make_powers(k)

            pool.wait_ge(s_opdma, 16 * OPS_STORES * BLOCKS)
            pool.wait_ge(s_cpst, 16 * BLOCKS)
            pool.dma_start(JP[:], consts[2]).then_inc(s_jp, 16)
            for k in (3, 4, 0, 1, 2):
                if k < 3:
                    pool.wait_ge(s_used, FFN0A2 + 2 * HALF + min(4 * k + 4, HALF))
                pool.dma_start(SLOT[:, k, :], ops_dram[k]).then_inc(s_slot[k], 16)

            def cos(dst, src, k):
                cosb = SLOT[:, k % N_SLOTS, O_COS:O_COS + 512]
                return tt(dst[k % 2][:], src, cosb, ALU.mult)

            def input_cos(k):
                pool.wait_ge(s_sc, k + 1)
                if k >= 2:
                    pool.wait_ge(s_z, k - 1)
                cos(IC, SQ[:, k % 2, :], k).then_inc(s_ic, 1)

            input_cos(0)
            for k in range(BLOCKS):
                if k + 1 < BLOCKS:
                    input_cos(k + 1)
                pool.wait_ge(s_z, k + 1)
                if k >= 2:
                    pool.wait_ge(s_xs, k - 1)
                cos(ZC, ZS[k % 2][:], k).then_inc(s_zc, 1)
            pool.wait_ge(s_xs, BLOCKS)
            pool.dma_start(POS[:], pos).then_inc(s_pos, 16)
            sum_squares(N_IN0B)

            pool.wait_ge(s_pos, 16)
            link(nc.gpsimd.tensor_copy(SIN[:], POS[:]))
            link(ts(SIN[:], SIN[:], col(C_INVF), None, ALU.mult))
            reduced(ts, tt, link, SIN[:], CN[:], COS[:]).then_inc(s_ang, 1)
            pool.wait_ge(s_trig, 4)
            ts(SIN[:], SIN[:], col(C_SGNR), None, ALU.mult).then_inc(s_rope, 1)

            sum_squares(N_KV)
            sum_squares(N_DQ)
            pool.wait_ge(s_cqsq, 2)
            pool.wait_ge(s_ssq, N_DQ + 1)
            nc.gpsimd.tensor_tensor(ACC[:], SQ[:, 0, :], SQ[:, 1, :], ALU.add).then_inc(s_cqsum, 1)
            sum_squares(N_IN1B)
            pool.wait_ge(s_rstd, N_FINAL + 1)
            for k in range(DT - POOL_TILES, DT):
                pool.wait_ge(s_gained, k + 1)
                tt(X[:, k, :], X[:, k, :], RSTD[:], ALU.mult).then_inc(s_fin_p, 1)

        @block.scalar
        def _(act):
            def split(stage, j, i=None):
                c = stage + j + AHEAD
                r = c % RING
                turn = c // RING + 1
                if i is None:
                    act.wait_ge(s_raw[r], 16 * turn)
                    if c >= RING:
                        act.wait_ge(s_used, c - RING + 1)
                else:
                    act.wait_ge(s_raw[r], i * 16 + 16 * turn)
                    act.wait_ge(s_used, i * 4 + (c - RING + 1))
                nc.scalar.activation(W[:, r, 0, :], RAW[:, r, :], ACT.Copy).then_inc(s_hi, 1)

            def gate(stage, f):
                F = f + F_BASE[stage]
                act.wait_ge(s_read, F + 1)
                nc.scalar.activation(GT[:], GT[:], ACT.Silu).then_inc(s_silu, 1)
                act.wait_ge(s_prod, F + 1)
                nc.scalar.activation(gt_part(f, 0), GT[:], ACT.Copy).then_inc(s_g_hi, 1)

            def h_hi(k, gains, dst):
                nc.scalar.activation(dst[:, k, 0, :], X[:, k, :], ACT.Identity, scale=col(gains + k)).then_inc(s_h_hi, 1)

            def square(n, k):
                if k >= 3:
                    act.wait_ge(s_sum, SUMS[n] * (DT - 1) + k - 2)
                dst = ACC[:] if k == 0 else SQ[:, k % 2, :]
                nc.scalar.activation(dst, X[:, k, :], ACT.Square).then_inc(s_sq, 1)

            def wide_squares(n, stage):
                nc.scalar.preload_act_table(ACT.Sqrt)
                for k in range(DT):
                    act.wait_ge(s_x, X_BASE[stage] + k + 1)
                    nc.scalar.activation(SQ8[:, k, :], X[:, k, :], ACT.Square).then_inc(s_sq8, 1)

            def root(n, dst=RSTD):
                act.wait_ge(s_rcp, n + 1)
                nc.scalar.activation(dst[:], dst[:], ACT.Sqrt).then_inc(s_rstd, 1)

            def copy_b_op(stage, k):
                act.wait_ge(s_turned, k + 1)
                if not (isinstance(k, int) and k == 0):
                    act.wait_ge(s_opdma, k * (16 * OPS_STORES))
                b = (BASE[stage] + 6) % 8
                for q in range(2):
                    ins = nc.scalar.activation(OUTB[:, O_B + 512 * q:O_B + 512 * (q + 1)], BK[b + q][:], ACT.Copy)
                ins.then_inc(s_btc, 1)

            def ffn_in_turn(stage, i, k=None):
                for a in range(2):
                    split(stage, 4 + 2 * a, i)
                    gate(stage, i * 2 + (1 + a))
                    if a == 1 and k is not None:
                        copy_b_op(stage, k)
                    split(stage, 4 + 2 * a + 1, i)

            def ffn_in_loop(stage):
                n = TILES[stage]
                nc.scalar.preload_act_table(ACT.Silu)
                in_turns(act, stage, ffn_in_turn)
                if n % 2:
                    split(stage, 2 * n - 2)
                    gate(stage, n - 2)
                    split(stage, 2 * n - 1)
                if stage == FFN0A1:
                    copy_b_op(stage, BLOCKS // 2 - 1)

            def ffn_in(stage, n=None, done=0):
                for j in range(done, 3):
                    split(stage, j)
                if n is not None:
                    root(n)
                gate(stage, 0)
                split(stage, 3)
                ffn_in_loop(stage)

            def ffn_out(stage, between=None):
                n = TILES[stage]
                split(stage, 2 * n)
                gate(stage, n - 1)
                if between:
                    between()
                split(stage, 2 * n + 1)
                with act.Fori(0, (n - 2) // 4) as i:
                    for j in range(4):
                        split(stage, 2 * n + 2 + j, i)
                for j in range(2 + (n - 2) // 4 * 4, n):
                    split(stage, 2 * n + j)

            act.wait_ge(s_early, 16 * 2)
            nc.scalar.activation(S6[:, 0, :], LAM[:, 2, :], ACT.Exp).then_inc(s_expo, 1)

            for k in range(DT):
                act.wait_ge(s_xin[k], 16)
                h_hi(k, G_IN0A, H)
                square(N_IN0A, k)
                if k < AHEAD:
                    split(FFN0A1, k - AHEAD)
            split(FFN0A1, 0)

            act.wait_ge(s_args, 1)
            nc.scalar.activation(S6[:, 7, :], S6[:, 6, :], ACT.Exp).then_inc(s_expo, 1)
            nc.scalar.activation(R8[:], S6[:, 6, :], ACT.Exp, scale=float(T)).then_inc(s_expo, 1)
            act.wait_ge(s_args, 2)
            nc.scalar.activation(S6[:, 4, :], S6[:, 1, :], ACT.Sin).then_inc(s_trig, 1)
            nc.scalar.activation(S6[:, 5, :], S6[:, 3, :], ACT.Sin).then_inc(s_trig, 1)

            ffn_in(FFN0A1, N_IN0A, 1)
            ffn_out(FFN0A1)
            ffn_in(FFN0A2)
            ffn_out(FFN0A2)

            act.wait_ge(s_opdma, 16 * OPS_STORES * BLOCKS)
            wide_squares(N_S5, FFN0A2)
            root(N_S5)
            for k in range(DT):
                act.wait_ge(s_hn, k + 1)
                act.dma_start(u_dram[k * P:(k + 1) * P], HN[:, k]).then_inc(s_ust[k // QK], 16)

            def copy_s(k):
                act.wait_ge(s_s, k + 1)
                if k >= 2:
                    act.wait_ge(s_z, k - 1)
                nc.scalar.activation(SQ[:, k % 2, :], BK[k % 2][:], ACT.Copy).then_inc(s_sc, 1)

            def gelu(k):
                act.wait_ge(s_yp, k + 1)
                nc.scalar.activation(UY[:, k * GB:(k + 1) * GB, :].rearrange("p g j -> p (g j)"), BK[4 + k % 2][:],
                                     ACT.Gelu_apprx_tanh).then_inc(s_y, 1)

            for k in range(3):
                copy_s(k)
            for k in range(BLOCKS):
                if k + 3 < BLOCKS:
                    copy_s(k + 3)
                gelu(k)
            for k in range(DT):
                act.wait_ge(s_yld[k // QK], 16 * QK)
                nc.scalar.activation(G[:, k, 0, :], YT[:, k, :], ACT.Copy).then_inc(s_y_hi, 1)

            def glu(k):
                act.wait_ge(s_used, GLU + 2 * k + 2)
                if k >= 1:
                    act.wait_ge(s_x, X_BASE[GLU] + k)
                nc.scalar.activation(GT[:], in_banks(0, k)[1][:], ACT.Sigmoid).then_inc(s_sig, 1)
                if k >= 1:
                    h_hi(k - 1, G_IN0B, H)
                    square(N_IN0B, k - 1)

            split(GLU, 0)
            split(GLU, 1)
            for f in range(1, DT):
                split(GLU, 2 * f)
                glu(f - 1)
                split(GLU, 2 * f + 1)
            split(FFN0B, 0)
            glu(DT - 1)
            act.wait_ge(s_x, X_BASE[GLU] + DT)
            h_hi(DT - 1, G_IN0B, H)
            square(N_IN0B, DT - 1)
            split(FFN0B, 1)
            split(FFN0B, 2)
            root(N_IN0B)
            gate(FFN0B, 0)
            split(FFN0B, 3)
            ffn_in_loop(FFN0B)

            def rope_tables():
                act.wait_ge(s_ang, 1)
                nc.scalar.activation(SIN[:], SIN[:], ACT.Sin).then_inc(s_trig, 1)
                nc.scalar.activation(COS[:], COS[:], ACT.Sin).then_inc(s_trig, 1)

            ffn_out(FFN0B, rope_tables)

            for k in range(DT):
                act.wait_ge(s_x, X_BASE[FFN0B] + k + 1)
                h_hi(k, G_KV, G)
            for k in range(DT):
                h_hi(k, G_IN1A, H)
                square(N_KV, k)
            split(KVD, 0)
            split(KVD, 1)
            split(KVD, 2)
            split(FFN1A, 0)
            root(N_KV)
            act.wait_ge(s_cn, 1)
            nc.scalar.activation(SQ[:, 0, :], CN[:], ACT.Square).then_inc(s_cnsq, 1)
            split(FFN1A, 1)
            split(FFN1A, 2)
            gate(FFN1A, 0)
            split(FFN1A, 3)
            root(N_LAT, R2)
            ffn_in_loop(FFN1A)
            ffn_out(FFN1A)

            for k in range(DT):
                act.wait_ge(s_x, X_BASE[FFN1A] + k + 1)
                h_hi(k, G_DQ, H)
            act.wait_ge(s_cn, 2)
            nc.scalar.activation(CS[:, 0, :], CN[:], ACT.Copy).then_inc(s_cs_hi, 1)
            for k in range(DT):
                square(N_DQ, k)
            split(DQ, 0)
            split(DQ, 1)
            split(UKV, 0)
            for q in range(2):
                wait_product(act, MQ + q)
                nc.scalar.activation(CQS[:, q, 0, :], BK[q][:], ACT.Identity, scale=col(C_QN + q)).then_inc(s_cq_hi, 1)
            act.wait_ge(s_sum, (SUMS[N_DQ] + 1) * (DT - 1))
            for q in range(2):
                act.wait_ge(s_cq_lo, q + 1)
                nc.scalar.activation(SQ[:, q, :], BK[q][:], ACT.Square).then_inc(s_cqsq, 1)
            root(N_DQ)
            for h in range(HEADS):
                wait_product(act, MK + h)
                nc.scalar.activation(KN[:, h, :], BK[(MK + h) % 8][:], ACT.Copy).then_inc(s_ev_a, 1)
            split(UKV, 1)
            split(UQ, 0)
            root(N_CQ, UT)
            split(UQ, 1)
            split(UQ, 2)
            split(UQ, 3)

            def soft(h, t):
                i = 4 * h + t
                n = P * (t + 1)
                act.wait_ge(s_max, i + 1)
                if h >= 2:
                    act.wait_ge(s_tp, i - 7)
                nc.scalar.activation(PR[:, h % 2, t, 0:n], BK[t][:, 0:n], ACT.Exp, bias=STAT[:, 4 + t:5 + t],
                                     scale=QK_SCALE, accum_out=STAT[:, 8 + t:9 + t]).then_inc(s_exp, 1)

            def copy_pt(h, t):
                i = 4 * h + t
                act.wait_ge(s_tp, i + 1)
                if h >= 2:
                    act.wait_ge(s_o, h - 1)
                n = t + 1
                nc.scalar.activation(PT[:, h % 2, 0:n, t * P:(t + 1) * P],
                                     BK[4 + t % 2][:, 0:n * P].rearrange("p (a q) -> p a q", a=n),
                                     ACT.Copy).then_inc(s_pt, 1)

            def o_hi(h):
                act.wait_ge(s_o, h + 1)
                nc.scalar.activation(H[:, h, 0, :], BK[6 + h % 2][:], ACT.Copy).then_inc(s_o_hi, 1)

            for h in range(HEADS + 2):
                for t in range(4):
                    if h < HEADS:
                        soft(h, t)
                    if 1 <= h <= HEADS:
                        copy_pt(h - 1, t)
                    if t == 2 and h >= 2:
                        o_hi(h - 2)

            for d in range(DT):
                split(WO, d)
                if d >= 1:
                    act.wait_ge(s_x, X_BASE[WO] + d)
                    square(N_IN1B, d - 1)
            act.wait_ge(s_used, WO + DT)
            for k in range(DT):
                act.wait_ge(s_x, X_BASE[WO] + k + 1)
                h_hi(k, G_IN1B, H)
            square(N_IN1B, DT - 1)
            ffn_in(FFN1B, N_IN1B)
            ffn_out(FFN1B)

            wide_squares(N_FINAL, FFN1B)
            act.wait_ge(s_sq8, DT * (PE_SUMS[N_FINAL] + 1))
            for k in range(DT):
                nc.scalar.activation(X[:, k, :], X[:, k, :], ACT.Identity, scale=col(G_FIN + k)).then_inc(s_gained, 1)
            root(N_FINAL)

        @block.vector
        def _(dve):
            chain = [0]

            def link(ins):
                chain[0] += 1
                ins.then_inc(s_ch, 1)
                dve.wait_ge(s_ch, chain[0])

            tt, ts, stt = nc.vector.tensor_tensor, nc.vector.tensor_scalar, nc.vector.scalar_tensor_tensor

            def split(stage, j, i=None):
                c = stage + j + AHEAD
                r = c % RING
                dve.wait_ge(s_hi, c + 1 if i is None else i * 4 + (c + 1))
                tt(W[:, r, 1, :], RAW[:, r, :], W[:, r, 0, :].bitcast(F32), ALU.subtract).then_inc(s_lo, 1)

            def gated(stage, f, par, packs_done):
                F = f + F_BASE[stage]
                gb, ub = in_banks(BASE[stage], par)
                dve.wait_ge(s_used, packs_done)
                if not (isinstance(F, int) and F == 0):
                    dve.wait_ge(s_g_lo, F)
                tt(UT[:], ub[:], RSTD[:], ALU.mult)
                tt(GT[:], gb[:], RSTD[:], ALU.mult).then_inc(s_read, 1)
                dve.wait_ge(s_silu, F + 1)
                tt(GT[:], GT[:], UT[:], ALU.mult).then_inc(s_prod, 1)
                dve.wait_ge(s_g_hi, F + 1)
                tt(gt_part(f, 1), GT[:], gt_part(f, 0).bitcast(F32), ALU.subtract).then_inc(s_g_lo, 1)

            def h_lo(k, gains, dst, base):
                dve.wait_ge(s_h_hi, base + k + 1)
                stt(dst[:, k, 1, :], X[:, k, :], col(gains + k), dst[:, k, 0, :].bitcast(F32),
                    ALU.mult, ALU.subtract).then_inc(s_h_lo, 1)

            def mean_rcp(n, bank, width=D, dst=RSTD):
                dve.wait_ge(s_ssq, n + 1)
                link(ts(dst[:], bank[:], 1.0 / width, EPS, ALU.mult, ALU.add))
                nc.vector.reciprocal(dst[:], dst[:]).then_inc(s_rcp, 1)

            t1, t2 = GT[:, 0:256], GT[:, 256:512]

            def squared(dst, src):
                cmul(tt, link, dst[0], dst[1], src[0], src[1], src[0], src[1], t1[:, 0:GROUPS], t2[:, 0:GROUPS])

            def near_powers():
                dve.wait_ge(s_g_lo, 2)
                for tab in (PA, PB):
                    nc.vector.memset(tab[:, 0, 0, :], 1.0)
                    nc.vector.memset(tab[:, 1, 0, :], 0.0)
                u1, u2, u4 = (S6[:, 5, :], S6[:, 4, :]), (S6[:, 9, :], S6[:, 10, :]), (S6[:, 11, :], S6[:, 12, :])
                squared(u2, u1)
                squared(u4, u2)
                squared((PB[:, 0, 1, :], PB[:, 1, 1, :]), u4)
                powers(tt, link, PB, 7, t1, t2)

            def far_powers():
                dve.wait_ge(s_g_lo, 3)
                squared((PA[:, 0, 1, :], PA[:, 1, 1, :]), (PB[:, 0, 4, :], PB[:, 1, 4, :]))
                powers(tt, link, PA, 7, t1, t2)

            def block_tables(stage, k, F):
                if not (isinstance(k, int) and k == 0):
                    dve.wait_ge(s_opdma, k * (16 * OPS_STORES))
                dve.wait_ge(s_g_lo, F + 1)
                gs = block_groups(k)
                ar, ai = (PA[:, ri, :, gs].rearrange("p a g -> p g a").unsqueeze(3).broadcast_to([P, GB, 8, 8])
                          for ri in range(2))
                br, bi = (PB[:, ri, :, gs].rearrange("p b g -> p g b").unsqueeze(2).broadcast_to([P, GB, 8, 8])
                          for ri in range(2))
                ct, st, v1, v2 = (ap.rearrange("p (g a b) -> p g a b", g=GB, a=8) for ap in (
                    OUTB[:, O_COS:O_COS + 512], OUTB[:, O_SIN:O_SIN + 512], GT[:], UT[:]))
                tt(DI[:], DS[:, gs].unsqueeze(2).broadcast_to([GC, GB, GC]),
                   EYE[0:GC, 0:GC].unsqueeze(1).broadcast_to([GC, GB, GC]), ALU.mult)
                tt(v1, ai, bi, ALU.mult)
                tt(v2, ar, bi, ALU.mult)
                tt(ct, ar, br, ALU.mult)
                tt(st, ai, br, ALU.mult).then_inc(s_phase, 1)
                dve.wait_ge(s_phase, k * 2 + 1)
                tt(ct, ct, v1, ALU.subtract)
                tt(st, st, v2, ALU.add).then_inc(s_phase, 1)
                dve.wait_ge(s_phase, k * 2 + 2)

            def block_taps(stage, k):
                b = (BASE[stage] + 4) % 8
                dve.wait_ge(s_turned, k + 1)
                if isinstance(k, int) and k == 0:
                    nc.vector.memset(KT[:, :, 0:T - 1, :], 0.0)
                for q in range(2):
                    ins = nc.vector.tensor_copy(KT[:, 4 * q:4 * q + 4, T - 1:, :].rearrange("c g t d -> c g (t d)"),
                                                BK[b + q][0:GC, :].rearrange("c (g n) -> c g n", g=4))
                ins.then_inc(s_window, 1)
                dve.wait_ge(s_window, k + 1)
                tt(KT[:, :, T - 1, :], KT[:, :, T - 1, :], DI[:], ALU.add).then_inc(s_taps, 1)

            def block_b_bar(k, F):

                def chan(ap):
                    return ap.rearrange("p (g c) -> p g c", g=GB)

                wb, xb = chan(BC[:, 0, :]), chan(BC[:, 1, :])
                er, ei = (EC[:, ri, block_groups(k)].unsqueeze(2).broadcast_to([P, GB, GC]) for ri in range(2))
                a1, a2 = chan(GT[:, 0:GB * GC]), chan(GT[:, GB * GC:2 * GB * GC])
                dve.wait_ge(s_bc, k * 16 + 16)
                if isinstance(k, int) and k == 0:
                    dve.wait_ge(s_tables, 1)
                else:
                    dve.wait_ge(s_made, k)
                dve.wait_ge(s_g_lo, F + 1)
                tt(a1, xb, ei, ALU.mult)
                tt(a2, wb, ei, ALU.mult)
                tt(chan(WB[:]), wb, er, ALU.mult)
                tt(chan(XB[:]), xb, er, ALU.mult).then_inc(s_eb, 1)
                dve.wait_ge(s_eb, k + 1)
                tt(chan(WB[:]), chan(WB[:]), a1, ALU.subtract)
                tt(chan(XB[:]), chan(XB[:]), a2, ALU.add).then_inc(s_bbar, 1)
                dve.wait_ge(s_bbar, k + 1)

            def ffn_in_turn(stage, i, k=None):
                if isinstance(k, int) and k == 0:
                    far_powers()
                for a in range(2):
                    f = i * 2 + (1 + a)
                    split(stage, 4 + 2 * a, i)
                    gated(stage, f, (1 + a) % 2, i * 4 + (stage + 4 + 2 * a))
                    split(stage, 4 + 2 * a + 1, i)
                    if stage == FFN0A1 and isinstance(i, int) and i + a == 0:
                        near_powers()
                    if k is not None:
                        if a == 0:
                            block_tables(stage, k, f + F_BASE[stage])
                        else:
                            block_taps(stage, k)
                            if not (isinstance(k, int) and k == BLOCKS - 1):
                                block_b_bar(k + 1, f + F_BASE[stage])

            def ffn_in_loop(stage):
                n = TILES[stage]
                in_turns(dve, stage, ffn_in_turn)
                if n % 2:
                    split(stage, 2 * n - 2)
                    gated(stage, n - 2, (n - 2) % 2, stage + 2 * n - 2)
                    split(stage, 2 * n - 1)
                if stage == FFN0A1:
                    block_tables(stage, BLOCKS // 2 - 1, n - 2)
                    block_taps(stage, BLOCKS // 2 - 1)
                    block_b_bar(BLOCKS // 2, n - 2)

            def ffn_in(stage, n=None):
                for j in range(3):
                    split(stage, j)
                if n is not None:
                    mean_rcp(n, BK[(BASE[stage] + 4) % 8])
                    dve.wait_ge(s_rstd, n + 1)
                gated(stage, 0, 0, stage + 2)
                split(stage, 3)
                if stage == FFN0A1:
                    block_b_bar(0, 0)
                ffn_in_loop(stage)

            def ffn_out(stage):
                n = TILES[stage]
                split(stage, 2 * n)
                gated(stage, n - 1, (n - 1) % 2, stage + 2 * n)
                split(stage, 2 * n + 1)
                with dve.Fori(0, (n - 2) // 4) as i:
                    for j in range(4):
                        split(stage, 2 * n + 2 + j, i)
                for j in range(2 + (n - 2) // 4 * 4, n):
                    split(stage, 2 * n + j)

            def add_ffn(stage, d):
                wait_acc(dve, stage, d)
                stt(X[:, d, :], out_bank(stage, d)[:], 0.5, X[:, d, :], ALU.mult, ALU.add).then_inc(s_x, 1)

            dve.wait_ge(s_early, 16 * 2)
            dve.wait_ge(s_expo, 1)
            link(tt(S6[:, 6, :], LAM[:, 0, :], S6[:, 0, :], ALU.mult))
            tt(S6[:, 1, :], LAM[:, 1, :], S6[:, 0, :], ALU.mult).then_inc(s_args, 1)
            dve.wait_ge(s_args, 1)

            for k in range(DT):
                h_lo(k, G_IN0A, H, H_BASE[FFN0A1])
                if k < AHEAD:
                    split(FFN0A1, k - AHEAD)

            reduced(ts, tt, link, S6[:, 1, :], S6[:, 8, :], S6[:, 3, :]).then_inc(s_args, 1)
            ts(S6[:, 13, :], LAM[:, 1, :], col(C_SGN), None, ALU.mult)
            tt(S6[:, 15, :], LAM[:, 0, :], LAM[:, 0, :], ALU.mult)
            link(tt(S6[:, 16, :], LAM[:, 1, :], LAM[:, 1, :], ALU.mult))
            link(tt(S6[:, 15, :], S6[:, 15, :], S6[:, 16, :], ALU.add))
            link(nc.vector.reciprocal(S6[:, 15, :], S6[:, 15, :]))
            dve.wait_ge(s_trig, 2)
            link(ts(S6[:, 4, :], S6[:, 4, :], col(C_SGN), None, ALU.mult))
            tt(PW[:, 0, 1, :], S6[:, 7, :], S6[:, 5, :], ALU.mult)
            tt(PW[:, 1, 1, :], S6[:, 7, :], S6[:, 4, :], ALU.mult).then_inc(s_small, 1)
            dve.wait_ge(s_small, 1)
            lr, li, nr, ni = LAM[:, 0, :], S6[:, 13, :], S6[:, 14, :], PW[:, 1, 1, :]
            link(ts(nr, PW[:, 0, 1, :], -1.0, None, ALU.add))
            tt(S6[:, 17, :], nr, lr, ALU.mult)
            tt(S6[:, 18, :], ni, li, ALU.mult)
            tt(S6[:, 19, :], ni, lr, ALU.mult)
            link(tt(S6[:, 20, :], nr, li, ALU.mult))
            tt(S6[:, 17, :], S6[:, 17, :], S6[:, 18, :], ALU.add)
            link(tt(S6[:, 19, :], S6[:, 19, :], S6[:, 20, :], ALU.subtract))
            tt(EC[:, 0, :], S6[:, 17, :], S6[:, 15, :], ALU.mult)
            tt(EC[:, 1, :], S6[:, 19, :], S6[:, 15, :], ALU.mult).then_inc(s_tables, 1)

            dve.wait_ge(s_const, 16 * CONSTS)
            ffn_in(FFN0A1, N_IN0A)
            ffn_out(FFN0A1)
            for d in range(DT):
                add_ffn(FFN0A1, d)
            ffn_in(FFN0A2)
            ffn_out(FFN0A2)

            for d in range(DT):
                add_ffn(FFN0A2, d)
            mean_rcp(N_S5, out_bank(FFN0A2, 0))
            dve.wait_ge(s_rstd, N_S5 + 1)
            for k in range(DT):
                stt(HN[:, k].rearrange("p t j -> p j t"), X[:, k, :].rearrange("p (j t) -> p j t", t=T),
                    col(G_S5 + k), RSTD[:].rearrange("p (j t) -> p j t", t=T), ALU.mult, ALU.mult).then_inc(s_hn, 1)
            nc.vector.memset(XS[:, :, :, 0:1], 0.0).then_inc(s_zero, 1)

            def scan(k):
                dve.wait_ge(s_js, k + 1)
                link(tt(UT[:], BK[2 + k % 2][:], SLOT[:, k % N_SLOTS, O_SIN:O_SIN + 512], ALU.mult))
                dve.wait_ge(s_ic, k + 1)
                link(tt(IC[k % 2][:], IC[k % 2][:], UT[:], ALU.add))
                for g in range(GB):
                    ins = nc.vector.tensor_tensor_scan(
                        ZS[k % 2][:, g * STEPS:(g + 1) * STEPS],
                        R8[:, k * GB + g:k * GB + g + 1].broadcast_to([P, STEPS]),
                        IC[k % 2][:, g * STEPS:(g + 1) * STEPS], 0.0, ALU.mult, ALU.add)
                ins.then_inc(s_z, 1)
                dve.wait_ge(s_z, k + 1)

            def turn_state(k):
                dve.wait_ge(s_jz, k + 1)
                link(tt(KR[:], BK[6 + k % 2][:], SLOT[:, k % N_SLOTS, O_SIN:O_SIN + 512], ALU.mult))
                dve.wait_ge(s_zc, k + 1)
                if k >= 2:
                    dve.wait_ge(s_yp, k - 1)
                tt(XS[:, k % 2, :, 1:], ZC[k % 2][:].rearrange("p (g j) -> p g j", g=GB),
                   KR[:].rearrange("p (g j) -> p g j", g=GB), ALU.subtract).then_inc(s_xs, 1)
                dve.wait_ge(s_xs, k + 1)

            scan(0)
            for k in range(BLOCKS):
                if k + 1 < BLOCKS:
                    scan(k + 1)
                turn_state(k)
            for k in range(DT):
                dve.wait_ge(s_y_hi, k + 1)
                tt(G[:, k, 1, :], YT[:, k, :], G[:, k, 0, :].bitcast(F32), ALU.subtract).then_inc(s_y_lo, 1)

            def glu(k):
                dve.wait_ge(s_sig, k + 1)
                dve.wait_ge(s_x, X_BASE[GLU] + k)
                tt(UT[:], in_banks(0, k)[0][:], GT[:], ALU.mult).then_inc(s_glu, 1)
                dve.wait_ge(s_glu, k + 1)
                xk = X[:, k, :].rearrange("p (j t) -> p t j", t=T)
                tt(xk, xk, UT[:].rearrange("p (t j) -> p t j", t=T), ALU.add).then_inc(s_x, 1)
                if k >= 1:
                    h_lo(k - 1, G_IN0B, H, H_BASE[FFN0B])

            split(GLU, 0)
            split(GLU, 1)
            for f in range(1, DT):
                split(GLU, 2 * f)
                glu(f - 1)
                split(GLU, 2 * f + 1)
            split(FFN0B, 0)
            glu(DT - 1)
            h_lo(DT - 1, G_IN0B, H, H_BASE[FFN0B])
            split(FFN0B, 1)
            split(FFN0B, 2)
            mean_rcp(N_IN0B, BK[0])
            dve.wait_ge(s_rstd, N_IN0B + 1)
            gated(FFN0B, 0, 0, FFN0B + 2)
            split(FFN0B, 3)
            ffn_in_loop(FFN0B)
            ffn_out(FFN0B)

            for d in range(DT):
                add_ffn(FFN0B, d)
                if d >= 1:
                    h_lo(d - 1, G_KV, G, H_BASE[KVD])
            h_lo(DT - 1, G_KV, G, H_BASE[KVD])
            for k in range(DT):
                h_lo(k, G_IN1A, H, H_BASE[FFN1A])
            split(KVD, 0)
            split(KVD, 1)
            split(KVD, 2)
            split(FFN1A, 0)
            mean_rcp(N_KV, BK[3])
            dve.wait_ge(s_rstd, N_KV + 1)
            dve.wait_ge(s_rope, 1)
            tt(KR[:], BK[1][:], RSTD[:], ALU.mult)
            tt(UT[:], BK[2][:], RSTD[:], ALU.mult)
            tt(CN[:], BK[0][:], RSTD[:], ALU.mult).then_inc(s_cn, 1)
            dve.wait_ge(s_cn, 1)
            tt(KR[:], KR[:], COS[:], ALU.mult)
            link(tt(UT[:], UT[:], SIN[:], ALU.mult))
            link(tt(KR[:], KR[:], UT[:], ALU.add))
            split(FFN1A, 1)
            split(FFN1A, 2)
            gated(FFN1A, 0, 0, FFN1A + 2)
            split(FFN1A, 3)
            mean_rcp(N_LAT, BK[3], P, R2)
            dve.wait_ge(s_rstd, N_LAT + 1)
            stt(CN[:], CN[:], col(C_LAT), R2[:], ALU.mult, ALU.mult).then_inc(s_cn, 1)
            ffn_in_loop(FFN1A)
            ffn_out(FFN1A)

            for d in range(DT):
                add_ffn(FFN1A, d)
                if d >= 1:
                    h_lo(d - 1, G_DQ, H, H_BASE[DQ])
            h_lo(DT - 1, G_DQ, H, H_BASE[DQ])
            dve.wait_ge(s_cs_hi, 1)
            tt(CS[:, 1, :], CN[:], CS[:, 0, :].bitcast(F32), ALU.subtract).then_inc(s_cs_lo, 1)
            split(DQ, 0)
            split(DQ, 1)
            split(UKV, 0)
            for q in range(2):
                dve.wait_ge(s_cq_hi, q + 1)
                stt(CQS[:, q, 1, :], BK[q][:], col(C_QN + q), CQS[:, q, 0, :].bitcast(F32),
                    ALU.mult, ALU.subtract).then_inc(s_cq_lo, 1)
            dve.wait_ge(s_ssq, N_DQ + 1)
            ts(RSTD[:], BK[MSTAT % 8][:], 1.0 / D, EPS, ALU.mult, ALU.add).then_inc(s_ev_v, 1)
            dve.wait_ge(s_ev_v, 1)
            nc.vector.reciprocal(RSTD[:], RSTD[:]).then_inc(s_rcp, 1)
            dve.wait_ge(s_ssq, N_CQ + 1)
            ts(UT[:], BK[MCQ % 8][:], 1.0 / 256, None, ALU.mult).then_inc(s_ev_v, 1)
            for m in range(8):
                wait_product(dve, MV + m)
                nc.vector.tensor_copy(VV[:, m // 2, (m % 2) * 512:(m % 2 + 1) * 512], BK[(MV + m) % 8][:]).then_inc(s_ev_v, 1)
            split(UKV, 1)
            dve.wait_ge(s_rstd, N_DQ + 1)
            link(tt(UT[:], UT[:], RSTD[:], ALU.mult))
            link(tt(UT[:], UT[:], RSTD[:], ALU.mult))
            link(ts(UT[:], UT[:], EPS, None, ALU.add))
            nc.vector.reciprocal(UT[:], UT[:]).then_inc(s_rcp, 1)
            split(UQ, 0)
            dve.wait_ge(s_rstd, N_CQ + 1)
            link(tt(UT[:], UT[:], RSTD[:], ALU.mult))
            tt(COS[:], COS[:], UT[:], ALU.mult)
            tt(SIN[:], SIN[:], UT[:], ALU.mult)
            for h in range(HEADS):
                if h == 4:
                    split(UQ, 1)
                wait_product(dve, MN + h)
                tt(QN[:, h, :], BK[(MN + h) % 8][:], UT[:], ALU.mult).then_inc(s_ev_v, 1)
            for q in range(4):
                ea, eb = MR + 2 * q, MR + 2 * q + 1
                wait_product(dve, ea)
                tt(QR[:, q, :], BK[ea % 8][:], COS[:], ALU.mult).then_inc(s_ev_v, 1)
                wait_product(dve, eb)
                tt(GT[:], BK[eb % 8][:], SIN[:], ALU.mult).then_inc(s_ev_v, 1)
                wait_read(dve, eb)
                tt(QR[:, q, :], QR[:, q, :], GT[:], ALU.add).then_inc(s_qr, 1)
                dve.wait_ge(s_qr, q + 1)
            split(UQ, 2)
            split(UQ, 3)

            def top(h, t):
                i = 4 * h + t
                dve.wait_ge(s_scores, i + 1)
                link(nc.vector.reduce_max(STAT[:, t:t + 1], BK[t][:, 0:P * (t + 1)], AX.X))
                ts(STAT[:, 4 + t:5 + t], STAT[:, t:t + 1], -QK_SCALE, None, ALU.mult).then_inc(s_max, 1)

            def scale(h, t):
                i = 4 * h + t
                n = P * (t + 1)
                dve.wait_ge(s_exp, i + 1)
                link(nc.vector.reciprocal(STAT[:, 12 + t:13 + t], STAT[:, 8 + t:9 + t]))
                ts(PR[:, h % 2, t, 0:n], PR[:, h % 2, t, 0:n], STAT[:, 12 + t:13 + t], None, ALU.mult).then_inc(s_p, 1)
                dve.wait_ge(s_p, i + 1)

            def o_lo(h):
                dve.wait_ge(s_o_hi, h + 1)
                tt(H[:, h, 1, :], BK[6 + h % 2][:], H[:, h, 0, :].bitcast(F32), ALU.subtract).then_inc(s_o_lo, 1)

            for h in range(HEADS):
                for t in range(4):
                    top(h, t)
                    if t >= 1:
                        scale(h, t - 1)
                    if t == 3 and h >= 2:
                        o_lo(h - 2)
                scale(h, 3)
            o_lo(HEADS - 2)
            o_lo(HEADS - 1)

            def add_wo(d):
                dve.wait_ge(s_used, WO + d + 1)
                tt(X[:, d, :], X[:, d, :], BK[d][:], ALU.add).then_inc(s_x, 1)

            for d in range(DT):
                split(WO, d)
                if d >= 1:
                    add_wo(d - 1)
            add_wo(DT - 1)
            for k in range(DT):
                h_lo(k, G_IN1B, H, H_BASE[FFN1B])
            ffn_in(FFN1B, N_IN1B)
            ffn_out(FFN1B)

            for d in range(DT):
                add_ffn(FFN1B, d)
            mean_rcp(N_FINAL, out_bank(FFN1B, 0))
            dve.wait_ge(s_rstd, N_FINAL + 1)
            for k in range(DT - POOL_TILES):
                dve.wait_ge(s_gained, k + 1)
                tt(X[:, k, :], X[:, k, :], RSTD[:], ALU.mult).then_inc(s_fin_v, 1)

        @block.tensor
        def _(pe):
            mm = nc.tensor.matmul

            def three(bank, hi, lo, x_hi, x_lo, start, cols=None):
                mm(bank, hi, x_hi, start=start, stop=True, skip_group_check=True)
                mm(bank, hi, x_lo, start=False, stop=True, skip_group_check=True)
                return mm(bank, lo, x_hi, start=False, stop=True, skip_group_check=True)

            def tile(c, k):
                r = c % RING
                return W[:, r, 0, k * P:(k + 1) * P], W[:, r, 1, k * P:(k + 1) * P]

            def pack(n):
                pe.wait_ge(s_lo, n + 1)

            def column(c, bank, src, wait=None):
                for k in range(DT):
                    if wait:
                        wait(k)
                    last = three(bank[:], *tile(c, k), src[:, k, 0, :], src[:, k, 1, :], k == 0)
                last.then_inc(s_used, 1)

            def stat(n, bank):
                pe.wait_ge(s_sum, (SUMS[n] + 1) * (DT - 1))
                mm(bank[:], ONES[:], ACC[:], start=True, stop=True).then_inc(s_ssq, 1)

            def wide_stat(n, stage):
                pe.wait_ge(s_x, X_BASE[stage] + 1)
                for k in range(DT):
                    pe.wait_ge(s_sq8, PE_SUMS[n] * DT + k + 1)
                    last = mm(out_bank(stage, 0)[:], ONES[:], SQ8[:, k, :], start=(k == 0), stop=True,
                              skip_group_check=True)
                last.then_inc(s_ssq, 1)

            def keep_warm(n, src, bank):
                for _ in range(n):
                    mm(bank[:], src[:, 0:P], src[:], start=True, stop=True)

            def first_pair(stage, base, src, wait):
                banks = in_banks(base, 0)
                for k in range(DT):
                    wait(k)
                    for q in range(2):
                        if k == 0:
                            pack(stage + q)
                        last = three(banks[q][:], *tile(stage + q, k), src[:, k, 0, :], src[:, k, 1, :], k == 0)
                        if k == DT - 1:
                            last.then_inc(s_used, 1)

            def in_tile(stage, f, par, base, src, i=None, between=None):
                for q in range(2):
                    if q and between:
                        between()
                    c = stage + f * 2 + q
                    pack(c if i is None else i * 4 + c)
                    column(c, in_banks(base, par)[q], src)

            def turn_block(stage, k):
                b = (BASE[stage] + 4) % 8
                pe.wait_ge(s_made, k + 1)
                if isinstance(k, int) and k == 0:
                    pe.wait_ge(s_rcp, N_IN0A + 1)
                else:
                    pe.wait_ge(s_taps, k)
                    pe.wait_ge(s_btc, k)
                for g in range(GB):
                    mm(BK[b + g // 4][0:GC, (g % 4) * P:(g % 4 + 1) * P], BP[:, g, 0, :],
                       CP[:, g, 0:T, :].rearrange("p m c -> p (m c)"), start=(g % 4 == 0), stop=True,
                       skip_group_check=True)
                for g in range(GB):
                    last = nc.tensor.transpose(BK[b + 2 + g // 4][:, (g % 4) * P:(g % 4 + 1) * P],
                                               BP[:, g].rearrange("p m c -> p (m c)"), EYE[:])
                last.then_inc(s_turned, 1)

            def ffn_in_turn(stage, i, k=None, src=H):
                for a in range(2):
                    pe.wait_ge(s_read, i * 2 + (F_BASE[stage] + a + 1))
                    in_tile(stage, 2 + a, a, BASE[stage], src, i)
                    if a == 0 and k is not None:
                        turn_block(stage, k)

            def ffn_in(stage, src, wait, between=None, after=None):
                base, n = BASE[stage], TILES[stage]
                first_pair(stage, base, src, wait)
                if between:
                    between()
                in_tile(stage, 1, 1, base, src)
                if after:
                    after()
                in_turns(pe, stage, ffn_in_turn)
                if n % 2:
                    pe.wait_ge(s_read, F_BASE[stage] + n - 2)
                    in_tile(stage, n - 1, (n - 1) % 2, base, src,
                            between=(lambda: turn_block(stage, BLOCKS // 2 - 1)) if stage == FFN0A1 else None)
            def ffn_out(stage):
                F, n = F_BASE[stage], TILES[stage]

                def row(j, c, at, x_hi, x_lo, last_row=False):
                    pack(at)
                    for d in range(DT):
                        if j == 0 and d in (4, 6):
                            pe.wait_ge(s_read, F + n - 1 + (d == 6))
                        last = three(out_bank(stage, d)[:], *tile(c, d), x_hi, x_lo, j == 0)
                        if last_row and d < DT - 1:
                            last.then_inc(s_acc, 1)
                    last.then_inc(s_used, 1)

                if stage in BLOCK_BASE:
                    pe.wait_ge(s_taps, BLOCK_BASE[stage] + BLOCKS // 2)
                    pe.wait_ge(s_btc, BLOCK_BASE[stage] + BLOCKS // 2)
                for j in range(2):
                    pe.wait_ge(s_g_lo, F + j + 1)
                    row(j, stage + 2 * n + j, stage + 2 * n + j, G[:, j, 0, :], G[:, j, 1, :])
                pe.wait_ge(s_g_lo, F + n - 2)
                turns = (n - 5) // 4
                with pe.Fori(0, turns) as i:
                    for a in range(4):
                        c = stage + 2 * n + 2 + a
                        f = i * 4 + (2 + a)
                        row(2 + a, c, i * 4 + c, gt_part(f, 0), gt_part(f, 1))
                pe.wait_ge(s_g_lo, F + n)
                for j in range(2 + 4 * turns, n):
                    at = stage + 2 * n + j
                    row(j, at, at, G[:, j, 0, :], G[:, j, 1, :], j == n - 1)

            pe.wait_ge(s_warm, 1)
            keep_warm(4, RSTD, BK[7])

            def first_stat():
                pe.wait_ge(s_const, 16 * CONSTS)
                stat(N_IN0A, BK[4])

            ffn_in(FFN0A1, H, lambda k: pe.wait_ge(s_h_lo, H_BASE[FFN0A1] + k + 1), between=first_stat)
            ffn_out(FFN0A1)

            def second_half(k):
                if k == 0:
                    pe.wait_ge(s_x, X_BASE[FFN0A1] + 2)

            ffn_in(FFN0A2, H, second_half, between=lambda: pe.wait_ge(s_x, X_BASE[FFN0A1] + DT))
            ffn_out(FFN0A2)

            wide_stat(N_S5, FFN0A2)

            def group(ap, g, n=P):
                return ap[:, g * n:(g + 1) * n]

            def step_input(k):
                ops = SLOT[:, k % N_SLOTS]
                if k % 2 == 0:
                    pe.wait_ge(s_uld[k // 2], 16 * T)
                pe.wait_ge(s_slot[k] if k < N_SLOTS else s_again[k - N_SLOTS], 16)
                if k >= 2:
                    pe.wait_ge(s_sc, k - 1)
                for g in range(GB):
                    last = mm(group(BK[k % 2], g, STEPS), group(ops[:, O_B:O_B + 1024], g), UY[:, k * GB + g, :],
                              start=(g == 0), stop=True, skip_group_check=True)
                last.then_inc(s_s, 1)

            def swap_input(k):
                pe.wait_ge(s_sc, k + 1)
                if k >= 2:
                    pe.wait_ge(s_z, k - 1)
                mm(BK[2 + k % 2][:], JP[:], SQ[:, k % 2, :], start=True, stop=True).then_inc(s_js, 1)

            def swap_state(k):
                pe.wait_ge(s_z, k + 1)
                if k >= 2:
                    pe.wait_ge(s_xs, k - 1)
                mm(BK[6 + k % 2][:], JP[:], ZS[k % 2][:], start=True, stop=True).then_inc(s_jz, 1)

            def from_inputs(k):
                ops = SLOT[:, k % N_SLOTS]
                if k >= 2:
                    pe.wait_ge(s_y, k - 1)
                for g in range(GB):
                    mm(group(BK[4 + k % 2], g, STEPS), group(ops[:, O_T:OPS], g), UY[:, k * GB + g, :],
                       start=(g == 0), stop=True, skip_group_check=True)

            def from_states(k):
                ops = SLOT[:, k % N_SLOTS]
                pe.wait_ge(s_xs, k + 1)
                for g in range(GB):
                    last = mm(group(BK[4 + k % 2], g, STEPS), group(ops[:, O_C:O_T], g), XS[:, k % 2, g, 0:STEPS],
                              start=False, stop=True, skip_group_check=True)
                last.then_inc(s_yp, 1)

            pe.wait_ge(s_hn, 1)
            keep_warm(11, RSTD, BK[7])
            pe.wait_ge(s_jp, 16)
            pe.wait_ge(s_zero, 1)
            step_input(0)
            swap_input(0)
            step_input(1)
            for k in range(BLOCKS + 1):
                if k + 1 < BLOCKS:
                    swap_input(k + 1)
                if k < BLOCKS:
                    swap_state(k)
                if k + 2 < BLOCKS:
                    step_input(k + 2)
                if k >= 1:
                    from_states(k - 1)
                if k < BLOCKS:
                    from_inputs(k)

            first_pair(GLU, 0, G, lambda k: pe.wait_ge(s_y_lo, k + 1))
            for f in range(1, DT):
                if f >= 2:
                    pe.wait_ge(s_glu, f - 1)
                in_tile(GLU, f, f % 2, 0, G)

            ffn_in(FFN0B, H, lambda k: pe.wait_ge(s_h_lo, H_BASE[FFN0B] + k + 1), between=lambda: stat(N_IN0B, BK[0]))
            ffn_out(FFN0B)
            for q in range(3):
                pack(KVD + q)
                column(KVD + q, BK[q], G,
                       (lambda k: (pe.wait_ge(s_h_lo, H_BASE[KVD] + k + 1), pe.wait_ge(s_x, X_BASE[FFN0B] + 1 + k))) if q == 0 else None)
            stat(N_KV, BK[3])

            def latent_stat():
                pe.wait_ge(s_cnsq, 1)
                pe.wait_ge(s_rcp, N_KV + 1)
                mm(BK[3][:], ONES[:], SQ[:, 0, :], start=True, stop=True).then_inc(s_ssq, 1)

            ffn_in(FFN1A, H, lambda k: pe.wait_ge(s_h_lo, H_BASE[FFN1A] + k + 1), after=latent_stat)
            ffn_out(FFN1A)

            def free(m):
                if m >= 8:
                    wait_read(pe, m - 8)
                return BK[m % 8]

            def product(m, c, tiles, src):
                b = free(m)
                for q, k in enumerate(tiles):
                    last = three(b[:], *tile(c, k), src[q][0], src[q][1], q == 0)
                signal(last, m)

            for q in range(2):
                pack(DQ + q)
                for k in range(DT):
                    if q == 0:
                        pe.wait_ge(s_h_lo, H_BASE[DQ] + k + 1)
                    last = three(BK[q][:], *tile(DQ + q, k), H[:, k, 0, :], H[:, k, 1, :], k == 0)
                signal(last, MQ + q)
            pe.wait_ge(s_sum, (SUMS[N_DQ] + 1) * (DT - 1))
            mm(BK[MSTAT][:], ONES[:], ACC[:], start=True, stop=True).then_inc(s_ssq, 1)
            pe.wait_ge(s_cs_lo, 1)
            pack(UKV)
            for h in range(HEADS):
                product(MK + h, UKV, [h], [(CS[:, 0, :], CS[:, 1, :])])
            pe.wait_ge(s_cqsum, 1)
            free(MCQ)
            mm(BK[MCQ % 8][:], ONES[:], ACC[:], start=True, stop=True).then_inc(s_ssq, 1)
            pack(UKV + 1)
            for m in range(8):
                t, half = m // 2, m % 2
                b = free(MV + m)
                r = (UKV + 1) % RING
                tok = slice(t * P, (t + 1) * P)
                w_hi, w_lo = (W[:, r, q, half * 512:(half + 1) * 512] for q in range(2))
                mm(b[:], CS[:, 0, tok], w_hi, start=True, stop=True, skip_group_check=True)
                mm(b[:], CS[:, 0, tok], w_lo, start=False, stop=True, skip_group_check=True)
                signal(mm(b[:], CS[:, 1, tok], w_hi, start=False, stop=True, skip_group_check=True), MV + m)
            pe.wait_ge(s_cq_lo, 2)
            cq = [(CQS[:, q, 0, :], CQS[:, q, 1, :]) for q in range(2)]
            for h in range(HEADS):
                if h % 4 == 0:
                    pack(UQ + h // 4)
                product(MN + h, UQ + h // 4, [2 * (h % 4), 2 * (h % 4) + 1], cq)
            pack(UQ + 3)
            for q in range(4):
                for side in range(2):
                    product(MR + 2 * q + side, UQ + 2 + side, [2 * q, 2 * q + 1], cq)

            wait_read(pe, MCQ - 1)
            wait_read(pe, MID - 1)
            pe.wait_ge(s_qr, 4)

            def scores(h, t):
                if h >= 1:
                    pe.wait_ge(s_exp, 4 * (h - 1) + t + 1)
                n = P * (t + 1)
                q0 = 64 * (h % 2)
                mm(BK[t][:, 0:n], QN[:, h, t * P:(t + 1) * P], KN[:, h, 0:n], start=True, stop=True, skip_group_check=True)
                mm(BK[t][:, 0:n], QR[q0:q0 + 64, h // 2, t * P:(t + 1) * P], KR[q0:q0 + 64, 0:n],
                   start=False, stop=True, skip_group_check=True)
                mm(BK[t][:, n - 64:n], MASK[0:1, 0:P], MASK[0:1, P:P + 64], start=False, stop=True,
                   skip_group_check=True).then_inc(s_scores, 1)

            def turn(h, t):
                i = 4 * h + t
                pe.wait_ge(s_p, i + 1)
                if i >= 2:
                    pe.wait_ge(s_pt, i - 1)
                for a in range(t + 1):
                    last = nc.tensor.transpose(BK[4 + t % 2][:, a * P:(a + 1) * P],
                                               PR[:, h % 2, t, a * P:(a + 1) * P], EYE[:])
                last.then_inc(s_tp, 1)

            def values(h):
                if h >= 2:
                    pe.wait_ge(s_o_lo, h - 1)
                pe.wait_ge(s_pt, 4 * h + 4)
                for a in range(4):
                    last = mm(BK[6 + h % 2][:, a * P:], VV[:, a, h * P:(h + 1) * P], PT[:, h % 2, a, a * P:],
                              start=(a == 0), stop=True, skip_group_check=True)
                last.then_inc(s_o, 1)

            for h in range(HEADS + 2):
                for t in range(4):
                    if h < HEADS:
                        scores(h, t)
                    if 1 <= h <= HEADS:
                        turn(h - 1, t)
                    if t == 1 and h >= 2:
                        values(h - 2)

            for d in range(DT):
                pack(WO + d)
                if d in (4, 6, 7):
                    pe.wait_ge(s_o_lo, HEADS)
                column(WO + d, BK[d], H, (lambda k: pe.wait_ge(s_o_lo, k + 1)) if d == 0 else None)

            ffn_in(FFN1B, H, lambda k: pe.wait_ge(s_h_lo, H_BASE[FFN1B] + k + 1), between=lambda: stat(N_IN1B, BK[4]))
            ffn_out(FFN1B)
            wide_stat(N_FINAL, FFN1B)

    return nc


def column_packs(w):
    k, n = w.shape
    return w.reshape(k // P, P, n // P, P).transpose(2, 1, 0, 3).reshape(n // P, P, k)


def weight_stream(ffn_w_in, ffn_w_out, s5_w_glu, w_dkv, w_ukv, mla_w_dq, mla_w_uq, mla_w_o):
    s = np.zeros((N_LOADS, P, 1024), np.float32)

    def gated(at, w, f0, f1):
        packs = column_packs(w)
        up, n = len(packs) // 2, f1 - f0
        s[at:at + 2 * n:2], s[at + 1:at + 2 * n:2] = packs[f0:f1], packs[up + f0:up + f1]

    for at, layer, i, f0, f1 in ((FFN0A1, 0, 0, 0, HALF), (FFN0A2, 0, 0, HALF, FT), (FFN0B, 0, 1, 0, FT),
                                 (FFN1A, 1, 0, 0, FT), (FFN1B, 1, 1, 0, FT)):
        n = f1 - f0
        gated(at, ffn_w_in[layer, i], f0, f1)
        s[at + 2 * n:at + 3 * n] = ffn_w_out[layer, i].reshape(FT, P, D)[f0:f1]
    gated(GLU, s5_w_glu[0], 0, DT)
    s[KVD] = column_packs(w_dkv[:, :P])[0]
    r = w_dkv[:, P:]
    x = np.concatenate([r[:, 32:], r[:, :32]], 1)
    s[KVD + 1] = column_packs(np.concatenate([r, r], 1))[0]
    s[KVD + 2] = column_packs(np.concatenate([x, x], 1))[0]
    ukv = w_ukv.reshape(P, HEADS, 2, P)
    s[UKV], s[UKV + 1] = ukv[:, :, 0].reshape(P, 1024), ukv[:, :, 1].reshape(P, 1024)
    s[DQ:DQ + 2] = column_packs(mla_w_dq[0])
    uq = mla_w_uq[0].reshape(2, P, HEADS, 192)
    nope = uq[..., :P].transpose(1, 2, 0, 3).reshape(P, 2, 1024)
    s[UQ], s[UQ + 1] = nope[:, 0], nope[:, 1]
    rope = uq[..., P:]
    swap = np.concatenate([rope[..., 32:], rope[..., :32]], -1)
    for q, part in enumerate((rope, swap)):
        s[UQ + 2 + q] = part.reshape(2, P, 4, 2, 64).transpose(1, 2, 0, 3, 4).reshape(P, 1024)
    s[WO:WO + DT] = column_packs(mla_w_o[0])
    return s


def kernel(**inputs):
    import concourse.bacc as bacc
    from concourse.bass_utils import run_bass_kernel_spmd

    a = {k: np.asarray(v) for k, v in inputs.items()}
    f = np.float32

    def columns(v):
        return v.reshape(-1, P).T

    g = a["norm_gains"]
    half, quarter = np.repeat([1.0, -1.0], 64), np.tile(np.repeat([-1.0, 1.0], 32), 2)
    inv_freq = (1.0 / (10000.0 ** (np.arange(0, 64, 2) / 64)).astype(f)).astype(f)
    cols = np.concatenate([columns(v) for v in (
        g[0, 0], g[0, 1], g[0, 2], a["kv_in_norm"], g[1, 0], g[1, 1], g[1, 2], a["final_norm"],
        a["kv_latent_norm"], a["mla_q_norm"][0], half.astype(f), quarter.astype(f), np.tile(inv_freq, 4))], 1)
    eye = np.eye(P, dtype=f)
    consts = np.stack([np.ones((P, P), f), eye, np.roll(eye, 64, 0)])
    mask = np.concatenate([np.repeat([1.0, 0.0], 64), np.full(64, NEG)]).astype(f)[None]

    def states(v):
        return np.concatenate([v.T, v.T], 0)

    lam = np.stack([states(a["s5_lambda_re"][0]), states(a["s5_lambda_im"][0]),
                    np.broadcast_to(a["s5_log_step"][0], (P, GROUPS))], 1)
    b_re, b_im = (a[n][0].transpose(1, 0, 2) for n in ("s5_b_re", "s5_b_im"))
    c_re, c_im = (a[n][0].transpose(2, 0, 1) for n in ("s5_c_re", "s5_c_im"))
    bcd = np.stack([np.concatenate(v, 0) for v in ((b_re, b_im), (b_im, b_re), (c_re, c_im), (c_im, c_re))], 1)
    bcd = bcd.reshape(P, 4, BLOCKS, GB * GC).transpose(2, 0, 1, 3)
    arrays = {
        "xT": a["x"][0].T.reshape(DT, P, SEQ),
        "wstream": weight_stream(*(a[n] for n in ("ffn_w_in", "ffn_w_out", "s5_w_glu", "w_dkv", "w_ukv",
                                                  "mla_w_dq", "mla_w_uq", "mla_w_o"))),
        "cols": cols, "consts": consts, "mask": mask,
        "pos": np.broadcast_to(a["positions"], (P, SEQ)),
        "lam": lam, "bcd": bcd, "dskip": a["s5_d"][0].reshape(GROUPS, GC).T,
    }
    arrays = {k: np.ascontiguousarray(v) for k, v in arrays.items()}

    nc = bacc.Bacc("TRN2", target_bir_lowering=False, num_devices=1)
    aps = {k: nc.dram_tensor(k, v.shape, mybir.dt.from_np(v.dtype), kind="ExternalInput").ap()
           for k, v in arrays.items()}
    out = nc.dram_tensor("out", (DT, P, SEQ), F32, kind="ExternalOutput").ap()
    build(nc, out=out, **aps)
    r = run_bass_kernel_spmd(nc, [arrays], core_ids=[0])
    return r.results[0]["out"].reshape(D, SEQ).T[None]
```
